# Optimizing a Trainium2 kernel written in Bass

```python
import math
import jax, jax.numpy as jnp
from jax import lax
import numpy as np

D_MODEL = 1024
BATCH = 1
SEQ = 256
DEPTH = 2

N_META = 16
HEAD_DIM = 64
N_Q_HEADS = 8
N_KV_HEADS = 2
GROUP = N_Q_HEADS // N_KV_HEADS
ATTN_WIDTH = N_Q_HEADS * HEAD_DIM
KV_WIDTH = N_KV_HEADS * HEAD_DIM
WINDOW = 128
BLOCK = 128
CONV_CH = D_MODEL // 2
CONV_WIDTH = 31
N_BUCKETS = 32
MAX_DISTANCE = 128
D_FF = 2816
N_EXPERTS = 8
TOP_K = 2
D_EXPERT = 1408
N_DENSE = (DEPTH + 1) // 2
N_MOE = DEPTH // 2
ALPHA = (2 * DEPTH) ** 0.25
BETA = (8 * DEPTH) ** -0.25
LN_EPS = 1e-5
Q_END = ATTN_WIDTH
K_END = Q_END + KV_WIDTH
V_END = K_END + KV_WIDTH
GLU_END = V_END + 2 * CONV_CH
GA_END = GLU_END + D_MODEL
GC_END = GA_END + D_MODEL
IN_WIDTH = GC_END


def layer_norm(x, g, b):
    xf = x.astype(jnp.float32)
    mu = jnp.mean(xf, -1, keepdims=True)
    var = jnp.mean(jnp.square(xf - mu), -1, keepdims=True)
    y = (xf - mu) * lax.rsqrt(var + LN_EPS) * g.astype(jnp.float32) + b.astype(jnp.float32)
    return y.astype(x.dtype)

def rel_bucket(dist):
    n = jnp.maximum(dist, 0)
    max_exact = N_BUCKETS // 2
    nf = jnp.maximum(n, 1).astype(jnp.float32)
    large = max_exact + (jnp.log(nf / max_exact) / math.log(MAX_DISTANCE / max_exact)
                         * (N_BUCKETS - max_exact)).astype(jnp.int32)
    large = jnp.minimum(large, N_BUCKETS - 1)
    return jnp.where(n < max_exact, n, large)

def head_bias(rel_bias, bucket):
    b = rel_bias.astype(jnp.float32)[bucket]
    b = jnp.moveaxis(b, -1, -3)
    return b.reshape(b.shape[:-3] + (N_KV_HEADS, GROUP) + b.shape[-2:])

def sink_softmax(s, sink):
    m = jnp.maximum(jnp.max(s, -1, keepdims=True), sink)
    p = jnp.exp(s - m)
    return p / (jnp.sum(p, -1, keepdims=True) + jnp.exp(sink - m))

def sliding_window_attention(q, k, v, sinks, rel_bias):
    B, L = q.shape[:2]
    S = L - N_META
    nb = S // BLOCK
    scale = HEAD_DIM ** -0.5
    sink = sinks.astype(jnp.float32).reshape(N_KV_HEADS, GROUP)[:, :, None, None]

    qm = q[:, :N_META].reshape(B, N_META, N_KV_HEADS, GROUP, HEAD_DIM)
    km, vm = k[:, :N_META], v[:, :N_META]

    pos_m = jnp.arange(N_META)
    dist_mm = pos_m[:, None] - pos_m[None, :]
    s_mm = jnp.einsum('bqhgd,bkhd->bhgqk', qm, km).astype(jnp.float32) * scale
    s_mm = s_mm + head_bias(rel_bias, rel_bucket(dist_mm))
    s_mm = jnp.where(dist_mm >= 0, s_mm, -jnp.inf)
    p_mm = sink_softmax(s_mm, sink).astype(v.dtype)
    o_m = jnp.einsum('bhgqk,bkhd->bqhgd', p_mm, vm).reshape(B, N_META, ATTN_WIDTH)

    qr = q[:, N_META:].reshape(B, nb, BLOCK, N_KV_HEADS, GROUP, HEAD_DIM)
    kr = k[:, N_META:].reshape(B, nb, BLOCK, N_KV_HEADS, HEAD_DIM)
    vr = v[:, N_META:].reshape(B, nb, BLOCK, N_KV_HEADS, HEAD_DIM)
    zpad = jnp.zeros_like(kr[:, :1])
    kb = jnp.concatenate([jnp.concatenate([zpad, kr[:, :-1]], 1), kr], 2)
    vb = jnp.concatenate([jnp.concatenate([zpad, vr[:, :-1]], 1), vr], 2)

    a = jnp.arange(BLOCK)
    kk = jnp.arange(2 * BLOCK)
    blk = jnp.arange(nb)
    dist_band = BLOCK + a[:, None] - kk[None, :]
    mask_band = ((dist_band >= 0) & (dist_band < WINDOW))[None] & \
        ((blk[:, None, None] > 0) | (kk[None, None, :] >= BLOCK))
    q_pos = N_META + blk[:, None] * BLOCK + a[None, :]
    dist_meta = q_pos[:, :, None] - pos_m[None, None, :]

    s_band = jnp.einsum('bnqhgd,bnkhd->bnhgqk', qr, kb).astype(jnp.float32) * scale
    s_band = s_band + head_bias(rel_bias, rel_bucket(dist_band))
    s_band = jnp.where(mask_band[None, :, None, None], s_band, -jnp.inf)
    s_meta = jnp.einsum('bnqhgd,bmhd->bnhgqm', qr, km).astype(jnp.float32) * scale
    s_meta = s_meta + head_bias(rel_bias, rel_bucket(dist_meta))
    p = sink_softmax(jnp.concatenate([s_meta, s_band], -1), sink).astype(v.dtype)
    o_r = jnp.einsum('bnhgqm,bmhd->bnqhgd', p[..., :N_META], vm) + \
        jnp.einsum('bnhgqk,bnkhd->bnqhgd', p[..., N_META:], vb)
    o_r = o_r.reshape(B, S, ATTN_WIDTH)
    return jnp.concatenate([o_m, o_r], 1)

def conformer_conv(u, dw, db, g, b):
    val, gate = jnp.split(u, 2, axis=-1)
    h = val * jax.nn.sigmoid(gate)
    h = lax.conv_general_dilated(h, dw[:, None, :].astype(h.dtype), window_strides=(1,),
                                 padding=[(CONV_WIDTH - 1, 0)],
                                 dimension_numbers=('NWC', 'WIO', 'NWC'),
                                 feature_group_count=CONV_CH) + db
    h = layer_norm(h, g, b)
    return jax.nn.silu(h)

def swiglu(t, wg, wu, wd):
    return (jax.nn.silu(t @ wg) * (t @ wu)) @ wd

def moe_swiglu(h, router, wg, wu, wd):
    B, L, D = h.shape
    t = h.reshape(B * L, D)
    logits = (t @ router).astype(jnp.float32)
    vals, idx = lax.top_k(logits, TOP_K)
    gates = jax.nn.softmax(vals, axis=-1)
    combine = jnp.sum(jax.nn.one_hot(idx, N_EXPERTS, dtype=jnp.float32) * gates[..., None], 1)
    out = jnp.zeros_like(t)
    for e in range(N_EXPERTS):
        out = out + combine[:, e:e + 1].astype(t.dtype) * swiglu(t, wg[e], wu[e], wd[e])
    return out.reshape(B, L, D)

def first_inputs(seed: int = 0) -> dict:
    key = jax.random.key(seed)
    ks = iter(jax.random.split(key, 32))
    n = lambda shape, s: jax.random.normal(next(ks), shape, jnp.float32) * s
    D = D_MODEL
    return {
        "x": n((BATCH, SEQ, D), 1.0),
        "meta_tokens": n((N_META, D), 1.0),
        "emb_ln_g": 1.0 + n((D,), 0.02),
        "emb_ln_b": n((D,), 0.02),
        "rel_bias": n((N_BUCKETS, N_Q_HEADS), 0.5),
        "w_in": n((DEPTH, D, IN_WIDTH), D ** -0.5),
        "conv_dw": n((DEPTH, CONV_WIDTH, CONV_CH), CONV_WIDTH ** -0.5),
        "conv_b": n((DEPTH, CONV_CH), 0.02),
        "conv_ln_g": 1.0 + n((DEPTH, CONV_CH), 0.02),
        "conv_ln_b": n((DEPTH, CONV_CH), 0.02),
        "sinks": n((DEPTH, N_Q_HEADS), 0.5),
        "w_attn_proj": n((DEPTH, ATTN_WIDTH, D), ATTN_WIDTH ** -0.5),
        "w_conv_proj": n((DEPTH, CONV_CH, D), CONV_CH ** -0.5),
        "w_out": n((DEPTH, D, D), BETA * D ** -0.5),
        "ln1_g": 1.0 + n((DEPTH, D), 0.02),
        "ln1_b": n((DEPTH, D), 0.02),
        "ffn_w_gate": n((N_DENSE, D, D_FF), D ** -0.5),
        "ffn_w_up": n((N_DENSE, D, D_FF), D ** -0.5),
        "ffn_w_down": n((N_DENSE, D_FF, D), BETA * D_FF ** -0.5),
        "router": n((N_MOE, D, N_EXPERTS), D ** -0.5),
        "moe_w_gate": n((N_MOE, N_EXPERTS, D, D_EXPERT), D ** -0.5),
        "moe_w_up": n((N_MOE, N_EXPERTS, D, D_EXPERT), D ** -0.5),
        "moe_w_down": n((N_MOE, N_EXPERTS, D_EXPERT, D), BETA * D_EXPERT ** -0.5),
        "ln2_g": 1.0 + n((DEPTH, D), 0.02),
        "ln2_b": n((DEPTH, D), 0.02),
    }

def first_block(x, meta_tokens, emb_ln_g, emb_ln_b, rel_bias, w_in, conv_dw, conv_b,
              conv_ln_g, conv_ln_b, sinks, w_attn_proj, w_conv_proj, w_out, ln1_g, ln1_b,
              ffn_w_gate, ffn_w_up, ffn_w_down, router, moe_w_gate, moe_w_up, moe_w_down,
              ln2_g, ln2_b):
    B = x.shape[0]
    meta = jnp.broadcast_to(meta_tokens[None].astype(x.dtype), (B, N_META, D_MODEL))
    h = layer_norm(jnp.concatenate([meta, x], axis=1), emb_ln_g, emb_ln_b)
    L = h.shape[1]
    for i in range(DEPTH):
        u = h @ w_in[i]
        q = u[..., :Q_END].reshape(B, L, N_Q_HEADS, HEAD_DIM)
        k = u[..., Q_END:K_END].reshape(B, L, N_KV_HEADS, HEAD_DIM)
        v = u[..., K_END:V_END].reshape(B, L, N_KV_HEADS, HEAD_DIM)
        y_attn = sliding_window_attention(q, k, v, sinks[i], rel_bias) @ w_attn_proj[i]
        y_conv = conformer_conv(u[..., V_END:GLU_END], conv_dw[i], conv_b[i],
                                conv_ln_g[i], conv_ln_b[i]) @ w_conv_proj[i]
        mix = (jax.nn.sigmoid(u[..., GLU_END:GA_END]) * y_attn
               + jax.nn.sigmoid(u[..., GA_END:GC_END]) * y_conv) @ w_out[i]
        h = layer_norm(ALPHA * h + mix, ln1_g[i], ln1_b[i])
        j = i // 2
        if i % 2 == 0:
            f = swiglu(h, ffn_w_gate[j], ffn_w_up[j], ffn_w_down[j])
        else:
            f = moe_swiglu(h, router[j], moe_w_gate[j], moe_w_up[j], moe_w_down[j])
        h = layer_norm(ALPHA * h + f, ln2_g[i], ln2_b[i])
    return h[:, N_META:]


GRID_W = 64
CTX_LEN = 256
N_MIXERS = 2
N_HEADS = 16
HEAD_DIM_2 = D_MODEL // N_HEADS
NA_KH = 8
NA_KW = 16
NA_QCB = NA_KW
NA_KCB = 2 * NA_KW
WA_KV_HEADS = 4
WA_GROUPS = N_HEADS // WA_KV_HEADS
WA_WINDOW = 128
WA_BLOCK = 128
FFN_RES = 0.5
ROPE_BASE = 10000.0
N_MOD = 9
ALPHA_2 = (2 * DEPTH) ** 0.25
BETA_2 = (8 * DEPTH) ** -0.25
NEG_INF = -1e30
N_NA_LAYERS = (DEPTH + 1) // 2
N_WA_LAYERS = DEPTH // 2


def layer_norm_2(x, g, b):
    xf = x.astype(jnp.float32)
    mu = jnp.mean(xf, axis=-1, keepdims=True)
    var = jnp.mean(jnp.square(xf - mu), axis=-1, keepdims=True)
    return ((xf - mu) * lax.rsqrt(var + LN_EPS)).astype(x.dtype) * g + b

def modulate(h, shift, scale):
    return h * (1.0 + scale) + shift

def swiglu_2(u, w_in, w_out):
    a, v = jnp.split(u @ w_in, 2, axis=-1)
    return (jax.nn.silu(a) * v) @ w_out

def ffn_sublayer(h, shift, scale, gate, w_in, w_out, g, b):
    y = swiglu_2(modulate(h, shift, scale), w_in, w_out)
    return layer_norm_2(ALPHA_2 * h + FFN_RES * gate * y, g, b)

def axial_rope(x):
    S = x.shape[1]
    t = jnp.arange(S, dtype=jnp.int32)
    rows = (t // GRID_W).astype(jnp.float32)
    cols = (t % GRID_W).astype(jnp.float32)
    n = HEAD_DIM_2 // 4
    inv_freq = ROPE_BASE ** (-jnp.arange(n, dtype=jnp.float32) / n)
    half = HEAD_DIM_2 // 2

    def rot(xa, pos):
        ang = pos[:, None] * inv_freq[None, :]
        cos = jnp.cos(ang)[None, :, None, :].astype(x.dtype)
        sin = jnp.sin(ang)[None, :, None, :].astype(x.dtype)
        x1, x2 = xa[..., :n], xa[..., n:]
        return jnp.concatenate([x1 * cos - x2 * sin, x2 * cos + x1 * sin], axis=-1)

    return jnp.concatenate([rot(x[..., :half], rows), rot(x[..., half:], cols)], axis=-1)

def ctx_attention(qc, kc, vc, sink):
    B, C, H, d = qc.shape
    hk = kc.shape[2]
    g = H // hk
    qg = qc.reshape(B, C, hk, g, d)
    s = jnp.einsum('bqhgd,bkhd->bhgqk', qg, kc).astype(jnp.float32)
    if sink is not None:
        sk = jnp.broadcast_to(sink.astype(jnp.float32).reshape(1, hk, g, 1, 1), s.shape[:-1] + (1,))
        s = jnp.concatenate([s, sk], axis=-1)
    p = jax.nn.softmax(s, axis=-1)[..., :C].astype(vc.dtype)
    o = jnp.einsum('bhgqk,bkhd->bqhgd', p, vc)
    return o.reshape(B, C, H * d)

def neighborhood_attention(u_lat, u_ctx, w_qkv, w_o, rpb, with_ctx_out):
    B, S, _ = u_lat.shape
    C = u_ctx.shape[1]
    rows = S // GRID_W
    kh = min(NA_KH, rows)
    scale = HEAD_DIM_2 ** -0.5
    qkv = (u_lat @ w_qkv).reshape(B, rows, GRID_W, 3, N_HEADS, HEAD_DIM_2)
    q = qkv[:, :, :, 0] * scale
    k = qkv[:, :, :, 1]
    v = qkv[:, :, :, 2]
    kvc = (u_ctx @ w_qkv[:, D_MODEL:]).reshape(B, C, 2, N_HEADS, HEAD_DIM_2)
    kc, vc = kvc[:, :, 0], kvc[:, :, 1]

    ncb = GRID_W // NA_QCB
    qcol = np.arange(GRID_W).reshape(ncb, NA_QCB)
    blk_start = np.clip(np.arange(ncb) * NA_QCB - NA_KW // 2, 0, GRID_W - NA_KCB)
    kcol = blk_start[:, None] + np.arange(NA_KCB)[None, :]
    win_start = np.clip(qcol - NA_KW // 2, 0, GRID_W - NA_KW)
    col_valid = (kcol[:, None, :] >= win_start[..., None]) & (kcol[:, None, :] < win_start[..., None] + NA_KW)
    col_off = np.clip(kcol[:, None, :] - qcol[..., None], -(NA_KW - 1), NA_KW - 1) + NA_KW - 1
    bias_cols = jnp.where(col_valid, rpb[:, :, col_off].astype(jnp.float32), NEG_INF)
    n_win = kh * NA_KCB

    def row_block(r):
        rs = jnp.clip(r - kh // 2, 0, rows - kh)
        q_r = lax.dynamic_index_in_dim(q, r, axis=1, keepdims=False).reshape(B, ncb, NA_QCB, N_HEADS, HEAD_DIM_2)
        k_r = lax.dynamic_slice_in_dim(k, rs, kh, axis=1)[:, :, kcol]
        v_r = lax.dynamic_slice_in_dim(v, rs, kh, axis=1)[:, :, kcol]
        row_idx = rs + jnp.arange(kh) - r + NA_KH - 1
        bias = jnp.take(bias_cols, row_idx, axis=1).transpose(0, 2, 3, 1, 4)[None]
        s_win = jnp.einsum('bcqhd,bicjhd->bhcqij', q_r, k_r).astype(jnp.float32) + bias
        s_win = s_win.reshape(B, N_HEADS, ncb, NA_QCB, n_win)
        s_ctx = jnp.einsum('bcqhd,bkhd->bhcqk', q_r, kc).astype(jnp.float32)
        p = jax.nn.softmax(jnp.concatenate([s_win, s_ctx], axis=-1), axis=-1).astype(v.dtype)
        p_win = p[..., :n_win].reshape(B, N_HEADS, ncb, NA_QCB, kh, NA_KCB)
        p_ctx = p[..., n_win:]
        o = (jnp.einsum('bhcqij,bicjhd->bcqhd', p_win, v_r)
             + jnp.einsum('bhcqk,bkhd->bcqhd', p_ctx, vc))
        return o.reshape(B, GRID_W, D_MODEL)

    out = lax.map(row_block, jnp.arange(rows, dtype=jnp.int32))
    y_lat = out.transpose(1, 0, 2, 3).reshape(B, S, D_MODEL) @ w_o
    y_ctx = None
    if with_ctx_out:
        qc = (u_ctx @ w_qkv[:, :D_MODEL]).reshape(B, C, N_HEADS, HEAD_DIM_2) * scale
        y_ctx = ctx_attention(qc, kc, vc, None) @ w_o
    return y_lat, y_ctx

def window_gqa(u_lat, u_ctx, w_qkv, w_o, sinks, with_ctx_out):
    B, S, _ = u_lat.shape
    C = u_ctx.shape[1]
    dq = N_HEADS * HEAD_DIM_2
    dkv = WA_KV_HEADS * HEAD_DIM_2
    scale = HEAD_DIM_2 ** -0.5
    qkv = u_lat @ w_qkv
    q = axial_rope(qkv[..., :dq].reshape(B, S, N_HEADS, HEAD_DIM_2)) * scale
    k = axial_rope(qkv[..., dq:dq + dkv].reshape(B, S, WA_KV_HEADS, HEAD_DIM_2))
    v = qkv[..., dq + dkv:].reshape(B, S, WA_KV_HEADS, HEAD_DIM_2)
    kvc = u_ctx @ w_qkv[:, dq:]
    kc = kvc[..., :dkv].reshape(B, C, WA_KV_HEADS, HEAD_DIM_2)
    vc = kvc[..., dkv:].reshape(B, C, WA_KV_HEADS, HEAD_DIM_2)

    nb = S // WA_BLOCK
    pad = ((0, 0), (WA_BLOCK, WA_BLOCK), (0, 0), (0, 0))
    k_pad = jnp.pad(k, pad)
    v_pad = jnp.pad(v, pad)
    q_blk = q.reshape(B, nb, WA_BLOCK, WA_KV_HEADS, WA_GROUPS, HEAD_DIM_2)
    sink = sinks.astype(jnp.float32).reshape(1, WA_KV_HEADS, WA_GROUPS, 1, 1)
    qi = jnp.arange(WA_BLOCK, dtype=jnp.int32)
    kj = jnp.arange(3 * WA_BLOCK, dtype=jnp.int32)
    n_win = 3 * WA_BLOCK

    def band_block(b):
        qb = lax.dynamic_index_in_dim(q_blk, b, axis=1, keepdims=False)
        kb = lax.dynamic_slice_in_dim(k_pad, b * WA_BLOCK, n_win, axis=1)
        vb = lax.dynamic_slice_in_dim(v_pad, b * WA_BLOCK, n_win, axis=1)
        pos_q = b * WA_BLOCK + qi
        pos_k = (b - 1) * WA_BLOCK + kj
        valid = ((jnp.abs(pos_q[:, None] - pos_k[None, :]) <= WA_WINDOW)
                 & (pos_k >= 0)[None, :] & (pos_k < S)[None, :])
        s_win = jnp.where(valid, jnp.einsum('bqhgd,bkhd->bhgqk', qb, kb).astype(jnp.float32), NEG_INF)
        s_ctx = jnp.einsum('bqhgd,bkhd->bhgqk', qb, kc).astype(jnp.float32)
        s_sink = jnp.broadcast_to(sink, s_win.shape[:-1] + (1,))
        p = jax.nn.softmax(jnp.concatenate([s_win, s_ctx, s_sink], axis=-1), axis=-1).astype(v.dtype)
        o = (jnp.einsum('bhgqk,bkhd->bqhgd', p[..., :n_win], vb)
             + jnp.einsum('bhgqk,bkhd->bqhgd', p[..., n_win:n_win + C], vc))
        return o.reshape(B, WA_BLOCK, D_MODEL)

    out = lax.map(band_block, jnp.arange(nb, dtype=jnp.int32))
    y_lat = out.transpose(1, 0, 2, 3).reshape(B, S, D_MODEL) @ w_o
    y_ctx = None
    if with_ctx_out:
        qc = (u_ctx @ w_qkv[:, :dq]).reshape(B, C, N_HEADS, HEAD_DIM_2) * scale
        y_ctx = ctx_attention(qc, kc, vc, sinks) @ w_o
    return y_lat, y_ctx

def second_inputs(seed: int = 0) -> dict:
    key = jax.random.key(seed)
    ks = jax.random.split(key, 16)
    f32 = jnp.float32
    dq = N_HEADS * HEAD_DIM_2
    dkv = WA_KV_HEADS * HEAD_DIM_2

    def nrm(k, shape, s):
        return jax.random.normal(k, shape, f32) * s

    return {
        "x": nrm(ks[0], (BATCH, SEQ, D_MODEL), 1.0),
        "c": nrm(ks[1], (BATCH, D_MODEL), 1.0),
        "ctx": nrm(ks[2], (BATCH, CTX_LEN, D_MODEL), 1.0),
        "c_ctx": nrm(ks[3], (D_MODEL,), 1.0),
        "w_mod": nrm(ks[4], (DEPTH, D_MODEL, N_MOD * D_MODEL), 0.5 * D_MODEL ** -0.5),
        "b_mod": nrm(ks[5], (DEPTH, N_MOD * D_MODEL), 0.02),
        "ln_g": 1.0 + nrm(ks[6], (DEPTH, 3, D_MODEL), 0.02),
        "ln_b": nrm(ks[7], (DEPTH, 3, D_MODEL), 0.02),
        "ffn_w_in": nrm(ks[8], (DEPTH, 2, D_MODEL, 2 * D_FF), D_MODEL ** -0.5),
        "ffn_w_out": nrm(ks[9], (DEPTH, 2, D_FF, D_MODEL), BETA_2 * D_FF ** -0.5),
        "na_w_qkv": nrm(ks[10], (N_NA_LAYERS, D_MODEL, 3 * dq), D_MODEL ** -0.5),
        "na_w_o": nrm(ks[11], (N_NA_LAYERS, dq, D_MODEL), BETA_2 * dq ** -0.5),
        "na_rpb": nrm(ks[12], (N_NA_LAYERS, N_HEADS, 2 * NA_KH - 1, 2 * NA_KW - 1), 0.1),
        "wa_w_qkv": nrm(ks[13], (N_WA_LAYERS, D_MODEL, dq + 2 * dkv), D_MODEL ** -0.5),
        "wa_w_o": nrm(ks[14], (N_WA_LAYERS, dq, D_MODEL), BETA_2 * dq ** -0.5),
        "wa_sinks": nrm(ks[15], (N_WA_LAYERS, N_HEADS), 0.5),
    }

def second_block(x, c, ctx, c_ctx, w_mod, b_mod, ln_g, ln_b, ffn_w_in, ffn_w_out,
              na_w_qkv, na_w_o, na_rpb, wa_w_qkv, wa_w_o, wa_sinks):
    h_lat, h_ctx = x, ctx
    silu_c = jax.nn.silu(c)
    silu_cc = jax.nn.silu(c_ctx)
    for i in range(DEPTH):
        ctx_needed = i < DEPTH - 1
        m_lat = jnp.split((silu_c @ w_mod[i] + b_mod[i])[:, None, :], N_MOD, axis=-1)
        m_ctx = jnp.split((silu_cc @ w_mod[i] + b_mod[i])[None, None, :], N_MOD, axis=-1)

        h_lat = ffn_sublayer(h_lat, m_lat[0], m_lat[1], m_lat[2], ffn_w_in[i, 0], ffn_w_out[i, 0], ln_g[i, 0], ln_b[i, 0])
        h_ctx = ffn_sublayer(h_ctx, m_ctx[0], m_ctx[1], m_ctx[2], ffn_w_in[i, 0], ffn_w_out[i, 0], ln_g[i, 0], ln_b[i, 0])

        u_lat = modulate(h_lat, m_lat[3], m_lat[4])
        u_ctx = modulate(h_ctx, m_ctx[3], m_ctx[4])
        j = i // N_MIXERS
        if i % N_MIXERS == 0:
            y_lat, y_ctx = neighborhood_attention(u_lat, u_ctx, na_w_qkv[j], na_w_o[j], na_rpb[j], ctx_needed)
        else:
            y_lat, y_ctx = window_gqa(u_lat, u_ctx, wa_w_qkv[j], wa_w_o[j], wa_sinks[j], ctx_needed)
        h_lat = layer_norm_2(ALPHA_2 * h_lat + m_lat[5] * y_lat, ln_g[i, 1], ln_b[i, 1])

        h_lat = ffn_sublayer(h_lat, m_lat[6], m_lat[7], m_lat[8], ffn_w_in[i, 1], ffn_w_out[i, 1], ln_g[i, 2], ln_b[i, 2])
        if ctx_needed:
            h_ctx = layer_norm_2(ALPHA_2 * h_ctx + m_ctx[5] * y_ctx, ln_g[i, 1], ln_b[i, 1])
            h_ctx = ffn_sublayer(h_ctx, m_ctx[6], m_ctx[7], m_ctx[8], ffn_w_in[i, 1], ffn_w_out[i, 1], ln_g[i, 2], ln_b[i, 2])
    return h_lat


def setup_inputs(seed=0):
    out = dict(first_inputs(seed))
    for name, value in second_inputs(seed + 1).items():
        if name != "x":
            out[name + "_2"] = value
    return out


def reference(
    x, meta_tokens, emb_ln_g, emb_ln_b, rel_bias, w_in, conv_dw, conv_b, conv_ln_g, conv_ln_b,
    sinks, w_attn_proj, w_conv_proj, w_out, ln1_g, ln1_b, ffn_w_gate, ffn_w_up, ffn_w_down,
    router, moe_w_gate, moe_w_up, moe_w_down, ln2_g, ln2_b, c_2, ctx_2, c_ctx_2, w_mod_2,
    b_mod_2, ln_g_2, ln_b_2, ffn_w_in_2, ffn_w_out_2, na_w_qkv_2, na_w_o_2, na_rpb_2,
    wa_w_qkv_2, wa_w_o_2, wa_sinks_2,
):
    x = first_block(
        x, meta_tokens, emb_ln_g, emb_ln_b, rel_bias, w_in, conv_dw, conv_b, conv_ln_g,
        conv_ln_b, sinks, w_attn_proj, w_conv_proj, w_out, ln1_g, ln1_b, ffn_w_gate, ffn_w_up,
        ffn_w_down, router, moe_w_gate, moe_w_up, moe_w_down, ln2_g, ln2_b,
    )
    return second_block(
        x, c_2, ctx_2, c_ctx_2, w_mod_2, b_mod_2, ln_g_2, ln_b_2, ffn_w_in_2, ffn_w_out_2,
        na_w_qkv_2, na_w_o_2, na_rpb_2, wa_w_qkv_2, wa_w_o_2, wa_sinks_2,
    )


_drawn_inputs = setup_inputs


def setup_inputs(seed=0):
    import zlib

    import numpy as np

    out = dict(_drawn_inputs(seed))
    spreads = {}
    factors = {'conv_b': 4.659,
     'conv_ln_g': 14.112,
     'conv_ln_b': 26.286,
     'sinks': 23.664,
     'ctx_2': 121.39,
     'b_mod_2': 7.934,
     'na_rpb_2': 64.0,
     'wa_sinks_2': 143.894,
     'rel_bias': 2.817,
     'c_ctx_2': 3.21}
    for name, (base, spread) in spreads.items():
        noise = np.random.default_rng([zlib.crc32(name.encode()), seed]).standard_normal(out[name].shape)
        drawn = base * np.exp(spread * noise) if base else spread * noise
        out[name] = __import__('jax').numpy.asarray(drawn.astype(out[name].dtype))
    for name, factor in factors.items():
        out[name] = (out[name] * factor).astype(out[name].dtype)
    return out
```

```python
import math
from contextlib import ExitStack, nullcontext

import numpy as np

import concourse.bass as bass
import concourse.mybir as mybir

F32 = mybir.dt.float32
F32R = mybir.dt.float32r
U32 = mybir.dt.uint32
ACT = mybir.ActivationFunctionType
ALU = mybir.AluOpType
AX_X = mybir.AxisListType.X

P = 128
D = 1024
KC = D // P
NMETA, SEQ, CTX = 16, 256, 256
L1 = NMETA + SEQ
T2 = SEQ + CTX
TALL = L1 + CTX
DEPTH = 2
ALPHA = float((2 * DEPTH) ** 0.25)
EPS = 1e-5
HD = 64
SCALE = HD ** -0.5
D_EXP = 1408
KH = D_EXP // P
N_EXP = 8
CONVC = 512
KCV = CONVC // P
TAPS = 31
NBUCK = 32
NEG = -1e30
RAW_SLOTS = 4
W_STEP = 2048
MOD_STEPS = 2 * 9 * D // 256
MOD_PER_EXPERT = MOD_STEPS // N_EXP
BW = 400
RPB_R, RPB_C = 15, 31
RPB_LEN = 16 * RPB_R * RPB_C

C_ID, C_PERM, C_COS, C_SIN = 0, 128, 256, 512
C_NAM, C_WAM, C_IOTA, C_END = 768, 832, 1344, 1352

V_EMB = 0
V_LN1 = 16
V_LN2 = V_LN1 + 32
V_B = V_LN2 + 32
V_CLN = V_B + 96
V_CB = V_CLN + 16
V_DW = V_CB + 8
V_BM = V_DW + 2 * KCV * TAPS
V_END = V_BM + 144


def shape_constants():
    c = np.zeros((P, C_END), np.float32)
    c[:, C_ID:C_ID + P] = np.eye(P)
    inv = (10000.0 ** (-np.arange(16, dtype=np.float32) / 16)).astype(np.float32)
    t = np.arange(SEQ)
    for p in range(P):
        d = p % HD
        second = d % 32 >= 16
        partner = p - 16 if second else p + 16
        c[partner, C_PERM + p] = 1.0
        pos = (t // 64 if d < 32 else t % 64).astype(np.float32)
        ang = pos * inv[d % 16]
        c[p, C_COS:C_COS + SEQ] = np.cos(ang)
        c[p, C_SIN:C_SIN + SEQ] = np.sin(ang) * (1.0 if second else -1.0)
    qc, kc = np.arange(64)[:, None], np.arange(64)[None, :]
    start = np.clip(qc - 8, 0, 48)
    seen = (kc >= start) & (kc < start + 16)
    c[:, C_NAM:C_NAM + 64] = np.tile(np.where(seen, 0.0, NEG), (2, 1))
    for b in range(2):
        q = b * P + np.arange(P)[:, None]
        far = np.abs(q - np.arange(SEQ)[None, :]) > 128
        c[:, C_WAM + b * SEQ:C_WAM + (b + 1) * SEQ] = np.where(far, NEG, 0.0)
    c[:, C_IOTA:C_IOTA + 8] = np.arange(8)
    oh = np.zeros((NBUCK + 1, 2, BW), np.float32)
    dist = L1 - np.arange(BW)
    n = np.maximum(dist, 0)
    nf = np.maximum(n, 1).astype(np.float32)
    large = 16 + (np.log(nf / np.float32(16)) / np.float32(math.log(8)) * 16).astype(np.int32)
    bucket = np.where(n < 16, n, np.minimum(large, 31))
    for v in range(2):
        oh[bucket, v, np.arange(BW)] = 1.0
        masked = (dist < 0) | ((dist >= 128) if v else False)
        oh[NBUCK, v] = np.where(masked, 1.0, 0.0)
    return c, oh.reshape(NBUCK + 1, 2 * BW)


class Phase:

    def __init__(self, prev, n_iter, kinds, cols):
        self.n_iter, self.kinds, self.cols, self.n = n_iter, kinds, cols, len(kinds)
        if prev is None:
            self.g0 = self.a0 = self.d0 = 0
            self.raw0 = [0] * RAW_SLOTS
            pn = 0
        else:
            self.g0 = prev.g0 + prev.n * prev.n_iter
            self.a0 = prev.a0 + prev.kinds.count("a") * prev.n_iter
            self.d0 = prev.d0 + prev.kinds.count("d") * prev.n_iter
            self.raw0 = [prev.raw0[r] + prev.n_iter * len(range(r, prev.n, RAW_SLOTS)) for r in range(RAW_SLOTS)]
            pn = prev.n
        self.skip = max(-self.n % RAW_SLOTS, -pn % RAW_SLOTS)
        self.odd = self.n % 2 or pn % 2

    def step(self, i, s):
        return self.g0 + s + i * self.n

    def evacs(self, kind, i, s):
        base = self.a0 if kind == "a" else self.d0
        return base + self.kinds[:s].count(kind) + i * self.kinds.count(kind)

    def loads(self, i, s):
        r = s % RAW_SLOTS
        per = len(range(r, self.n, RAW_SLOTS))
        return self.raw0[r] + s // RAW_SLOTS + 1 + i * per


def plan():
    ph = {}
    prev = None
    full, down = [W_STEP] * KH, [D_EXP] * KC

    def add(name, n_iter, kinds, cols=None):
        nonlocal prev
        prev = ph[name] = Phase(prev, n_iter, kinds, cols or [W_STEP] * len(kinds))
        prev.name, prev.last = name, name == "fb1"

    moe_kinds, moe_cols = "", []
    for k in range(KH):
        moe_kinds += "d" + ("a" if k < MOD_PER_EXPERT else "")
        moe_cols += [W_STEP] * (2 if k < MOD_PER_EXPERT else 1)
    for i in range(2):
        add(f"win{i}", 1, "aaa" + "dddd" + "a" * 8)
        add(f"proj{i}", 1, "dddd")
        add(f"wout{i}", 1, "dddd")
        if i == 0:
            add("ffn", 2, "d" * 19, full + down)
        else:
            add("moe", N_EXP, moe_kinds + "d" * 8, moe_cols + down)
    for i in range(2):
        add(f"fa{i}", 2, "d" * 19, full + down)
        if i == 0:
            add("naqkv", 3, "aaaa")
        else:
            add("waqkv", 1, "aaaaaa")
        add(f"wo{i}", 1, "dddd")
        add(f"fb{i}", 2, "d" * 19, full + down)
    return ph


class Tally:

    def __init__(self, sem):
        self.sem, self.n, self.off = sem, 0, 0

    def inc(self, ins, by=1):
        self.n += by
        ins.then_inc(self.sem, by)
        return ins

    @property
    def value(self):
        return self.n + self.off


def build(nc, ins, out, upto=99):
    ph = plan()
    names = list(ph)
    ctx = ExitStack()
    with ctx:
        def sb(name, shape, dt=F32, where=None):
            return (where or ctx).enter_context(nc.sbuf_tensor(name, shape, dt))

        def sem(name):
            return ctx.enter_context(nc.semaphore(name))

        RAW = sb("RAW", [P, RAW_SLOTS, W_STEP])
        WH = [sb(f"WH{h}", [P, W_STEP], F32R) for h in range(2)]
        WL = [sb(f"WL{h}", [P, W_STEP], F32R) for h in range(2)]
        H = sb("H", [P, KC, TALL])
        UH = sb("UH", [P, KC, TALL], F32R)
        UL = sb("UL", [P, KC, TALL], F32R)
        TMP = sb("TMP", [P, 4, T2])
        STD = sb("STD", [P, T2])
        RSTD = sb("RSTD", [P, T2])
        CST = sb("CST", [P, C_END])
        VEC = sb("VEC", [P, V_END])
        MOD = sb("MOD", [P, MOD_STEPS, 2, 2])
        RT = sb("RT", [P, KC, N_EXP])
        CC = sb("CC", [P, KC, 2])
        SCF = sb("SCF", [P, KC, 2])
        SCH = sb("SCH", [P, KC, 2], F32R)
        SCL = sb("SCL", [P, KC, 2], F32R)
        ONES = sb("ONES", [P, P])
        ONESC = sb("ONESC", [P, P])
        EPST = sb("EPST", [P, 1])
        SK1 = sb("SK1", [P, 2, 8])
        SK2 = sb("SK2", [P, 16])
        NSK1 = sb("NSK1", [P, 2, 8])
        NSK2 = sb("NSK2", [P, 16])
        NM = sb("NM", [P, 2])
        NMX = sb("NMX", [P, 2])
        DEN = sb("DEN", [P, 2])
        ESK = sb("ESK", [P, 2])
        RDEN = sb("RDEN", [P, 2])
        LG = sb("LG", [P, 2, 8])
        MX8 = sb("MX8", [P, 2, 8])
        IX8 = sb("IX8", [P, 2, 8], U32)
        IXF = sb("IXF", [P, 2, 8])
        OH1 = sb("OH1", [P, 2, 8])
        OH2 = sb("OH2", [P, 2, 8])
        GT = sb("GT", [P, 2, 4])
        with ExitStack() as region:
            HIDH = sb("HIDH", [P, KH, T2], F32R, region)
            HIDL = sb("HIDL", [P, KH, T2], F32R, region)
            SIL = sb("SIL", [P, 2, T2], where=region)
            HT = sb("HT", [P, 2, T2], where=region)
            CB = sb("CB", [P, N_EXP, SEQ], where=region)
            CBB = sb("CBB", [P, 2, N_EXP, P], where=region)
        with ExitStack() as region:
            QKV = sb("QKV", [P, 24, T2], where=region)
            NB = sb("NB", [P, 2, 2, SEQ], where=region)
            QS2 = sb("QS2", [P, T2], where=region)
            KS2 = sb("KS2", [P, T2], where=region)
            VT2 = sb("VT2", [P, T2], where=region)
            VS2 = sb("VS2", [P, 4, P], where=region)
            SB2 = sb("SB2", [P, 2, T2], where=region)
            PT2 = sb("PT2", [P, 2, T2], where=region)
            OS2 = sb("OS2", [P, 4, P], where=region)
        with ExitStack() as region:
            SG = sb("SG", [P, 16, L1], where=region)
            HPAD = sb("HPAD", [P, KCV, TAPS - 1 + L1], where=region)
            CONV = sb("CONV", [P, KCV, L1], where=region)
            QS1 = sb("QS1", [P, L1], where=region)
            VS1 = sb("VS1", [P, 3, P], where=region)
            SB1 = sb("SB1", [P, 2, T2], where=region)
            PT1 = sb("PT1", [P, 2, T2], where=region)
            OS1 = sb("OS1", [P, 3, P], where=region)
            OHT = sb("OHT", [NBUCK + 1, 2 * BW], where=region)
            BROW = sb("BROW", [8, 2 * BW], where=region)
            RB = sb("RB", [NBUCK + 1, 8], where=region)
            with ExitStack() as sub:
                Q1 = sb("Q1", [P, 6, L1], where=sub)
                B1 = [sb(f"B1_{q}", [P, 8, n], where=sub) for q, n in enumerate((NMETA, NMETA + P, L1))]
            with ExitStack() as sub:
                MIXH = sb("MIXH", [P, KC, L1], F32R, sub)
                MIXL = sb("MIXL", [P, KC, L1], F32R, sub)
        PS = [ctx.enter_context(nc.psum_tensor(f"PS{b}", [P, 512], F32)) for b in range(8)]
        bias_rows = nc.dram_tensor("bias_rows", (8, 2, P, BW), F32, kind="Internal").ap()
        rpb_rows = nc.dram_tensor("rpb_rows", (64, RPB_LEN), F32, kind="Internal").ap()
        na_bias = nc.dram_tensor("na_bias", (8, 2, 64, 2, 2, SEQ), F32, kind="Internal").ap()

        IDENT = CST[:, C_ID:C_ID + P]

        s_const = sem("s_const")
        s_x = sem("s_x")
        s_raw = [sem(f"s_raw{r}") for r in range(RAW_SLOTS)]
        s_hi = sem("s_hi")
        s_lo = sem("s_lo")
        s_step = sem("s_step")
        s_eva = sem("s_eva")
        s_evd = sem("s_evd")
        s_ms = sem("s_ms")
        s_uh = sem("s_uh")
        s_ul = sem("s_ul")
        s_um = sem("s_um")
        s_hs = sem("s_hs")
        s_hid = sem("s_hid")
        s_hidl = sem("s_hidl")
        s_sil = sem("s_sil")
        s_mean = sem("s_mean")
        s_xc = sem("s_xc")
        s_sq = sem("s_sq")
        s_sqf = sem("s_sqf")
        s_std = sem("s_std")
        s_nrm = sem("s_nrm")
        s_ln = sem("s_ln")
        s_dve = sem("s_dve")
        s_sc = sem("s_sc")
        s_sb = sem("s_sb")
        s_ex = sem("s_ex")
        s_tp = sem("s_tp")
        s_pt = sem("s_pt")
        s_pv = sem("s_pv")
        s_o = sem("s_o")
        s_ot = sem("s_ot")
        s_ath = sem("s_ath")
        s_atl = sem("s_atl")
        s_stq = sem("s_stq")
        s_stk = sem("s_stk")
        s_vt = sem("s_vt")
        s_vs = sem("s_vs")
        s_nbd = sem("s_nbd")
        s_nb = sem("s_nb")
        s_rpb = sem("s_rpb")
        s_nas = sem("s_nas")
        s_brow = sem("s_brow")
        s_browd = sem("s_browd")
        s_b1 = sem("s_b1")
        s_cv = sem("s_cv")
        s_mix = sem("s_mix")
        s_mixh = sem("s_mixh")
        s_mixl = sem("s_mixl")
        s_rt = sem("s_rt")
        s_gate = sem("s_gate")
        s_gexp = sem("s_gexp")
        s_cbp = sem("s_cbp")
        s_cb = sem("s_cb")
        s_silc = sem("s_silc")
        s_mod = sem("s_mod")
        s_rsw = sem("s_rsw")
        s_rope = sem("s_rope")
        s_out = sem("s_out")

        block = ctx.enter_context(nc.Block())

        U_BEFORE = ["win0", "ffn", "win1", "moe", "fa0", "naqkv", "fb0", "fa1", "waqkv", "fb1"]
        U_IDX = {n: k for k, n in enumerate(U_BEFORE)}
        S_BEFORE = ["ffn", "moe", "fa0", "naqkv", "fb0", "fa1", "waqkv", "fb1"]
        S_IDX = {n: k for k, n in enumerate(S_BEFORE)}
        LNS = ["emb", "cv0", "a0", "b0", "cv1", "a1", "b1", "2a0", "2n0", "2b0", "2a1", "2n1", "2b1"]
        LN_IDX = {n: k for k, n in enumerate(LNS)}
        LN_BASE, base = {}, 0
        for n in LNS:
            LN_BASE[n] = base
            base += KCV if n.startswith("cv") else KC
        UM_IDX = {n: k for k, n in enumerate(["fa0", "naqkv", "fb0", "fa1", "waqkv", "fb1"])}
        SIL_BASE, base = {}, 0
        for n in ("win0", "ffn", "win1", "moe", "fa0", "fb0", "fa1", "fb1"):
            SIL_BASE[n] = base
            base += KCV if n.startswith("win") else KH * ph[n].n_iter
        HID_BASE, base = {}, 0
        for n in ("ffn", "moe", "fa0", "fb0", "fa1", "fb1"):
            HID_BASE[n] = base
            base += KH * ph[n].n_iter

        def iterate(eng, p, body):
            if p.last:
                for i in range(p.n_iter):
                    body(i)
            else:
                with eng.Fori(0, p.n_iter) as i:
                    body(i)

        def pairs_of_heads(eng, a):
            if a.name == "b0":
                return [nullcontext(i) for i in range(a.inner)]
            return [eng.Fori(0, a.inner)]

        class Att:
            pass

        atts = {}
        unit = kvn = its = 0
        for name, nq, groups, inner, kv_dyn in (
                ("b0", 3, 1, 4, False), ("b1", 2, 1, 4, False), ("na", 4, 1, 8, True), ("wa", 2, 2, 4, False)):
            a = atts[name] = Att()
            a.name, a.groups, a.inner, a.kv_dyn = name, groups, inner, kv_dyn
            a.units = 2 * nq
            a.unit0, a.it0, a.kv0 = unit, its, kvn
            unit += a.units * groups * inner
            its += groups * inner
            kvn += groups * (inner if kv_dyn else 1)
            if name[0] == "b":
                a.layer = int(name[1])
                a.qts = [(0, NMETA), (NMETA, P), (NMETA + P, P)][-nq:]
                a.keys = [(0, NMETA), (0, NMETA + P), (0, L1)][-nq:]
                a.vt = [(0, NMETA), (NMETA, P), (NMETA + P, P)]
                a.qs, a.vs, a.sbf, a.pt, a.os = QS1, VS1, SB1, PT1, OS1
                a.u0 = 0
            else:
                a.layer = 0 if name == "na" else 1
                a.qts = [(0, P), (P, P), (2 * P, P), (3 * P, P)][:nq]
                a.keys = [(0, T2), (0, T2), (SEQ, CTX), (SEQ, CTX)][:nq]
                a.vt = [(j * P, P) for j in range(4)]
                a.qs, a.vs, a.sbf, a.pt, a.os = QS2, VS2, SB2, PT2, OS2
                a.u0 = NMETA
            a.sink = name != "na"
            a.lo = a.qts[0][0]
            a.hi = a.qts[-1][0] + a.qts[-1][1]

        def unit_of(a, u):
            half, qt = divmod(u, len(a.qts))
            k0, nk = a.keys[qt]
            tiles = [j for j, (c, n) in enumerate(a.vt) if c >= k0 and c + n <= k0 + nk]
            return half, qt, k0, nk, tiles

        def two_ago(a, it, u):
            return a.unit0 + it * a.units + max(u - 1, 0)

        def reach(eng, sm, value):
            if not (isinstance(value, int) and value <= 0):
                eng.wait_ge(sm, value)

        def vec(col, n=1):
            return VEC[:, col:col + n]

        def mod(layer, idx, c, s):
            t = layer * 72 + idx * KC + c
            return MOD[:, t // 2, t % 2, s:s + 1]

        STREAM = [(NMETA, SEQ), (L1, CTX)]

        @block.sync
        def _(sp):
            def load(p, i, s, src):
                g = p.step(i, s)
                lag = RAW_SLOTS - (p.skip if s < RAW_SLOTS else 0)
                if not (isinstance(g, int) and g < lag):
                    sp.wait_ge(s_lo, g - lag + 1)
                sp.dma_start(RAW[:, s % RAW_SLOTS, 0:p.cols[s]], src).then_inc(s_raw[s % RAW_SLOTS], 16)

            def straight(name, w, k0=0):
                p = ph[name]
                for s in range(p.n):
                    load(p, 0, s, w[k0 + s])

            def experts(name, e0, with_mod=False):
                p = ph[name]

                def body(i):
                    s = 0
                    for k in range(KH):
                        load(p, i, s, ins["w_gu"][i + e0, k])
                        s += 1
                        if with_mod and k < MOD_PER_EXPERT:
                            load(p, i, s, ins["w_mod"][i * MOD_PER_EXPERT + k])
                            s += 1
                    for m in range(KC):
                        load(p, i, s, ins["w_dn"][i + e0, m])
                        s += 1

                iterate(sp, p, body)

            def bias_tiles(layer):
                if layer == 0:
                    sp.wait_ge(s_brow, 4)
                    for v in range(2):
                        row = BROW[:, v * BW:(v + 1) * BW].rearrange("h (a w) -> h a w", a=1)
                        sp.dma_start(bias_rows[:, v], row.to_broadcast([8, P, BW])).then_inc(s_browd, 16)
                    sp.wait_ge(s_browd, 32)
                else:
                    sp.wait_ge(s_step, ph["win1"].g0)
                for q, (q0, nq) in enumerate(((0, NMETA), (NMETA, P), (NMETA + P, P))):
                    nk = q0 + nq
                    pieces = [(0, 0, NMETA)] + ([(1, NMETA, nk - NMETA)] if q else [])
                    for v, k0, n in pieces:
                        src = bass.AP(tensor=bias_rows.tensor, offset=v * P * BW + L1 - q0 + k0,
                                      ap=[[BW - 1, nq], [2 * P * BW, 8], [1, n]])
                        sp.dma_start(B1[q][0:nq, :, k0:k0 + n], src).then_inc(s_b1, 16)

            for i in range(DEPTH):
                if i == 0:
                    for s in range(3):
                        load(ph["win0"], 0, s, ins["w_in"][0, s])
                    bias_tiles(0)
                    for s in range(3, 15):
                        load(ph["win0"], 0, s, ins["w_in"][0, s])
                else:
                    straight(f"win{i}", ins["w_in"][i])
                    bias_tiles(1)
                straight(f"proj{i}", ins["w_proj"][i])
                straight(f"wout{i}", ins["w_out"][i])
                if i == 0:
                    experts("ffn", 0)
                else:
                    experts("moe", 2, True)
            for i in range(DEPTH):
                experts(f"fa{i}", 2 + N_EXP + 4 * i)
                if i == 0:
                    p = ph["naqkv"]
                    with sp.Fori(0, p.n_iter) as it:
                        for s in range(4):
                            load(p, it, s, ins["w_na"][it * 4 + s])
                else:
                    straight("waqkv", ins["w_wa"])
                straight(f"wo{i}", ins["w_o"][i])
                if i == 0:
                    a = atts["na"]
                    sp.wait_ge(s_nas, 16 * 64)
                    sp.wait_ge(s_step, ph["naqkv"].g0)
                    with sp.Fori(0, a.inner) as it:
                        sp.wait_ge(s_sb, a.unit0 + it * a.units)
                        sp.dma_start(NB[:, :, :, :], na_bias[it].rearrange("r q a h k -> (r q) a h k"))\
                            .then_inc(s_nbd, 16)
                experts(f"fb{i}", 2 + N_EXP + 4 * i + 2)
            sp.wait_ge(s_ln, LN_BASE["2b1"] + KC)
            sp.dma_start(out, H[:, :, NMETA:L1]).then_inc(s_out, 16)
            sp.wait_ge(s_out, 16)

        @block.gpsimd
        def _(pool):
            pool.memset(ONES[:, :], 1.0 / D).then_inc(s_ms, 1)
            pool.memset(ONESC[:, :], 1.0 / CONVC).then_inc(s_ms, 1)
            pool.memset(EPST[:, :], EPS).then_inc(s_ms, 1)
            pool.dma_start(rpb_rows, ins["na_rpb"].to_broadcast([64, RPB_LEN])).then_inc(s_rpb, 16)
            pool.wait_ge(s_rpb, 16)
            for qr in range(4):
                for h in range(16):
                    src = bass.AP(tensor=rpb_rows.tensor,
                                  offset=h * RPB_R * RPB_C + (7 - qr) * RPB_C + 15,
                                  ap=[[RPB_LEN - 1, 64], [RPB_C, 4], [1, 64]])
                    dst = na_bias[h // 2, qr % 2, :, qr // 2, h % 2, :].rearrange("q (r k) -> q r k", r=4)
                    pool.dma_start(dst, src).then_inc(s_nas, 16)
            for i in range(DEPTH):
                if i == 1:
                    pool.wait_ge(s_step, ph["win1"].g0)
                pool.memset(HPAD[:, :, 0:TAPS - 1], 0.0).then_inc(s_ms, 1)
                a = atts[f"b{i}"]
                pool.wait_ge(s_eva, ph[f"win{i}"].evacs("a", 0, 3))
                for loop in pairs_of_heads(pool, a):
                    with loop as it:
                        reach(pool, s_sc, a.unit0 + it * a.units)
                        pool.tensor_copy(QS1[:, :], Q1[:, bass.ds(it, 1), :].rearrange("p a t -> p (a t)"))\
                            .then_inc(s_stq, 1)
            a = atts["na"]
            pool.wait_ge(s_eva, ph["naqkv"].evacs("a", 3, 0))
            with pool.Fori(0, a.inner) as it:
                def chunk(first):
                    return QKV[:, bass.ds(first + it, 1), :].rearrange("p a t -> p (a t)")
                pool.wait_ge(s_sc, a.unit0 + it * a.units)
                pool.tensor_copy(QS2[:, :], chunk(0)).then_inc(s_stq, 1)
                pool.tensor_copy(KS2[:, :], chunk(8)).then_inc(s_stk, 1)
                pool.wait_ge(s_vt, a.kv0 + it)
                pool.tensor_copy(VT2[:, :], chunk(16)).then_inc(s_stk, 1)
                pool.wait_ge(s_nbd, it * 16 + 16)
                mask = CST[:, C_NAM:C_NAM + 64].rearrange("p (a k) -> p a k", a=1).to_broadcast([P, 16, 64])
                nbv = NB[:, :, :, :].rearrange("p a h (r k) -> p (a h r) k", r=4)
                pool.tensor_tensor(nbv, nbv, mask, ALU.add).then_inc(s_nb, 1)
            a = atts["wa"]
            pool.wait_ge(s_rope, 10)
            for grp in range(a.groups):
                with pool.Fori(0, a.inner) as it:
                    pool.wait_ge(s_sc, a.unit0 + (grp * a.inner + it) * a.units)
                    pool.tensor_copy(QS2[:, 0:SEQ], QKV[:, bass.ds(grp * a.inner + it, 1), 0:SEQ]
                                     .rearrange("p a t -> p (a t)")).then_inc(s_stq, 1)

        @block.tensor
        def _(pe):
            def product(ps, lhs, terms_h, terms_l, n):
                last = None
                for k in range(n):
                    wh, wl = lhs(k)
                    pe.matmul(ps, wh, terms_h(k), start=(k == 0), stop=False)
                    pe.matmul(ps, wh, terms_l(k), start=False, stop=False)
                    last = pe.matmul(ps, wl, terms_h(k), start=False, stop=(k == n - 1))
                return last

            def begin(p, i, s, wait_banks=True):
                pe.wait_ge(s_lo, p.step(i, s) + 1)
                if s >= 2:
                    kind = p.kinds[s - 2]
                    pe.wait_ge(s_eva if kind == "a" else s_evd, p.evacs(kind, i, s - 1))
                elif p.n_iter > 1:
                    kind = p.kinds[-1]
                    pe.wait_ge(s_eva if kind == "a" else s_evd,
                               p.evacs(kind, i, 0) - (0 if p.n % 2 or s else 1))

            def all_evacuated(p):
                if p.a0:
                    pe.wait_ge(s_eva, p.a0)
                if p.d0:
                    pe.wait_ge(s_evd, p.d0)

            def slot(s, off):
                return WH[s % 2][:, off:off + P], WL[s % 2][:, off:off + P]

            def pair_step(p, i, s, c0, n, xh=UH, xl=UL):
                begin(p, i, s)
                for j in range(2):
                    last = product(PS[4 * (s % 2) + j][:, 0:n], lambda k: slot(s, k * 256 + j * P),
                                   lambda k: xh[:, k, c0:c0 + n], lambda k: xl[:, k, c0:c0 + n], KC)
                last.then_inc(s_step, 1)

            def experts(name, c0, n):
                p = ph[name]
                all_evacuated(p)
                pe.wait_ge(s_ul, KC * (U_IDX[name] + 1))

                def body(i):
                    s = 0
                    for k in range(KH):
                        pair_step(p, i, s, c0, n)
                        s += 1
                        if p.kinds[s] == "a":
                            begin(p, i, s)
                            for j in range(2):
                                last = product(PS[4 * (s % 2)][:, 2 * j:2 * j + 2],
                                               lambda k: slot(s, k * 256 + j * P),
                                               lambda k: SCH[:, k, :], lambda k: SCL[:, k, :], KC)
                            last.then_inc(s_step, 1)
                            s += 1
                    for m in range(KC):
                        begin(p, i, s)
                        if m == 0:
                            pe.wait_ge(s_hidl, HID_BASE[name] + KH + i * KH)
                        product(PS[4 * (s % 2)][:, 0:n], lambda k: slot(s, k * P),
                                lambda k: HIDH[:, k, 0:n], lambda k: HIDL[:, k, 0:n], KH).then_inc(s_step, 1)
                        s += 1

                iterate(pe, p, body)

            def straight(name, c0, n, u=True, ranges=None, xh=UH, xl=UL):
                p = ph[name]
                all_evacuated(p)
                if u:
                    pe.wait_ge(s_ul, KC * (U_IDX[name] + 1))
                for s in range(p.n):
                    cc, nn = ranges[s] if ranges else (c0, n)
                    pair_step(p, 0, s, cc, nn, xh, xl)

            def norm(name, src, ones, c0, n, waits):
                b0, cs = LN_BASE[name], (KCV if name.startswith("cv") else KC)
                for sm, v in waits:
                    pe.wait_ge(sm, v)
                for c in range(cs):
                    last = pe.matmul(PS[0][:, 0:n], ones[:, :], src[:, c, c0:c0 + n], start=(c == 0), stop=(c == cs - 1))
                last.then_inc(s_mean, 1)
                for c in range(cs):
                    pe.wait_ge(s_sq, b0 + c + 1)
                    last = pe.matmul(PS[1][:, 0:n], ones[:, :], TMP[:, c % 4, 0:n], start=(c == 0), stop=(c == cs - 1))
                    last.then_inc(s_sqf, 1)

            def attention(name):
                a = atts[name]
                first = name[0] == "b"
                ksrc = Q1[:, 4, :] if first else KS2[:, :]
                def values(kv):
                    if a.kv_dyn:
                        pe.wait_ge(s_stk, 2 * (kv + 1))
                        pe.wait_ge(s_vs, a.kv0 + kv)
                    for j, (c, nt) in enumerate(a.vt):
                        last = pe.transpose(PS[7][0:nt, j * P:(j + 1) * P], a.vsrc[:, c:c + nt], IDENT)
                    last.then_inc(s_vt, 1)

                def scores(it, u):
                    half, qt, k0, nk, _ = unit_of(a, u)
                    q0, nq = a.qts[qt]
                    r = slice(HD * half, HD * half + HD)
                    reach(pe, s_sb, two_ago(a, it, u))
                    pe.matmul(PS[u % 2][0:nq, 0:nk], a.qs[r, q0:q0 + nq], ksrc_of(it)[r, k0:k0 + nk],
                              start=True, stop=True).then_inc(s_sc, 1)

                def ksrc_of(it):
                    return a.ksrc

                def turn(it, u):
                    half, qt, k0, nk, tiles = unit_of(a, u)
                    nq = a.qts[qt][1]
                    g = a.unit0 + it * a.units + u
                    pe.wait_ge(s_ex, g + 1)
                    reach(pe, s_pt, two_ago(a, it, u))
                    for x, j in enumerate(tiles):
                        c, nt = a.vt[j]
                        last = pe.transpose(PS[2 + u % 2][0:nt, x * P:x * P + nq],
                                            a.sbf[0:nq, u % 2, c - k0:c - k0 + nt], IDENT[0:nq, 0:nq])
                    last.then_inc(s_tp, 1)

                def times_values(it, u, kv):
                    half, qt, k0, nk, tiles = unit_of(a, u)
                    nq = a.qts[qt][1]
                    g = a.unit0 + it * a.units + u
                    if u == 0:
                        pe.wait_ge(s_vs, a.kv0 + kv + 1)
                    pe.wait_ge(s_pt, g + 1)
                    reach(pe, s_o, two_ago(a, it, u))
                    for x, j in enumerate(tiles):
                        nt = a.vt[j][1]
                        last = pe.matmul(PS[4 + u % 2][0:nq, 0:HD], a.pt[0:nt, u % 2, x * P:x * P + nq],
                                         a.vs[0:nt, j, HD * half:HD * half + HD],
                                         start=(x == 0), stop=(x == len(tiles) - 1))
                    last.then_inc(s_pv, 1)

                for grp in range(a.groups):
                    if first:
                        a.ksrc, a.vsrc = Q1[:, 4, :], Q1[:, 5, :]
                    elif a.kv_dyn:
                        a.ksrc, a.vsrc = KS2[:, :], VT2[:, :]
                    else:
                        a.ksrc, a.vsrc = QKV[:, 8 + grp, :], QKV[:, 10 + grp, :]
                    if not a.kv_dyn:
                        if grp:
                            pe.wait_ge(s_vs, a.kv0 + grp)
                        values(grp)
                    for loop in pairs_of_heads(pe, a):
                        with loop as i:
                            it = i + grp * a.inner
                            if a.kv_dyn:
                                values(it)
                            pe.wait_ge(s_stq, a.it0 + it + 1)
                            scores(it, 0)
                            scores(it, 1)
                            for u in range(a.units):
                                turn(it, u)
                                if u + 2 < a.units:
                                    scores(it, u + 2)
                                times_values(it, u, it if a.kv_dyn else grp)
                            pe.wait_ge(s_o, a.unit0 + it * a.units + a.units)
                            reach(pe, s_atl, a.it0 + it)
                            for q, (q0, nq) in enumerate(a.qts):
                                last = pe.transpose(PS[6][:, q0:q0 + nq], a.os[0:nq, q, :], IDENT[0:nq, 0:nq])
                            last.then_inc(s_ot, 1)

            pe.wait_ge(s_ms, 3)
            pe.wait_ge(s_const, 16 * 10)
            pe.matmul(PS[0][0:8, 0:BW], RB[:, :], OHT[:, 0:BW], start=True, stop=True).then_inc(s_brow, 1)
            pe.matmul(PS[1][0:8, 0:BW], RB[:, :], OHT[:, BW:2 * BW], start=True, stop=True).then_inc(s_brow, 1)
            pe.wait_ge(s_brow, 4)
            norm("emb", H, ONES, 0, L1, [(s_x, 32)])
            for i in range(DEPTH):
                c0, n = (0, L1) if i == 0 else (NMETA, SEQ)
                straight(f"win{i}", 0, L1)
                pe.wait_ge(s_eva, ph[f"win{i}"].evacs("a", 0, 15))
                attention(f"b{i}")
                norm(f"cv{i}", CONV, ONESC, c0, n, [(s_cv, KCV * (i + 1))])
                p = ph[f"proj{i}"]
                all_evacuated(p)
                pe.wait_ge(s_atl, atts[f"b{i}"].it0 + 4)
                pe.wait_ge(s_ul, KC * (U_IDX["win0" if i == 0 else "win1"] + 1))
                pe.wait_ge(s_mixl, (KCV + KC) * i + KCV)
                for s in range(p.n):
                    begin(p, 0, s)
                    for m in range(2):
                        for b in range(2):
                            last = product(PS[4 * (s % 2) + 2 * m + b][:, 0:n],
                                           lambda k: slot(s, b * 1024 + k * 256 + m * P),
                                           lambda k: UH[:, 4 * b + k, c0:c0 + n],
                                           lambda k: UL[:, 4 * b + k, c0:c0 + n], KCV)
                    last.then_inc(s_step, 1)
                p = ph[f"wout{i}"]
                pe.wait_ge(s_mixl, (KCV + KC) * (i + 1))
                straight(f"wout{i}", c0, n, False, None, MIXH, MIXL)
                norm(f"a{i}", H, ONES, c0, n, [(s_evd, ph[f"wout{i}"].evacs("d", 0, 4))])
                if i == 1:
                    pe.wait_ge(s_ln, LN_BASE["a1"] + KC)
                    for t in range(2):
                        for k in range(KC):
                            last = pe.matmul(PS[2][:, 8 * t:8 * t + 8], H[:, k, NMETA + t * P:NMETA + (t + 1) * P],
                                             RT[:, k, :], start=(k == 0), stop=(k == KC - 1))
                    last.then_inc(s_rt, 1)
                    pe.wait_ge(s_gate, 2)
                    for t in range(2):
                        for e in range(N_EXP):
                            last = pe.matmul(PS[4 + e // 2][:, (e % 2) * SEQ + t * P:(e % 2) * SEQ + (t + 1) * P],
                                             CBB[:, t, e, :], IDENT, start=True, stop=True)
                    last.then_inc(s_cbp, 1)
                    pe.wait_ge(s_cb, 4)
                    pe.wait_ge(s_silc, 3)
                experts("moe" if i else "ffn", c0, n)
                nm = "moe" if i else "ffn"
                norm(f"b{i}", H, ONES, c0, n, [(s_evd, ph[nm].evacs("d", ph[nm].n_iter, 0))])
            for i in range(DEPTH):
                nb = T2 if i == 0 else SEQ
                experts(f"fa{i}", NMETA, T2)
                norm(f"2a{i}", H, ONES, NMETA, T2, [(s_evd, ph[f"fa{i}"].evacs("d", 2, 0))])
                if i == 0:
                    p = ph["naqkv"]
                    all_evacuated(p)
                    pe.wait_ge(s_ul, KC * (U_IDX["naqkv"] + 1))
                    with pe.Fori(0, p.n_iter) as it:
                        for s in range(4):
                            pair_step(p, it, s, NMETA, T2)
                    pe.wait_ge(s_eva, p.evacs("a", 3, 0))
                    attention("na")
                else:
                    p = ph["waqkv"]
                    straight("waqkv", 0, 0, True, [(NMETA, SEQ)] * 4 + [(NMETA, T2)] * 2)
                    pe.wait_ge(s_eva, p.evacs("a", 0, 6))
                    for c in range(10):
                        if c >= 2:
                            pe.wait_ge(s_rope, c - 1)
                        pe.matmul(PS[c % 2][:, 0:SEQ], CST[:, C_PERM:C_PERM + P], QKV[:, c, 0:SEQ],
                                  start=True, stop=True).then_inc(s_rsw, 1)
                    pe.wait_ge(s_rope, 10)
                    attention("wa")
                pe.wait_ge(s_atl, atts["na" if i == 0 else "wa"].it0 + 8)
                straight(f"wo{i}", NMETA, nb, False)
                norm(f"2n{i}", H, ONES, NMETA, nb, [(s_evd, ph[f"wo{i}"].evacs("d", 0, 4))])
                experts(f"fb{i}", NMETA, nb)
                norm(f"2b{i}", H, ONES, NMETA, nb, [(s_evd, ph[f"fb{i}"].evacs("d", 2, 0))])

        @block.scalar
        def _(act):
            for dst, src in ((CST[:, :], ins["consts"]), (VEC[:, :], ins["vectors"]), (OHT[:, :], ins["onehot"]),
                             (RB[0:NBUCK, :], ins["rel_bias"]), (RB[NBUCK:NBUCK + 1, :], ins["neg_row"]),
                             (RT[:, :, :], ins["router"]), (CC[:, :, :], ins["cond"])):
                act.dma_start(dst, src).then_inc(s_const, 16)
            for l in range(2):
                act.dma_start(SK1[:, l, :], ins["sinks"][l:l + 1, :].to_broadcast([P, 8])).then_inc(s_const, 16)
            act.dma_start(SK2[:, :], ins["sinks_2"].to_broadcast([P, 16])).then_inc(s_const, 16)
            act.dma_start(H[:, :, 0:L1], ins["tokens"]).then_inc(s_x, 16)
            act.dma_start(H[:, :, L1:TALL], ins["ctx"]).then_inc(s_x, 16)

            def high(p, i, s):
                act.wait_ge(s_raw[s % RAW_SLOTS], p.loads(i, s) * 16)
                g = p.step(i, s)
                need = g if (s == 0 and p.odd) else g - 1
                if not (isinstance(need, int) and need <= 0):
                    act.wait_ge(s_step, need)
                n = p.cols[s]
                act.activation(WH[s % 2][:, 0:n], RAW[:, s % RAW_SLOTS, 0:n], ACT.Copy).then_inc(s_hi, 1)

            def ahead(p, i, s):
                if s + 1 < p.n:
                    high(p, i, s + 1)
                elif p.n_iter > 1 and not (isinstance(i, int) and i + 1 == p.n_iter):
                    high(p, i + 1, 0)
                else:
                    nxt = names.index(p.name) + 1
                    if nxt < len(names):
                        high(ph[names[nxt]], 0, 0)

            def norm(name, src, dst, gcol, c0, n, func=ACT.Identity):
                b0, cs = LN_BASE[name], (KCV if name.startswith("cv") else KC)
                for c in range(cs):
                    act.wait_ge(s_xc, b0 + c + 1)
                    if b0 + c >= 4:
                        act.wait_ge(s_sqf, b0 + c - 3)
                    act.activation(TMP[:, c % 4, 0:n], src[:, c, c0:c0 + n], ACT.Square).then_inc(s_sq, 1)
                act.wait_ge(s_sqf, b0 + cs)
                act.activation(STD[:, 0:n], PS[1][:, 0:n], ACT.Sqrt, bias=EPST[:, 0:1]).then_inc(s_std, 1)
                for c in range(cs):
                    act.wait_ge(s_nrm, b0 + c + 1)
                    act.activation(dst[:, c, c0:c0 + n], src[:, c, c0:c0 + n], func,
                                   bias=vec(gcol + cs + c), scale=vec(gcol + c)).then_inc(s_ln, 1)

            def make_u(name, c0, n, modulated, ln):
                b = KC * U_IDX[name]
                for c in range(KC):
                    if modulated:
                        act.wait_ge(s_um, UM_IDX[name] * KC + c + 1)
                        act.activation(UH[:, c, c0:c0 + n], TMP[:, c % 4, 0:n], ACT.Copy).then_inc(s_uh, 1)
                    else:
                        if c == 0:
                            act.wait_ge(s_ln, LN_BASE[ln] + KC)
                        act.activation(UH[:, c, c0:c0 + n], H[:, c, c0:c0 + n], ACT.Copy).then_inc(s_uh, 1)

            def scale_h(name, c0, n):
                act.wait_ge(s_ul, KC * (U_IDX[name] + 1))
                if name == "moe":
                    act.wait_ge(s_rt, 1)
                act.mul(H[:, :, c0:c0 + n], H[:, :, c0:c0 + n], ALPHA).then_inc(s_hs, 1)

            def experts(name, n):
                p = ph[name]

                def body(i):
                    s = 0
                    for k in range(KH):
                        ahead(p, i, s)
                        act.wait_ge(s_step, p.step(i, s) + 1)
                        if k >= 2:
                            act.wait_ge(s_hidl, HID_BASE[name] + k - 1 + i * KH)
                        act.activation(SIL[:, k % 2, 0:n], PS[4 * (s % 2)][:, 0:n], ACT.Silu).then_inc(s_sil, 1)
                        act.wait_ge(s_evd, p.evacs("d", i, s + 1))
                        act.activation(HIDH[:, k, 0:n], HT[:, k % 2, 0:n], ACT.Copy).then_inc(s_hid, 1)
                        s += 1
                        if p.kinds[s] == "a":
                            ahead(p, i, s)
                            act.wait_ge(s_step, p.step(i, s) + 1)
                            act.activation(MOD[:, bass.ds(i * MOD_PER_EXPERT + k, 1), :, :]
                                           .rearrange("p a b c -> p (a b c)"),
                                           PS[4 * (s % 2)][:, 0:4], ACT.Copy).then_inc(s_eva, 1)
                            s += 1
                    for m in range(KC):
                        ahead(p, i, s)
                        s += 1

                iterate(act, p, body)

            def copy_step(p, i, s, dsts, n):
                ahead(p, i, s)
                act.wait_ge(s_step, p.step(i, s) + 1)
                act.activation(dsts[0], PS[4 * (s % 2)][:, 0:n], ACT.Copy)
                act.activation(dsts[1], PS[4 * (s % 2) + 1][:, 0:n], ACT.Copy).then_inc(s_eva, 1)

            def attention(name):
                a = atts[name]

                def exps(it, u):
                    half, qt, k0, nk, _ = unit_of(a, u)
                    nq = a.qts[qt][1]
                    b = u % 2
                    g = a.unit0 + it * a.units + u
                    act.wait_ge(s_sb, g + 1)
                    reach(act, s_o, two_ago(a, it, u))
                    last = act.activation(a.sbf[0:nq, b, 0:nk], a.sbf[0:nq, b, 0:nk], ACT.Exp, bias=NM[0:nq, b:b + 1],
                                          accum_out=DEN[0:nq, b:b + 1])
                    if a.sink:
                        c = 2 * it + half
                        col = SK1[:, a.layer, bass.ds(c, 1)] if name[0] == "b" else SK2[:, bass.ds(c, 1)]
                        last = act.activation(ESK[0:nq, b:b + 1], col[0:nq, :], ACT.Exp, bias=NM[0:nq, b:b + 1])
                    last.then_inc(s_ex, 1)

                def copy_turned(it, u):
                    half, qt, k0, nk, tiles = unit_of(a, u)
                    nq = a.qts[qt][1]
                    g = a.unit0 + it * a.units + u
                    act.wait_ge(s_tp, g + 1)
                    reach(act, s_pv, two_ago(a, it, u))
                    if nq == P and all(a.vt[j][1] == P for j in tiles):
                        act.activation(a.pt[:, u % 2, 0:len(tiles) * P], PS[2 + u % 2][:, 0:len(tiles) * P],
                                       ACT.Copy).then_inc(s_pt, 1)
                    else:
                        for x, j in enumerate(tiles):
                            nt = a.vt[j][1]
                            last = act.activation(a.pt[0:nt, u % 2, x * P:x * P + nq],
                                                  PS[2 + u % 2][0:nt, x * P:x * P + nq], ACT.Copy)
                        last.then_inc(s_pt, 1)

                def values(it, kv):
                    act.wait_ge(s_vt, a.kv0 + kv + 1)
                    reach(act, s_pv, a.unit0 + it * a.units)
                    for j, (c, nt) in enumerate(a.vt):
                        last = act.activation(a.vs[0:nt, j, :], PS[7][0:nt, j * P:(j + 1) * P], ACT.Copy)
                    last.then_inc(s_vs, 1)

                for grp in range(a.groups):
                    if not a.kv_dyn:
                        values(grp * a.inner, grp)
                    for loop in pairs_of_heads(act, a):
                        with loop as i:
                            it = i + grp * a.inner
                            if a.kv_dyn:
                                values(it, it)
                            exps(it, 0)
                            for u in range(a.units):
                                if u + 1 < a.units:
                                    exps(it, u + 1)
                                copy_turned(it, u)
                            act.wait_ge(s_ot, a.it0 + it + 1)
                            act.activation(UH[:, bass.ds(it, 1), a.u0 + a.lo:a.u0 + a.hi].rearrange("p a t -> p (a t)"),
                                           PS[6][:, a.lo:a.hi], ACT.Copy).then_inc(s_ath, 1)

            act.wait_ge(s_const, 16 * 10)
            act.activation(SCF[:, :, :], CC[:, :, :], ACT.Silu).then_inc(s_silc, 1)
            act.wait_ge(s_silc, 1)
            act.activation(SCH[:, :, :], SCF[:, :, :], ACT.Copy).then_inc(s_silc, 1)
            act.wait_ge(s_brow, 2)
            act.activation(BROW[:, 0:BW], PS[0][0:8, 0:BW], ACT.Copy).then_inc(s_brow, 1)
            act.activation(BROW[:, BW:2 * BW], PS[1][0:8, 0:BW], ACT.Copy).then_inc(s_brow, 1)
            high(ph["win0"], 0, 0)
            norm("emb", H, H, V_EMB, 0, L1)
            for i in range(DEPTH):
                c0, n = (0, L1) if i == 0 else (NMETA, SEQ)
                p = ph[f"win{i}"]
                make_u(f"win{i}", 0, L1, False, "emb" if i == 0 else "b0")
                for s in range(3):
                    copy_step(p, 0, s, (Q1[:, 2 * s, :], Q1[:, 2 * s + 1, :]), L1)
                for s in range(3, 7):
                    ahead(p, 0, s)
                    act.wait_ge(s_step, p.step(0, s) + 1)
                    if s >= 5:
                        act.wait_ge(s_evd, p.evacs("d", 0, s - 1))
                    act.activation(TMP[:, s % 2, 0:L1], PS[4 * (s % 2) + 1][:, 0:L1], ACT.Sigmoid).then_inc(s_sil, 1)
                for s in range(7, 15):
                    ahead(p, 0, s)
                    act.wait_ge(s_step, p.step(0, s) + 1)
                    for j in range(2):
                        last = act.activation(SG[:, 2 * (s - 7) + j, :], PS[4 * (s % 2) + j][:, 0:L1], ACT.Sigmoid)
                    last.then_inc(s_eva, 1)
                attention(f"b{i}")
                norm(f"cv{i}", CONV, CONV, V_CLN + 8 * i, c0, n, ACT.Silu)
                for c in range(KCV):
                    act.wait_ge(s_ln, LN_BASE[f"cv{i}"] + c + 1)
                    act.activation(UH[:, 4 + c, c0:c0 + n], CONV[:, c, c0:c0 + n], ACT.Copy).then_inc(s_mixh, 1)
                p = ph[f"proj{i}"]
                for s in range(4):
                    ahead(p, 0, s)
                    for m in range(2):
                        act.wait_ge(s_mix, KC * i + 2 * s + m + 1)
                        act.activation(MIXH[:, 2 * s + m, c0:c0 + n], TMP[:, 2 + m, 0:n], ACT.Copy).then_inc(s_mixh, 1)
                p = ph[f"wout{i}"]
                for s in range(4):
                    ahead(p, 0, s)
                norm(f"a{i}", H, H, V_LN1 + 16 * i, c0, n)
                nm = "moe" if i else "ffn"
                make_u(nm, c0, n, False, f"a{i}")
                scale_h(nm, c0, n)
                if i == 1:
                    act.wait_ge(s_gate, 1)
                    act.activation(GT[:, :, 1:2], GT[:, :, 0:1], ACT.Exp).then_inc(s_gexp, 1)
                    act.wait_ge(s_cbp, 1)
                    for b in range(4):
                        act.activation(CB[:, 2 * b:2 * b + 2, :].rearrange("p a t -> p (a t)"), PS[4 + b][:, :],
                                       ACT.Copy).then_inc(s_cb, 1)
                experts(nm, n)
                norm(f"b{i}", H, H, V_LN2 + 16 * i, c0, n)
            for i in range(DEPTH):
                nb = T2 if i == 0 else SEQ
                make_u(f"fa{i}", NMETA, T2, True, None)
                scale_h(f"fa{i}", NMETA, T2)
                experts(f"fa{i}", T2)
                norm(f"2a{i}", H, H, V_B + 48 * i, NMETA, T2)
                nm = "waqkv" if i else "naqkv"
                make_u(nm, NMETA, T2, True, None)
                scale_h(nm, NMETA, nb)
                p = ph[nm]
                if i == 0:
                    with act.Fori(0, p.n_iter) as it:
                        for s in range(4):
                            copy_step(p, it, s, [QKV[:, bass.ds(it * 8 + 2 * s + j, 1), :].rearrange("p a t -> p (a t)")
                                                 for j in range(2)], T2)
                    attention("na")
                else:
                    for s in range(6):
                        n = SEQ if s < 4 else T2
                        copy_step(p, 0, s, (QKV[:, 2 * s, 0:n], QKV[:, 2 * s + 1, 0:n]), n)
                    attention("wa")
                p = ph[f"wo{i}"]
                for s in range(4):
                    ahead(p, 0, s)
                norm(f"2n{i}", H, H, V_B + 48 * i + 16, NMETA, nb)
                make_u(f"fb{i}", NMETA, nb, True, None)
                scale_h(f"fb{i}", NMETA, nb)
                experts(f"fb{i}", nb)
                norm(f"2b{i}", H, H, V_B + 48 * i + 32, NMETA, nb)

        @block.vector
        def _(dve):
            own = Tally(s_dve)

            def link(ins):
                own.inc(ins)
                dve.wait_ge(s_dve, own.value)

            class looped:

                def __init__(self, i, n_iter, per):
                    self.i, self.n_iter, self.per = i, n_iter, per

                def __enter__(self):
                    self.n0 = own.n
                    own.off = 0 if isinstance(self.i, int) else self.i * self.per

                def __exit__(self, *a):
                    assert own.n - self.n0 == self.per, (own.n - self.n0, self.per)
                    own.off = 0
                    if not isinstance(self.i, int):
                        own.n = self.n0 + self.per * self.n_iter

            def low(p, i, s):
                g = p.step(i, s)
                dve.wait_ge(s_hi, g + 1)
                n = p.cols[s]
                dve.tensor_tensor(WL[s % 2][:, 0:n], RAW[:, s % RAW_SLOTS, 0:n], WH[s % 2][:, 0:n].bitcast(F32),
                                  ALU.subtract).then_inc(s_lo, 1)

            def ahead(p, i, s):
                if s + 1 < p.n:
                    low(p, i, s + 1)
                elif p.n_iter > 1 and not (isinstance(i, int) and i + 1 == p.n_iter):
                    low(p, i + 1, 0)
                else:
                    nxt = names.index(p.name) + 1
                    if nxt < len(names):
                        low(ph[names[nxt]], 0, 0)

            def norm(name, src, c0, n):
                b0, cs = LN_BASE[name], (KCV if name.startswith("cv") else KC)
                dve.wait_ge(s_mean, LN_IDX[name] + 1)
                for c in range(cs):
                    x = src[:, c, c0:c0 + n]
                    dve.tensor_tensor(x, x, PS[0][:, 0:n], ALU.subtract).then_inc(s_xc, 1)
                dve.wait_ge(s_std, LN_IDX[name] + 1)
                dve.wait_ge(s_sq, b0 + cs)
                link(dve.reciprocal(RSTD[:, 0:n], STD[:, 0:n]))
                for c in range(cs):
                    x = src[:, c, c0:c0 + n]
                    dve.tensor_tensor(x, x, RSTD[:, 0:n], ALU.mult).then_inc(s_nrm, 1)

            def make_u(name, c0, n, ln, layer=None, idx=None):
                ub = KC * U_IDX[name]
                if layer is None:
                    for c in range(KC):
                        dve.wait_ge(s_uh, ub + c + 1)
                        dve.tensor_tensor(UL[:, c, c0:c0 + n], H[:, c, c0:c0 + n], UH[:, c, c0:c0 + n].bitcast(F32),
                                          ALU.subtract).then_inc(s_ul, 1)
                    return

                def modulate(c):
                    dve.wait_ge(s_ln, LN_BASE[ln] + min(c + 1, KC))
                    if c >= 4:
                        dve.wait_ge(s_ul, ub + c - 3)
                    for st, (t0, nt) in enumerate(STREAM):
                        if t0 < c0 + n:
                            last = dve.tensor_scalar(TMP[:, c % 4, t0 - c0:t0 - c0 + nt], H[:, c, t0:t0 + nt],
                                                     mod(layer, idx + 1, c, st), mod(layer, idx, c, st), ALU.mult, ALU.add)
                    last.then_inc(s_um, 1)

                modulate(0)
                modulate(1)
                for c in range(KC):
                    if c + 2 < KC:
                        modulate(c + 2)
                    dve.wait_ge(s_uh, ub + c + 1)
                    dve.tensor_tensor(UL[:, c, c0:c0 + n], TMP[:, c % 4, 0:n], UH[:, c, c0:c0 + n].bitcast(F32),
                                      ALU.subtract).then_inc(s_ul, 1)

            def experts(name, c0, n, gate=None):
                p = ph[name]
                moe = name == "moe"
                dve.wait_ge(s_hs, S_IDX[name] + 1)

                def body(i):
                    s = 0
                    for k in range(KH):
                        ahead(p, i, s)
                        dve.wait_ge(s_step, p.step(i, s) + 1)
                        dve.wait_ge(s_sil, SIL_BASE[name] + k + 1 + i * KH)
                        dve.tensor_tensor(HT[:, k % 2, 0:n], SIL[:, k % 2, 0:n], PS[4 * (s % 2) + 1][:, 0:n],
                                          ALU.mult).then_inc(s_evd, 1)
                        dve.wait_ge(s_hid, HID_BASE[name] + k + 1 + i * KH)
                        dve.wait_ge(s_evd, p.evacs("d", i, s + 1))
                        dve.tensor_tensor(HIDL[:, k, 0:n], HT[:, k % 2, 0:n], HIDH[:, k, 0:n].bitcast(F32),
                                          ALU.subtract).then_inc(s_hidl, 1)
                        s += 1
                        if p.kinds[s] == "a":
                            ahead(p, i, s)
                            s += 1
                    for m in range(KC):
                        ahead(p, i, s)
                        dve.wait_ge(s_step, p.step(i, s) + 1)
                        ps = PS[4 * (s % 2)]
                        if m == 0:
                            dve.wait_ge(s_evd, p.evacs("d", i, s))
                        if moe:
                            w = CB[:, bass.ds(i, 1), :].rearrange("p a t -> p (a t)")
                            link(dve.tensor_tensor(HT[:, m % 2, 0:n], ps[:, 0:n], w, ALU.mult))
                            x = H[:, m, c0:c0 + n]
                            dve.tensor_tensor(x, x, HT[:, m % 2, 0:n], ALU.add).then_inc(s_evd, 1)
                        elif gate is None:
                            x = H[:, m, c0:c0 + n]
                            dve.tensor_tensor(x, x, ps[:, 0:n], ALU.add).then_inc(s_evd, 1)
                        else:
                            gated(ps, m, n, gate)
                        s += 1

                if moe:
                    with dve.Fori(0, p.n_iter) as i, looped(i, p.n_iter, KC):
                        body(i)
                else:
                    iterate(dve, p, body)

            def gated(ps, m, n, gate):
                for st, (t0, nt) in enumerate(STREAM):
                    if t0 < NMETA + n:
                        x = H[:, m, t0:t0 + nt]
                        last = dve.scalar_tensor_tensor(x, ps[:, t0 - NMETA:t0 - NMETA + nt], mod(*gate, m, st), x,
                                                        ALU.mult, ALU.add)
                last.then_inc(s_evd, 1)

            def attention(name):
                a = atts[name]
                first = name[0] == "b"

                def biased(it, u):
                    half, qt, k0, nk, _ = unit_of(a, u)
                    q0, nq = a.qts[qt]
                    b = u % 2
                    g = a.unit0 + it * a.units + u
                    dve.wait_ge(s_sc, g + 1)
                    reach(dve, s_tp, two_ago(a, it, u))
                    ps = PS[b]
                    if first:
                        bt = B1[qt + 3 - len(a.qts)]
                        bias = bt[0:nq, bass.ds(2 * it + half, 1), 0:nk].rearrange("p a t -> p (a t)")
                        ins_ = dve.scalar_tensor_tensor(a.sbf[0:nq, b, 0:nk], ps[0:nq, 0:nk], SCALE, bias,
                                                        ALU.mult, ALU.add)
                    else:
                        nbias = SEQ if nk == T2 else 0
                        if nbias:
                            bias = NB[:, qt, half, :] if name == "na" else CST[:, C_WAM + SEQ * qt:C_WAM + SEQ * (qt + 1)]
                            dve.scalar_tensor_tensor(a.sbf[:, b, 0:SEQ], ps[:, 0:SEQ], SCALE, bias, ALU.mult, ALU.add)
                        ins_ = dve.tensor_scalar(a.sbf[:, b, nbias:nk], ps[:, nbias:nk], SCALE, None, ALU.mult)
                    link(ins_)
                    if a.sink:
                        link(dve.tensor_reduce(NMX[0:nq, b:b + 1], a.sbf[0:nq, b, 0:nk], AX_X, ALU.max, negate=True))
                        nsk = NSK1[:, a.layer, bass.ds(2 * it + half, 1)] if first else NSK2[:, bass.ds(2 * it + half, 1)]
                        dve.tensor_tensor(NM[0:nq, b:b + 1], NMX[0:nq, b:b + 1], nsk[0:nq, :], ALU.min).then_inc(s_sb, 1)
                    else:
                        dve.tensor_reduce(NM[0:nq, b:b + 1], a.sbf[0:nq, b, 0:nk], AX_X, ALU.max,
                                          negate=True).then_inc(s_sb, 1)

                def scaled(it, u):
                    half, qt, k0, nk, _ = unit_of(a, u)
                    nq = a.qts[qt][1]
                    b = u % 2
                    g = a.unit0 + it * a.units + u
                    dve.wait_ge(s_ex, g + 1)
                    if a.sink:
                        link(dve.tensor_tensor(DEN[0:nq, b:b + 1], DEN[0:nq, b:b + 1], ESK[0:nq, b:b + 1], ALU.add))
                    link(dve.reciprocal(RDEN[0:nq, b:b + 1], DEN[0:nq, b:b + 1]))
                    dve.wait_ge(s_pv, g + 1)
                    dve.tensor_scalar(a.os[0:nq, qt, HD * half:HD * half + HD], PS[4 + b][0:nq, 0:HD],
                                      RDEN[0:nq, b:b + 1], None, ALU.mult).then_inc(s_o, 1)

                per = a.units * (2 + 2 * a.sink)
                for grp in range(a.groups):
                    for loop in pairs_of_heads(dve, a):
                        with loop as i, looped(i, a.inner, per):
                            it = i + grp * a.inner
                            if name == "na":
                                dve.wait_ge(s_nb, it + 1)
                            biased(it, 0)
                            biased(it, 1)
                            reach(dve, s_ot, a.it0 + it)
                            for u in range(a.units):
                                if u + 2 < a.units:
                                    biased(it, u + 2)
                                scaled(it, u)
                            dve.wait_ge(s_ath, a.it0 + it + 1)
                            uu = slice(a.u0 + a.lo, a.u0 + a.hi)
                            dve.tensor_tensor(UL[:, bass.ds(it, 1), uu].rearrange("p a t -> p (a t)"),
                                              PS[6][:, a.lo:a.hi],
                                              UH[:, bass.ds(it, 1), uu].rearrange("p a t -> p (a t)").bitcast(F32),
                                              ALU.subtract).then_inc(s_atl, 1)

            def conv(layer, c0, n, lo, hi):
                for w in range(lo, hi):
                    for c in range(KCV):
                        x = HPAD[:, c, c0 + w:c0 + w + n]
                        y = CONV[:, c, c0:c0 + n]
                        tap = vec(V_DW + (layer * KCV + c) * TAPS + w)
                        if w == 0:
                            own.inc(dve.tensor_scalar(y, x, tap, vec(V_CB + 4 * layer + c), ALU.mult, ALU.add))
                        elif w < TAPS - 1:
                            dve.wait_ge(s_dve, own.value - KCV + 1)
                            own.inc(dve.scalar_tensor_tensor(y, x, tap, y, ALU.mult, ALU.add))
                        else:
                            dve.wait_ge(s_dve, own.value - KCV + 1 + c)
                            dve.scalar_tensor_tensor(y, x, tap, y, ALU.mult, ALU.add).then_inc(s_cv, 1)

            dve.wait_ge(s_silc, 2)
            dve.tensor_tensor(SCL[:, :, :], SCF[:, :, :], SCH[:, :, :].bitcast(F32), ALU.subtract).then_inc(s_silc, 1)
            dve.wait_ge(s_const, 16 * 10)
            own.inc(dve.tensor_scalar(NSK1[:, :, :], SK1[:, :, :], -1.0, None, ALU.mult))
            link(dve.tensor_scalar(NSK2[:, :], SK2[:, :], -1.0, None, ALU.mult))
            low(ph["win0"], 0, 0)
            norm("emb", H, 0, L1)
            for i in range(DEPTH):
                c0, n = (0, L1) if i == 0 else (NMETA, SEQ)
                make_u(f"win{i}", 0, L1, None)
                p = ph[f"win{i}"]
                for s in range(3):
                    ahead(p, 0, s)
                dve.wait_ge(s_ms, 4 + i)
                for s in range(3, 7):
                    ahead(p, 0, s)
                    dve.wait_ge(s_step, p.step(0, s) + 1)
                    dve.wait_ge(s_sil, SIL_BASE[f"win{i}"] + s - 2)
                    dve.tensor_tensor(HPAD[:, s - 3, TAPS - 1:TAPS - 1 + L1], PS[4 * (s % 2)][:, 0:L1],
                                      TMP[:, s % 2, 0:L1], ALU.mult).then_inc(s_evd, 1)
                dve.wait_ge(s_evd, p.evacs("d", 0, 7))
                for s in range(7, 15):
                    ahead(p, 0, s)
                    conv(i, c0, n, 4 * (s - 7), min(4 * (s - 6), TAPS))
                dve.wait_ge(s_b1, 16 * 5 * (i + 1))
                attention(f"b{i}")
                norm(f"cv{i}", CONV, c0, n)
                for c in range(KCV):
                    dve.wait_ge(s_mixh, (KCV + KC) * i + c + 1)
                    dve.tensor_tensor(UL[:, 4 + c, c0:c0 + n], CONV[:, c, c0:c0 + n],
                                      UH[:, 4 + c, c0:c0 + n].bitcast(F32), ALU.subtract).then_inc(s_mixl, 1)
                p = ph[f"proj{i}"]
                for s in range(4):
                    ahead(p, 0, s)
                    dve.wait_ge(s_step, p.step(0, s) + 1)
                    for m in range(2):
                        c = 2 * s + m
                        ps = [PS[4 * (s % 2) + 2 * m + b][:, 0:n] for b in range(2)]
                        dve.tensor_tensor(TMP[:, 0, 0:n], ps[0], SG[:, c, c0:c0 + n], ALU.mult)
                        second = dve.tensor_tensor(TMP[:, 1, 0:n], ps[1], SG[:, KC + c, c0:c0 + n], ALU.mult)
                        if m:
                            second.then_inc(s_evd, 1)
                            dve.wait_ge(s_evd, p.evacs("d", 0, s + 1))
                        else:
                            link(second)
                        dve.tensor_tensor(TMP[:, 2 + m, 0:n], TMP[:, 0, 0:n], TMP[:, 1, 0:n], ALU.add).then_inc(s_mix, 1)
                        dve.wait_ge(s_mixh, (KCV + KC) * i + KCV + c + 1)
                        dve.tensor_tensor(MIXL[:, c, c0:c0 + n], TMP[:, 2 + m, 0:n],
                                          MIXH[:, c, c0:c0 + n].bitcast(F32), ALU.subtract).then_inc(s_mixl, 1)
                p = ph[f"wout{i}"]
                for s in range(4):
                    ahead(p, 0, s)
                    dve.wait_ge(s_step, p.step(0, s) + 1)
                    for j in range(2):
                        x = H[:, 2 * s + j, c0:c0 + n]
                        last = dve.scalar_tensor_tensor(x, x, ALPHA, PS[4 * (s % 2) + j][:, 0:n], ALU.mult, ALU.add)
                    last.then_inc(s_evd, 1)
                norm(f"a{i}", H, c0, n)
                nm = "moe" if i else "ffn"
                make_u(nm, c0, n, None)
                if i == 1:
                    dve.wait_ge(s_rt, 1)
                    link(dve.tensor_copy(LG[:, :, :].rearrange("p a e -> p (a e)"), PS[2][:, 0:16]))
                    for t in range(2):
                        link(dve.max(MX8[:, t, :], LG[:, t, :]))
                        link(dve.max_index(IX8[:, t, :], MX8[:, t, :], LG[:, t, :]))
                    link(dve.tensor_copy(IXF[:, :, :], IX8[:, :, :]))
                    dve.tensor_tensor(GT[:, :, 0:1], MX8[:, :, 1:2], MX8[:, :, 0:1], ALU.subtract).then_inc(s_gate, 1)
                    dve.wait_ge(s_gexp, 1)
                    link(dve.tensor_scalar(GT[:, :, 2:3], GT[:, :, 1:2], 1.0, None, ALU.add))
                    link(dve.reciprocal(GT[:, :, 2:3], GT[:, :, 2:3]))
                    link(dve.tensor_tensor(GT[:, :, 3:4], GT[:, :, 1:2], GT[:, :, 2:3], ALU.mult))
                    for t in range(2):
                        for r, oh in enumerate((OH1, OH2)):
                            link(dve.tensor_scalar(oh[:, t, :], CST[:, C_IOTA:C_IOTA + 8], IXF[:, t, r:r + 1],
                                                   GT[:, t, 2 + r:3 + r], ALU.is_equal, ALU.mult))
                    link(dve.tensor_tensor(OH1[:, :, :], OH1[:, :, :], OH2[:, :, :], ALU.add))
                    for t in range(2):
                        last = dve.tensor_copy(CBB[:, t, :, :], OH1[:, t, :].rearrange("p (e a) -> p e a", a=1)
                                               .to_broadcast([P, N_EXP, P]))
                    last.then_inc(s_gate, 1)
                    dve.wait_ge(s_cb, 4)
                experts(nm, c0, n)
                dve.wait_ge(s_evd, ph[nm].evacs("d", ph[nm].n_iter, 0))
                norm(f"b{i}", H, c0, n)
            dve.wait_ge(s_eva, ph["moe"].evacs("a", N_EXP, 0))
            for st in range(2):
                own.inc(dve.tensor_tensor(MOD[:, :, :, st], MOD[:, :, :, st],
                                          vec(V_BM, 144).rearrange("p (t a) -> p t a", a=2), ALU.add))
            dve.wait_ge(s_dve, own.value)
            for l in range(2):
                for idx in (1, 4, 7, 2, 8):
                    m = MOD[:, l * 36 + idx * 4:l * 36 + idx * 4 + 4, :, :].rearrange("p a b c -> p (a b c)")
                    own.inc(dve.tensor_scalar(m, m, *((1.0, None, ALU.add) if idx in (1, 4, 7) else (0.5, None, ALU.mult))))
            dve.wait_ge(s_dve, own.value)
            for i in range(DEPTH):
                nb = T2 if i == 0 else SEQ
                make_u(f"fa{i}", NMETA, T2, "b1" if i == 0 else "2b0", i, 0)
                experts(f"fa{i}", NMETA, T2, (i, 2))
                dve.wait_ge(s_evd, ph[f"fa{i}"].evacs("d", 2, 0))
                norm(f"2a{i}", H, NMETA, T2)
                nm = "waqkv" if i else "naqkv"
                make_u(nm, NMETA, T2, f"2a{i}", i, 3)
                p = ph[nm]
                if i == 0:
                    with dve.Fori(0, p.n_iter) as it:
                        for s in range(4):
                            ahead(p, it, s)
                    attention("na")
                else:
                    for s in range(6):
                        ahead(p, 0, s)
                    dve.wait_ge(s_eva, p.evacs("a", 0, 6))
                    for c in range(10):
                        dve.wait_ge(s_rsw, c + 1)
                        x = QKV[:, c, 0:SEQ]
                        own.inc(dve.tensor_tensor(TMP[:, c % 2, 0:SEQ], PS[c % 2][:, 0:SEQ], CST[:, C_SIN:C_SIN + SEQ], ALU.mult))
                        link(dve.tensor_tensor(x, x, CST[:, C_COS:C_COS + SEQ], ALU.mult))
                        dve.tensor_tensor(x, x, TMP[:, c % 2, 0:SEQ], ALU.add).then_inc(s_rope, 1)
                    attention("wa")
                p = ph[f"wo{i}"]
                dve.wait_ge(s_hs, S_IDX[nm] + 1)
                for s in range(4):
                    ahead(p, 0, s)
                    dve.wait_ge(s_step, p.step(0, s) + 1)
                    for j in range(2):
                        m = 2 * s + j
                        for st, (t0, nt) in enumerate(STREAM):
                            if t0 < NMETA + nb:
                                x = H[:, m, t0:t0 + nt]
                                last = dve.scalar_tensor_tensor(x, PS[4 * (s % 2) + j][:, t0 - NMETA:t0 - NMETA + nt],
                                                                mod(i, 5, m, st), x, ALU.mult, ALU.add)
                    last.then_inc(s_evd, 1)
                norm(f"2n{i}", H, NMETA, nb)
                make_u(f"fb{i}", NMETA, nb, f"2n{i}", i, 6)
                experts(f"fb{i}", NMETA, nb, (i, 8))
                dve.wait_ge(s_evd, ph[f"fb{i}"].evacs("d", 2, 0))
                norm(f"2b{i}", H, NMETA, nb)


def _linear(w, order=None):
    if order is not None:
        w = w[:, order]
    k, m = w.shape
    return np.ascontiguousarray(w.reshape(k // P, P, m // 256, 256).transpose(2, 1, 0, 3).reshape(m // 256, P, -1))


def _gate_up(g, u):
    e = g.shape[0]
    both = np.stack([g, u], 2).reshape(e, KC, P, 2, KH, P)
    return both.transpose(0, 4, 2, 1, 3, 5).reshape(e, KH, P, W_STEP)


def _down(w):
    e = w.shape[0]
    return w.reshape(e, KH, P, KC, P).transpose(0, 3, 2, 1, 4).reshape(e, KC, P, D_EXP)


def _halves(w_in):
    return np.stack([w_in[:, :D_EXP], w_in[:, D_EXP:]])


def _features(v):
    v = np.asarray(v)
    return v.reshape(-1, P).T


def lay_out(x):
    x = {k: np.asarray(v) for k, v in x.items()}
    consts, onehot = shape_constants()
    heads = [h for c in range(4) for h in (c, 4 + c)]
    hcols = np.concatenate([np.arange(h * HD, (h + 1) * HD) for h in heads])
    order = [hcols, np.arange(512, 768)]
    for t in range(KCV):
        order += [768 + t * P + np.arange(P), 768 + CONVC + t * P + np.arange(P)]
    order = np.concatenate(order + [np.arange(768 + 2 * CONVC, 768 + 2 * CONVC + 2 * D)])
    wheads = [8 * p + 4 * half + i for p in range(2) for i in range(4) for half in range(2)]
    wcols = np.concatenate([np.arange(h * HD, (h + 1) * HD) for h in wheads])
    arrays = {
        "consts": consts, "onehot": onehot, "neg_row": np.full((1, 8), NEG, np.float32),
        "tokens": np.concatenate([x["meta_tokens"], x["x"][0]]).T.reshape(KC, P, L1).transpose(1, 0, 2),
        "ctx": x["ctx_2"][0].T.reshape(KC, P, CTX).transpose(1, 0, 2),
        "cond": np.stack([x["c_2"][0], x["c_ctx_2"]]).reshape(2, KC, P).transpose(2, 1, 0),
        "rel_bias": x["rel_bias"][:, heads],
        "sinks": x["sinks"][:, heads],
        "sinks_2": x["wa_sinks_2"][:, wheads],
        "router": x["router"][0].reshape(KC, P, N_EXP).transpose(1, 0, 2),
        "na_rpb": x["na_rpb_2"].reshape(1, -1),
        "w_in": np.stack([_linear(x["w_in"][i], order) for i in range(DEPTH)]),
        "w_proj": np.stack([np.concatenate([_linear(x["w_attn_proj"][i][hcols]), _linear(x["w_conv_proj"][i])], 2)
                            for i in range(DEPTH)]),
        "w_out": np.stack([_linear(x["w_out"][i]) for i in range(DEPTH)]),
        "w_mod": np.concatenate([_linear(x["w_mod_2"][i]) for i in range(DEPTH)]),
        "w_na": _linear(x["na_w_qkv_2"][0]),
        "w_wa": _linear(x["wa_w_qkv_2"][0], np.concatenate([wcols, np.arange(D, D + 512)])),
        "w_o": np.stack([_linear(x["na_w_o_2"][0]), _linear(x["wa_w_o_2"][0][wcols])]),
    }
    g, u, d = [_halves(x["ffn_w_gate"][0]), x["moe_w_gate"][0]], [_halves(x["ffn_w_up"][0]), x["moe_w_up"][0]], \
        [x["ffn_w_down"][0].reshape(2, D_EXP, D), x["moe_w_down"][0]]
    for i in range(DEPTH):
        for j in range(2):
            w = x["ffn_w_in_2"][i, j]
            g.append(_halves(w[:, :2 * D_EXP]))
            u.append(_halves(w[:, 2 * D_EXP:]))
            d.append(x["ffn_w_out_2"][i, j].reshape(2, D_EXP, D))
    arrays["w_gu"] = np.concatenate([_gate_up(a, b) for a, b in zip(g, u)])
    arrays["w_dn"] = np.concatenate([_down(a) for a in d])
    cols = [_features(x["emb_ln_g"]), _features(x["emb_ln_b"])]
    for gg, bb in (("ln1_g", "ln1_b"), ("ln2_g", "ln2_b")):
        for i in range(DEPTH):
            cols += [_features(x[gg][i]), _features(x[bb][i])]
    for i in range(DEPTH):
        for j in range(3):
            cols += [_features(x["ln_g_2"][i, j]), _features(x["ln_b_2"][i, j])]
    for i in range(DEPTH):
        cols += [_features(x["conv_ln_g"][i]), _features(x["conv_ln_b"][i])]
    cols += [_features(x["conv_b"])]
    for i in range(DEPTH):
        cols += [x["conv_dw"][i].T.reshape(KCV, P, TAPS).transpose(1, 0, 2).reshape(P, -1)]
    cols += [_features(x["b_mod_2"])]
    arrays["vectors"] = np.concatenate(cols, 1)
    return {k: np.ascontiguousarray(v) for k, v in arrays.items()}


def kernel(**inputs):
    import concourse.bacc as bacc
    from concourse.bass_utils import run_bass_kernel_spmd as run

    nc = bacc.Bacc("TRN2", target_bir_lowering=False, num_devices=1)
    arrays = lay_out(inputs)
    ins = {k: nc.dram_tensor(f"in_{k}", a.shape, F32, kind="ExternalInput").ap() for k, a in arrays.items()}
    out = nc.dram_tensor("out_h", (P, KC, SEQ), F32, kind="ExternalOutput").ap()
    build(nc, ins, out)
    r = run(nc, [{f"in_{k}": a for k, a in arrays.items()}], core_ids=[0])
    got = r.results[0]["out_h"]
    return got.transpose(2, 1, 0).reshape(1, SEQ, D)
```

```python
import math
from contextlib import ExitStack, nullcontext

import numpy as np

import concourse.bass as bass
import concourse.mybir as mybir

F32 = mybir.dt.float32
F32R = mybir.dt.float32r
U32 = mybir.dt.uint32
ACT = mybir.ActivationFunctionType
ALU = mybir.AluOpType
AX_X = mybir.AxisListType.X

P = 128
D = 1024
KC = D // P
NMETA, SEQ, CTX = 16, 256, 256
L1 = NMETA + SEQ
T2 = SEQ + CTX
TALL = L1 + CTX
DEPTH = 2
ALPHA = float((2 * DEPTH) ** 0.25)
EPS = 1e-5
HD = 64
SCALE = HD ** -0.5
D_EXP = 1408
KH = D_EXP // P
DOWN_CUT = 6
N_EXP = 8
CONVC = 512
KCV = CONVC // P
TAPS = 31
NBUCK = 32
NEG = -1e30
RAW_SLOTS = 4
PIECES = 2
PIECE_SLOTS = 4
PIECE_W = 1024
AHEAD = 2
BANK_SETS = 4
W_STEP = 2048
MOD_STEPS = 2 * 9 * D // 256
MOD_PER_EXPERT = MOD_STEPS // N_EXP
BW = 400
RPB_R, RPB_C = 15, 31
RPB_LEN = 16 * RPB_R * RPB_C

C_ID, C_PERM, C_COS, C_SIN = 0, 128, 256, 512
C_NAM, C_WAM, C_IOTA, C_END = 768, 832, 1344, 1352

V_EMB = 0
V_LN1 = 16
V_LN2 = V_LN1 + 32
V_B = V_LN2 + 32
V_CLN = V_B + 96
V_CB = V_CLN + 16
V_DW = V_CB + 8
V_BM = V_DW + 2 * KCV * TAPS
V_END = V_BM + 144


def shape_constants():
    c = np.zeros((P, C_END), np.float32)
    c[:, C_ID:C_ID + P] = np.eye(P)
    inv = (10000.0 ** (-np.arange(16, dtype=np.float32) / 16)).astype(np.float32)
    t = np.arange(SEQ)
    for p in range(P):
        d = p % HD
        second = d % 32 >= 16
        partner = p - 16 if second else p + 16
        c[partner, C_PERM + p] = 1.0
        pos = (t // 64 if d < 32 else t % 64).astype(np.float32)
        ang = pos * inv[d % 16]
        c[p, C_COS:C_COS + SEQ] = np.cos(ang)
        c[p, C_SIN:C_SIN + SEQ] = np.sin(ang) * (1.0 if second else -1.0)
    qc, kc = np.arange(64)[:, None], np.arange(64)[None, :]
    start = np.clip(qc - 8, 0, 48)
    seen = (kc >= start) & (kc < start + 16)
    c[:, C_NAM:C_NAM + 64] = np.tile(np.where(seen, 0.0, NEG), (2, 1))
    for b in range(2):
        q = b * P + np.arange(P)[:, None]
        far = np.abs(q - np.arange(SEQ)[None, :]) > 128
        c[:, C_WAM + b * SEQ:C_WAM + (b + 1) * SEQ] = np.where(far, NEG, 0.0)
    c[:, C_IOTA:C_IOTA + 8] = np.arange(8)
    oh = np.zeros((NBUCK + 1, 2, BW), np.float32)
    dist = L1 - np.arange(BW)
    n = np.maximum(dist, 0)
    nf = np.maximum(n, 1).astype(np.float32)
    large = 16 + (np.log(nf / np.float32(16)) / np.float32(math.log(8)) * 16).astype(np.int32)
    bucket = np.where(n < 16, n, np.minimum(large, 31))
    for v in range(2):
        oh[bucket, v, np.arange(BW)] = 1.0
        masked = (dist < 0) | ((dist >= 128) if v else False)
        oh[NBUCK, v] = np.where(masked, 1.0, 0.0)
    return c, oh.reshape(NBUCK + 1, 2 * BW)


class Phase:

    def __init__(self, name, prev, n_iter, kinds, cols, last):
        self.name, self.n_iter, self.kinds, self.cols, self.n, self.last = name, n_iter, kinds, cols, len(kinds), last
        self.pieces = PIECES * self.n
        self.prev = prev
        self.a0 = self.d0 = self.p0 = 0
        self.raw0 = [0] * RAW_SLOTS
        self.next = None
        if prev is not None:
            prev.next = self
            self.a0 = prev.evacs("a", prev.n_iter, 0)
            self.d0 = prev.evacs("d", prev.n_iter, 0)
            self.p0 = prev.p0 + prev.pieces * prev.n_iter
            self.raw0 = [prev.raw0[r] + prev.n_iter * len(range(r, prev.n, RAW_SLOTS)) for r in range(RAW_SLOTS)]

    def piece(self, i, s, h):
        return self.p0 + PIECES * s + h + i * self.pieces

    def piece_slot(self, s, h):
        return (PIECES * s + h) % PIECE_SLOTS

    def evacs(self, kind, i, s):
        if kind == "d":
            return self.d0 + self.kinds[:s].count("d") + i * self.kinds.count("d")
        return self.a0 + s - self.kinds[:s].count("d") + i * (self.n - self.kinds.count("d"))

    def loads(self, i, s):
        r = s % RAW_SLOTS
        per = len(range(r, self.n, RAW_SLOTS))
        return self.raw0[r] + s // RAW_SLOTS + 1 + i * per

    def behind(self, r):
        phases = [p for p in (self if self.n_iter > 1 else None, self.prev) if p is not None]
        return min(p.n - 1 - max(x for x in range(p.n) if x % RAW_SLOTS == r) for p in phases)

    def step_ahead(self, i, s):
        if s + AHEAD < self.n:
            return self, i, s + AHEAD
        if self.n_iter > 1 and not (isinstance(i, int) and i + 1 == self.n_iter):
            return self, i + 1, s + AHEAD - self.n
        return self.next and (self.next, 0, s + AHEAD - self.n)

    def raw_user(self, i, s):
        if s >= RAW_SLOTS:
            return self.piece(i, s - RAW_SLOTS, PIECES - 1) + 1
        return self.piece(i, 0, 0) - PIECES * self.behind(s % RAW_SLOTS)

    def piece_user(self, i, s, h):
        q = PIECES * s + h
        if q >= PIECE_SLOTS:
            return self.piece(i, s, h) - PIECE_SLOTS + 1
        before = self.prev if isinstance(i, int) and i == 0 else self
        follow = before.pieces - 1 - max(x for x in range(before.pieces) if x % PIECE_SLOTS == q)
        return self.piece(i, 0, 0) - follow

    def bank_user(self, i, s):
        if s >= BANK_SETS:
            kind = self.kinds[s - BANK_SETS]
            return kind, self.evacs(kind, i, s - BANK_SETS + 1)
        kind = self.kinds[-1]
        after = self.n - 1 - max(x for x in range(self.n) if x % BANK_SETS == s)
        assert set(self.kinds[self.n - BANK_SETS:]) == {kind}
        return kind, self.evacs(kind, i, 0) - after


def plan():
    ph = {}
    prev = None
    full, down = [W_STEP] * KH, [D_EXP] * KC

    def add(name, n_iter, kinds, cols=None):
        nonlocal prev
        prev = ph[name] = Phase(name, prev, n_iter, kinds, cols or [W_STEP] * len(kinds), name == "fb1")

    moe_kinds, moe_cols = "", []
    for k in range(KH):
        moe_kinds += "d" + ("a" if k < MOD_PER_EXPERT else "")
        moe_cols += [W_STEP] * (2 if k < MOD_PER_EXPERT else 1)
    for i in range(2):
        add(f"win{i}", 1, "aaa" + "dddd" + "a" * 8)
        add(f"proj{i}", 1, "dddd")
        add(f"wout{i}", 1, "dddd")
        if i == 0:
            add("ffn", 2, "d" * 19, full + down)
        else:
            add("moe", N_EXP, moe_kinds + "d" * 8, moe_cols + down)
    for i in range(2):
        add(f"fa{i}", 2, "d" * 19, full + down)
        if i == 0:
            add("naqkv", 3, "aaaa")
        else:
            add("waqkv", 1, "aaaaaa")
        add(f"wo{i}", 1, "dddd")
        add(f"fb{i}", 2, "d" * 19, full + down)
    return ph


class Tally:

    def __init__(self, sem):
        self.sem, self.n, self.off = sem, 0, 0

    def inc(self, ins, by=1):
        self.n += by
        ins.then_inc(self.sem, by)
        return ins

    @property
    def value(self):
        return self.n + self.off


def build(nc, ins, out, upto=99):
    ph = plan()
    ctx = ExitStack()
    with ctx:
        def sb(name, shape, dt=F32, where=None):
            return (where or ctx).enter_context(nc.sbuf_tensor(name, shape, dt))

        def sem(name):
            return ctx.enter_context(nc.semaphore(name))

        RAW = sb("RAW", [P, RAW_SLOTS, W_STEP])
        WH = [sb(f"WH{h}", [P, PIECE_W], F32R) for h in range(PIECE_SLOTS)]
        WL = [sb(f"WL{h}", [P, PIECE_W], F32R) for h in range(PIECE_SLOTS)]
        H = sb("H", [P, KC, TALL])
        UH = sb("UH", [P, KC, TALL], F32R)
        UL = sb("UL", [P, KC, TALL], F32R)
        TMP = sb("TMP", [P, 4, T2])
        MLD = TMP[0:MOD_STEPS, 0:2, :].rearrange("p a (b n) -> p (a b) n", b=2)
        STD = sb("STD", [P, T2])
        RSTD = sb("RSTD", [P, T2])
        CST = sb("CST", [P, C_END])
        VEC = sb("VEC", [P, V_END])
        MOD = sb("MOD", [P, 2, MOD_STEPS, 2])
        RT = sb("RT", [P, KC, N_EXP])
        CC = sb("CC", [P, KC, 2])
        SCF = sb("SCF", [P, KC, 2])
        ONES = sb("ONES", [P, P])
        ONESC = sb("ONESC", [P, P])
        EPST = sb("EPST", [P, 1])
        SK1 = sb("SK1", [P, 2, 8])
        SK2 = sb("SK2", [P, 16])
        NSK1 = sb("NSK1", [P, 2, 8])
        NSK2 = sb("NSK2", [P, 16])
        NM = sb("NM", [P, 2])
        NMX = sb("NMX", [P, 2])
        DEN = sb("DEN", [P, 2])
        ESK = sb("ESK", [P, 2])
        RDEN = sb("RDEN", [P, 2])
        LG = sb("LG", [P, 2, 8])
        MX8 = sb("MX8", [P, 2, 8])
        IX8 = sb("IX8", [P, 2, 8], U32)
        IXF = sb("IXF", [P, 2, 8])
        OH1 = sb("OH1", [P, 2, 8])
        OH2 = sb("OH2", [P, 2, 8])
        GT = sb("GT", [P, 2, 4])
        with ExitStack() as region:
            HIDH = sb("HIDH", [P, KH, T2], F32R, region)
            HIDL = sb("HIDL", [P, KH, T2], F32R, region)
            SILHT = sb("SILHT", [P, 4, T2], where=region)
            CB = sb("CB", [P, N_EXP, SEQ], where=region)
            SC4 = sb("SC4", [P, KC, 32, 4], F32R, region)
            MROW = sb("MROW", [4, 2, 256], where=region)
        SIL, HT = SILHT[:, 0:2, :], SILHT[:, 2:4, :]
        CBB = SILHT[:, :, :].rearrange("p a b -> p (a b)").rearrange("p (t e c) -> p t e c", t=2, e=N_EXP)
        with ExitStack() as region:
            QKV = sb("QKV", [P, 24, T2], where=region)
            NB = sb("NB", [P, 2, 2, SEQ], where=region)
            QS2 = sb("QS2", [P, T2], where=region)
            KS2 = sb("KS2", [P, T2], where=region)
            VT2 = sb("VT2", [P, T2], where=region)
            VS2 = sb("VS2", [P, 4, P], where=region)
            SB2 = sb("SB2", [P, 2, T2], where=region)
            PT2 = sb("PT2", [P, 2, T2], where=region)
            OS2 = sb("OS2", [P, 4, P], where=region)
        with ExitStack() as region:
            SG = sb("SG", [P, 16, L1], where=region)
            HPAD = sb("HPAD", [P, KCV, TAPS - 1 + L1], where=region)
            CONV = sb("CONV", [P, KCV, L1], where=region)
            QS1 = sb("QS1", [P, L1], where=region)
            VS1 = sb("VS1", [P, 3, P], where=region)
            SB1 = sb("SB1", [P, 2, T2], where=region)
            PT1 = sb("PT1", [P, 2, T2], where=region)
            OS1 = sb("OS1", [P, 3, P], where=region)
            OHT = sb("OHT", [NBUCK + 1, 2 * BW], where=region)
            BROW = sb("BROW", [8, 2 * BW], where=region)
            RB = sb("RB", [NBUCK + 1, 8], where=region)
            with ExitStack() as sub:
                Q1 = sb("Q1", [P, 6, L1], where=sub)
                B1 = [sb(f"B1_{q}", [P, 8, n], where=sub) for q, n in enumerate((NMETA, NMETA + P, L1))]
            with ExitStack() as sub:
                MIXH = sb("MIXH", [P, KC, L1], F32R, sub)
                MIXL = sb("MIXL", [P, KC, L1], F32R, sub)
        PS = [ctx.enter_context(nc.psum_tensor(f"PS{b}", [P, 512], F32)) for b in range(8)]
        bias_rows = nc.dram_tensor("bias_rows", (8, 2, P, BW), F32, kind="Internal").ap()
        rpb_rows = nc.dram_tensor("rpb_rows", (64, RPB_LEN), F32, kind="Internal").ap()
        mod_rows = nc.dram_tensor("mod_rows", (4, MOD_STEPS, 256), F32, kind="Internal").ap()
        na_bias = nc.dram_tensor("na_bias", (8, 2, 64, 2, 2, SEQ), F32, kind="Internal").ap()

        IDENT = CST[:, C_ID:C_ID + P]

        s_const = sem("s_const")
        s_x = sem("s_x")
        s_raw = [sem(f"s_raw{r}") for r in range(RAW_SLOTS)]
        s_hi = sem("s_hi")
        s_lo = sem("s_lo")
        s_pc = sem("s_pc")
        s_mr = [sem(f"s_mr{b}") for b in range(2)]
        s_mrl = sem("s_mrl")
        s_mrt = sem("s_mrt")
        s_mrs = sem("s_mrs")
        s_eva = sem("s_eva")
        s_evd = sem("s_evd")
        s_ms = sem("s_ms")
        s_uh = sem("s_uh")
        s_ul = sem("s_ul")
        s_um = sem("s_um")
        s_hs = sem("s_hs")
        s_hid = sem("s_hid")
        s_hidl = sem("s_hidl")
        s_sil = sem("s_sil")
        s_mean = sem("s_mean")
        s_xc = sem("s_xc")
        s_sq = sem("s_sq")
        s_sqf = sem("s_sqf")
        s_std = sem("s_std")
        s_nrm = sem("s_nrm")
        s_ln = sem("s_ln")
        s_dve = sem("s_dve")
        s_sc = sem("s_sc")
        s_sb = sem("s_sb")
        s_ex = sem("s_ex")
        s_tp = sem("s_tp")
        s_pt = sem("s_pt")
        s_pv = sem("s_pv")
        s_o = sem("s_o")
        s_ot = sem("s_ot")
        s_ath = sem("s_ath")
        s_atl = sem("s_atl")
        s_stq = sem("s_stq")
        s_stk = sem("s_stk")
        s_vt = sem("s_vt")
        s_vs = sem("s_vs")
        s_nbd = sem("s_nbd")
        s_nb = sem("s_nb")
        s_rpb = sem("s_rpb")
        s_nas = sem("s_nas")
        s_brow = sem("s_brow")
        s_browd = sem("s_browd")
        s_b1 = sem("s_b1")
        s_cv = sem("s_cv")
        s_mix = sem("s_mix")
        s_mixh = sem("s_mixh")
        s_mixl = sem("s_mixl")
        s_rt = sem("s_rt")
        s_gate = sem("s_gate")
        s_gexp = sem("s_gexp")
        s_cbp = sem("s_cbp")
        s_cb = sem("s_cb")
        s_silc = sem("s_silc")
        s_mod = sem("s_mod")
        s_rsw = sem("s_rsw")
        s_rope = sem("s_rope")
        s_out = sem("s_out")

        block = ctx.enter_context(nc.Block())

        U_BEFORE = ["win0", "ffn", "win1", "moe", "fa0", "naqkv", "fb0", "fa1", "waqkv", "fb1"]
        U_IDX = {n: k for k, n in enumerate(U_BEFORE)}
        S_BEFORE = ["ffn", "moe", "fa0", "naqkv", "fb0", "fa1", "waqkv", "fb1"]
        S_IDX = {n: k for k, n in enumerate(S_BEFORE)}
        LNS = ["emb", "cv0", "a0", "b0", "cv1", "a1", "b1", "2a0", "2n0", "2b0", "2a1", "2n1", "2b1"]
        LN_IDX = {n: k for k, n in enumerate(LNS)}
        LN_BASE, base = {}, 0
        for n in LNS:
            LN_BASE[n] = base
            base += KCV if n.startswith("cv") else KC
        UM_IDX = {n: k for k, n in enumerate(["fa0", "naqkv", "fb0", "fa1", "waqkv", "fb1"])}
        SIL_BASE, base = {}, 0
        for n in ("win0", "ffn", "win1", "moe", "fa0", "fb0", "fa1", "fb1"):
            SIL_BASE[n] = base
            base += KCV if n.startswith("win") else KH * ph[n].n_iter
        HID_BASE, base = {}, 0
        for n in ("ffn", "moe", "fa0", "fb0", "fa1", "fb1"):
            HID_BASE[n] = base
            base += KH * ph[n].n_iter

        def iterate(eng, p, body):
            if p.last:
                for i in range(p.n_iter):
                    body(i)
            else:
                with eng.Fori(0, p.n_iter) as i:
                    body(i)

        def pairs_of_heads(eng, a):
            if a.name == "b0":
                return [nullcontext(i) for i in range(a.inner)]
            return [eng.Fori(0, a.inner)]

        class Att:
            pass

        atts = {}
        unit = kvn = its = 0
        for name, nq, groups, inner, kv_dyn in (
                ("b0", 3, 1, 4, False), ("b1", 2, 1, 4, False), ("na", 4, 1, 8, True), ("wa", 2, 2, 4, False)):
            a = atts[name] = Att()
            a.name, a.groups, a.inner, a.kv_dyn = name, groups, inner, kv_dyn
            a.units = 2 * nq
            a.unit0, a.it0, a.kv0 = unit, its, kvn
            unit += a.units * groups * inner
            its += groups * inner
            kvn += groups * (inner if kv_dyn else 1)
            if name[0] == "b":
                a.layer = int(name[1])
                a.qts = [(0, NMETA), (NMETA, P), (NMETA + P, P)][-nq:]
                a.keys = [(0, NMETA), (0, NMETA + P), (0, L1)][-nq:]
                a.vt = [(0, NMETA), (NMETA, P), (NMETA + P, P)]
                a.qs, a.vs, a.sbf, a.pt, a.os = QS1, VS1, SB1, PT1, OS1
                a.u0 = 0
            else:
                a.layer = 0 if name == "na" else 1
                a.qts = [(0, P), (P, P), (2 * P, P), (3 * P, P)][:nq]
                a.keys = [(0, T2), (0, T2), (SEQ, CTX), (SEQ, CTX)][:nq]
                a.vt = [(j * P, P) for j in range(4)]
                a.qs, a.vs, a.sbf, a.pt, a.os = QS2, VS2, SB2, PT2, OS2
                a.u0 = NMETA
            a.sink = name != "na"
            a.lo = a.qts[0][0]
            a.hi = a.qts[-1][0] + a.qts[-1][1]

        def bounds(p, s, h):
            if p.cols[s] == W_STEP:
                return h * PIECE_W, (h + 1) * PIECE_W
            return (0, DOWN_CUT * P) if h == 0 else (DOWN_CUT * P, D_EXP)

        def multiplied(eng, p, i, s):
            eng.wait_ge(s_pc, p.piece(i, s, PIECES - 1) + 1)

        def unit_of(a, u):
            half, qt = divmod(u, len(a.qts))
            k0, nk = a.keys[qt]
            tiles = [j for j, (c, n) in enumerate(a.vt) if c >= k0 and c + n <= k0 + nk]
            return half, qt, k0, nk, tiles

        def two_ago(a, it, u):
            return a.unit0 + it * a.units + max(u - 1, 0)

        def reach(eng, sm, value):
            if not (isinstance(value, int) and value <= 0):
                eng.wait_ge(sm, value)

        def vec(col, n=1):
            return VEC[:, col:col + n]

        def mod(layer, idx, c, s):
            t = layer * 72 + idx * KC + c
            return MOD[:, s, t // 2, t % 2:t % 2 + 1]

        STREAM = [(NMETA, SEQ), (L1, CTX)]

        @block.sync
        def _(sp):
            def load(p, i, s, src):
                if not (p.prev is None and s < RAW_SLOTS):
                    sp.wait_ge(s_lo, p.raw_user(i, s))
                sp.dma_start(RAW[:, s % RAW_SLOTS, 0:p.cols[s]], src).then_inc(s_raw[s % RAW_SLOTS], 16)

            def straight(name, w, k0=0):
                p = ph[name]
                for s in range(p.n):
                    load(p, 0, s, w[k0 + s])

            def experts(name, e0, with_mod=False):
                p = ph[name]

                def body(i):
                    s = 0
                    for k in range(KH):
                        load(p, i, s, ins["w_gu"][i + e0, k])
                        s += 1
                        if with_mod and k < MOD_PER_EXPERT:
                            load(p, i, s, ins["w_mod"][i * MOD_PER_EXPERT + k])
                            s += 1
                    for m in range(KC):
                        load(p, i, s, ins["w_dn"][i + e0, m])
                        s += 1

                iterate(sp, p, body)

            def bias_tiles(layer):
                if layer == 0:
                    sp.wait_ge(s_brow, 4)
                    for v in range(2):
                        row = BROW[:, v * BW:(v + 1) * BW].rearrange("h (a w) -> h a w", a=1)
                        sp.dma_start(bias_rows[:, v], row.to_broadcast([8, P, BW])).then_inc(s_browd, 16)
                    sp.wait_ge(s_browd, 32)
                else:
                    sp.wait_ge(s_pc, ph["win1"].p0)
                for q, (q0, nq) in enumerate(((0, NMETA), (NMETA, P), (NMETA + P, P))):
                    nk = q0 + nq
                    pieces = [(0, 0, NMETA)] + ([(1, NMETA, nk - NMETA)] if q else [])
                    for v, k0, n in pieces:
                        src = bass.AP(tensor=bias_rows.tensor, offset=v * P * BW + L1 - q0 + k0,
                                      ap=[[BW - 1, nq], [2 * P * BW, 8], [1, n]])
                        sp.dma_start(B1[q][0:nq, :, k0:k0 + n], src).then_inc(s_b1, 16)

            for i in range(DEPTH):
                if i == 0:
                    for s in range(3):
                        load(ph["win0"], 0, s, ins["w_in"][0, s])
                    bias_tiles(0)
                    for s in range(3, 15):
                        load(ph["win0"], 0, s, ins["w_in"][0, s])
                else:
                    straight(f"win{i}", ins["w_in"][i])
                    bias_tiles(1)
                straight(f"proj{i}", ins["w_proj"][i])
                straight(f"wout{i}", ins["w_out"][i])
                if i == 0:
                    experts("ffn", 0)
                else:
                    experts("moe", 2, True)
            for i in range(DEPTH):
                experts(f"fa{i}", 2 + N_EXP + 4 * i)
                if i == 0:
                    p = ph["naqkv"]
                    with sp.Fori(0, p.n_iter) as it:
                        for s in range(4):
                            load(p, it, s, ins["w_na"][it * 4 + s])
                else:
                    straight("waqkv", ins["w_wa"])
                straight(f"wo{i}", ins["w_o"][i])
                if i == 0:
                    a = atts["na"]
                    sp.wait_ge(s_nas, 16 * 64)
                    sp.wait_ge(s_pc, ph["naqkv"].p0)
                    with sp.Fori(0, a.inner) as it:
                        sp.wait_ge(s_sb, a.unit0 + it * a.units)
                        sp.dma_start(NB[:, :, :, :], na_bias[it].rearrange("r q a h k -> (r q) a h k"))\
                            .then_inc(s_nbd, 16)
                experts(f"fb{i}", 2 + N_EXP + 4 * i + 2)
            sp.wait_ge(s_ln, LN_BASE["2b1"] + KC)
            sp.dma_start(out, H[:, :, NMETA:L1]).then_inc(s_out, 16)
            sp.wait_ge(s_out, 16)

        @block.gpsimd
        def _(pool):
            pool.memset(ONES[:, :], 1.0 / D).then_inc(s_ms, 1)
            pool.memset(ONESC[:, :], 1.0 / CONVC).then_inc(s_ms, 1)
            pool.memset(EPST[:, :], EPS).then_inc(s_ms, 1)
            pool.dma_start(rpb_rows, ins["na_rpb"].to_broadcast([64, RPB_LEN])).then_inc(s_rpb, 16)
            pool.wait_ge(s_rpb, 16)
            for qr in range(4):
                for h in range(16):
                    src = bass.AP(tensor=rpb_rows.tensor,
                                  offset=h * RPB_R * RPB_C + (7 - qr) * RPB_C + 15,
                                  ap=[[RPB_LEN - 1, 64], [RPB_C, 4], [1, 64]])
                    dst = na_bias[h // 2, qr % 2, :, qr // 2, h % 2, :].rearrange("q (r k) -> q r k", r=4)
                    pool.dma_start(dst, src).then_inc(s_nas, 16)
            for i in range(DEPTH):
                if i == 1:
                    pool.wait_ge(s_pc, ph["win1"].p0)
                pool.memset(HPAD[:, :, 0:TAPS - 1], 0.0).then_inc(s_ms, 1)
                a = atts[f"b{i}"]
                pool.wait_ge(s_eva, ph[f"win{i}"].evacs("a", 0, 3))
                for loop in pairs_of_heads(pool, a):
                    with loop as it:
                        reach(pool, s_sc, a.unit0 + it * a.units)
                        pool.tensor_copy(QS1[:, :], Q1[:, bass.ds(it, 1), :].rearrange("p a t -> p (a t)"))\
                            .then_inc(s_stq, 1)
            a = atts["na"]
            pool.wait_ge(s_eva, ph["naqkv"].evacs("a", 3, 0))
            with pool.Fori(0, a.inner) as it:
                def chunk(first):
                    return QKV[:, bass.ds(first + it, 1), :].rearrange("p a t -> p (a t)")
                pool.wait_ge(s_sc, a.unit0 + it * a.units)
                pool.tensor_copy(QS2[:, :], chunk(0)).then_inc(s_stq, 1)
                pool.tensor_copy(KS2[:, :], chunk(8)).then_inc(s_stk, 1)
                pool.wait_ge(s_vt, a.kv0 + it)
                pool.tensor_copy(VT2[:, :], chunk(16)).then_inc(s_stk, 1)
                pool.wait_ge(s_nbd, it * 16 + 16)
                mask = CST[:, C_NAM:C_NAM + 64].rearrange("p (a k) -> p a k", a=1).to_broadcast([P, 16, 64])
                nbv = NB[:, :, :, :].rearrange("p a h (r k) -> p (a h r) k", r=4)
                pool.tensor_tensor(nbv, nbv, mask, ALU.add).then_inc(s_nb, 1)
            a = atts["wa"]
            pool.wait_ge(s_rope, 10)
            for grp in range(a.groups):
                with pool.Fori(0, a.inner) as it:
                    pool.wait_ge(s_sc, a.unit0 + (grp * a.inner + it) * a.units)
                    pool.tensor_copy(QS2[:, 0:SEQ], QKV[:, bass.ds(grp * a.inner + it, 1), 0:SEQ]
                                     .rearrange("p a t -> p (a t)")).then_inc(s_stq, 1)

        @block.tensor
        def _(pe):
            def piece_product(p, i, s, h, groups, arrives=None):
                pe.wait_ge(s_lo, p.piece(i, s, h) + 1)
                slot = p.piece_slot(s, h)
                order = [(g, x) for g in range(len(groups)) for x in range(len(groups[g][1]))]
                if arrives:
                    order.sort(key=lambda gx: gx[1])
                for g, x in order:
                    ps, terms, opens, closes = groups[g]
                    if arrives and g == 0:
                        pe.wait_ge(arrives[0], arrives[1][x])
                    col, mh, ml = terms[x]
                    wh, wl = WH[slot][:, col:col + P], WL[slot][:, col:col + P]
                    pe.matmul(ps, wh, mh, start=opens and x == 0, stop=False)
                    pe.matmul(ps, wh, ml, start=False, stop=False)
                    last = pe.matmul(ps, wl, mh, start=False, stop=closes and x == len(terms) - 1)
                last.then_inc(s_pc, 1)

            def begin(p, i, s):
                if s >= BANK_SETS or p.n_iter > 1:
                    kind, count = p.bank_user(i, s)
                    pe.wait_ge(s_evd if kind == "d" else s_eva, count)

            def all_evacuated(p):
                if p.a0:
                    pe.wait_ge(s_eva, p.a0)
                if p.d0:
                    pe.wait_ge(s_evd, p.d0)

            def pair_step(p, i, s, xh, xl, u=None):
                begin(p, i, s)
                for h in range(PIECES):
                    groups = []
                    for j in range(2):
                        ps = PS[2 * (s % BANK_SETS) + j][:, 0:xh(0).shape[1]]
                        groups.append((ps, [(x * 256 + j * P, xh(4 * h + x), xl(4 * h + x)) for x in range(4)],
                                       h == 0, h == 1))
                    piece_product(p, i, s, h, groups, None if u is None else (s_ul, [KC * u + 4 * h + x + 1 for x in range(4)]))

            def mod_step(p, i, s):
                begin(p, i, s)
                for h in range(PIECES):
                    pe.wait_ge(s_lo, p.piece(i, s, h) + 1)
                    slot = p.piece_slot(s, h)
                    for x in range(4):
                        for w in (WH, WL):
                            last = pe.matmul(PS[2 * (s % BANK_SETS)][:, 0:256], SC4[:, 4 * h + x, :, :].rearrange("p a b -> p (a b)"),
                                             w[slot][:, x * 256:(x + 1) * 256], start=(h == 0 and x == 0 and w is WH),
                                             stop=(h == 1 and x == 3 and w is WL))
                    last.then_inc(s_pc, 1)

            def chunks(t, c0, n):
                return lambda k: t[:, k, c0:c0 + n]

            def experts(name, c0, n):
                p = ph[name]
                all_evacuated(p)

                def body(i):
                    s = 0
                    for k in range(KH):
                        pair_step(p, i, s, chunks(UH, c0, n), chunks(UL, c0, n), U_IDX[name] if k == 0 else None)
                        s += 1
                        if p.kinds[s] == "a":
                            mod_step(p, i, s)
                            s += 1
                    for m in range(KC):
                        begin(p, i, s)
                        for h, ks in enumerate((range(DOWN_CUT), range(DOWN_CUT, KH))):
                            terms = [((k - ks[0]) * P, HIDH[:, k, 0:n], HIDL[:, k, 0:n]) for k in ks]
                            made = (s_hidl, [HID_BASE[name] + k + 1 + i * KH for k in ks]) if m == 0 else None
                            piece_product(p, i, s, h, [(PS[2 * (s % BANK_SETS)][:, 0:n], terms, h == 0, h == 1)], made)
                        s += 1

                iterate(pe, p, body)

            def straight(name, c0, n, u=True, ranges=None, xh=UH, xl=UL):
                p = ph[name]
                all_evacuated(p)
                for s in range(p.n):
                    cc, nn = ranges[s] if ranges else (c0, n)
                    pair_step(p, 0, s, chunks(xh, cc, nn), chunks(xl, cc, nn), U_IDX[name] if u and s == 0 else None)

            def norm(name, src, ones, c0, n, waits):
                b0, cs = LN_BASE[name], (KCV if name.startswith("cv") else KC)
                for sm, v in waits:
                    pe.wait_ge(sm, v)
                for c in range(cs):
                    last = pe.matmul(PS[0][:, 0:n], ones[:, :], src[:, c, c0:c0 + n], start=(c == 0), stop=(c == cs - 1))
                last.then_inc(s_mean, 1)
                for c in range(cs):
                    pe.wait_ge(s_sq, b0 + c + 1)
                    last = pe.matmul(PS[1][:, 0:n], ones[:, :], TMP[:, c % 4, 0:n], start=(c == 0), stop=(c == cs - 1))
                    last.then_inc(s_sqf, 1)

            def attention(name):
                a = atts[name]
                first = name[0] == "b"
                ksrc = Q1[:, 4, :] if first else KS2[:, :]
                def values(kv):
                    if a.kv_dyn:
                        pe.wait_ge(s_stk, 2 * (kv + 1))
                        pe.wait_ge(s_vs, a.kv0 + kv)
                    for j, (c, nt) in enumerate(a.vt):
                        last = pe.transpose(PS[7][0:nt, j * P:(j + 1) * P], a.vsrc[:, c:c + nt], IDENT)
                    last.then_inc(s_vt, 1)

                def scores(it, u):
                    half, qt, k0, nk, _ = unit_of(a, u)
                    q0, nq = a.qts[qt]
                    r = slice(HD * half, HD * half + HD)
                    reach(pe, s_sb, two_ago(a, it, u))
                    pe.matmul(PS[u % 2][0:nq, 0:nk], a.qs[r, q0:q0 + nq], ksrc_of(it)[r, k0:k0 + nk],
                              start=True, stop=True).then_inc(s_sc, 1)

                def ksrc_of(it):
                    return a.ksrc

                def turn(it, u):
                    half, qt, k0, nk, tiles = unit_of(a, u)
                    nq = a.qts[qt][1]
                    g = a.unit0 + it * a.units + u
                    pe.wait_ge(s_ex, g + 1)
                    reach(pe, s_pt, two_ago(a, it, u))
                    for x, j in enumerate(tiles):
                        c, nt = a.vt[j]
                        last = pe.transpose(PS[2 + u % 2][0:nt, x * P:x * P + nq],
                                            a.sbf[0:nq, u % 2, c - k0:c - k0 + nt], IDENT[0:nq, 0:nq])
                    last.then_inc(s_tp, 1)

                def times_values(it, u, kv):
                    half, qt, k0, nk, tiles = unit_of(a, u)
                    nq = a.qts[qt][1]
                    g = a.unit0 + it * a.units + u
                    if u == 0:
                        pe.wait_ge(s_vs, a.kv0 + kv + 1)
                    pe.wait_ge(s_pt, g + 1)
                    reach(pe, s_o, two_ago(a, it, u))
                    for x, j in enumerate(tiles):
                        nt = a.vt[j][1]
                        last = pe.matmul(PS[4 + u % 2][0:nq, 0:HD], a.pt[0:nt, u % 2, x * P:x * P + nq],
                                         a.vs[0:nt, j, HD * half:HD * half + HD],
                                         start=(x == 0), stop=(x == len(tiles) - 1))
                    last.then_inc(s_pv, 1)

                for grp in range(a.groups):
                    if first:
                        a.ksrc, a.vsrc = Q1[:, 4, :], Q1[:, 5, :]
                    elif a.kv_dyn:
                        a.ksrc, a.vsrc = KS2[:, :], VT2[:, :]
                    else:
                        a.ksrc, a.vsrc = QKV[:, 8 + grp, :], QKV[:, 10 + grp, :]
                    if not a.kv_dyn:
                        if grp:
                            pe.wait_ge(s_vs, a.kv0 + grp)
                        values(grp)
                    for loop in pairs_of_heads(pe, a):
                        with loop as i:
                            it = i + grp * a.inner
                            if a.kv_dyn:
                                values(it)
                            pe.wait_ge(s_stq, a.it0 + it + 1)
                            scores(it, 0)
                            scores(it, 1)
                            for u in range(a.units):
                                turn(it, u)
                                if u + 2 < a.units:
                                    scores(it, u + 2)
                                times_values(it, u, it if a.kv_dyn else grp)
                            pe.wait_ge(s_o, a.unit0 + it * a.units + a.units)
                            reach(pe, s_atl, a.it0 + it)
                            for q, (q0, nq) in enumerate(a.qts):
                                last = pe.transpose(PS[6][:, q0:q0 + nq], a.os[0:nq, q, :], IDENT[0:nq, 0:nq])
                            last.then_inc(s_ot, 1)

            pe.wait_ge(s_ms, 3)
            pe.wait_ge(s_const, 16 * 10)
            pe.matmul(PS[0][0:8, 0:BW], RB[:, :], OHT[:, 0:BW], start=True, stop=True).then_inc(s_brow, 1)
            pe.matmul(PS[1][0:8, 0:BW], RB[:, :], OHT[:, BW:2 * BW], start=True, stop=True).then_inc(s_brow, 1)
            pe.wait_ge(s_brow, 4)
            norm("emb", H, ONES, 0, L1, [(s_x, 32)])
            for i in range(DEPTH):
                c0, n = (0, L1) if i == 0 else (NMETA, SEQ)
                straight(f"win{i}", 0, L1)
                pe.wait_ge(s_eva, ph[f"win{i}"].evacs("a", 0, 15))
                attention(f"b{i}")
                norm(f"cv{i}", CONV, ONESC, c0, n, [(s_cv, KCV * (i + 1))])
                p = ph[f"proj{i}"]
                all_evacuated(p)
                pe.wait_ge(s_atl, atts[f"b{i}"].it0 + 4)
                pe.wait_ge(s_ul, KC * (U_IDX["win0" if i == 0 else "win1"] + 1))
                pe.wait_ge(s_mixl, (KCV + KC) * i + KCV)
                for s in range(p.n):
                    if s >= 2:
                        pe.wait_ge(s_evd, p.evacs("d", 0, s - 1))
                    for b in range(2):
                        groups = [(PS[4 * (s % 2) + 2 * m + b][:, 0:n],
                                   [(k * 256 + m * P, UH[:, 4 * b + k, c0:c0 + n], UL[:, 4 * b + k, c0:c0 + n])
                                    for k in range(KCV)], True, True) for m in range(2)]
                        piece_product(p, 0, s, b, groups)
                p = ph[f"wout{i}"]
                pe.wait_ge(s_mixl, (KCV + KC) * (i + 1))
                straight(f"wout{i}", c0, n, False, None, MIXH, MIXL)
                norm(f"a{i}", H, ONES, c0, n, [(s_evd, ph[f"wout{i}"].evacs("d", 0, 4))])
                if i == 1:
                    pe.wait_ge(s_ln, LN_BASE["a1"] + KC)
                    for t in range(2):
                        for k in range(KC):
                            last = pe.matmul(PS[2][:, 8 * t:8 * t + 8], H[:, k, NMETA + t * P:NMETA + (t + 1) * P],
                                             RT[:, k, :], start=(k == 0), stop=(k == KC - 1))
                    last.then_inc(s_rt, 1)
                    pe.wait_ge(s_gate, 2)
                    for t in range(2):
                        for e in range(N_EXP):
                            last = pe.matmul(PS[4 + e // 2][:, (e % 2) * SEQ + t * P:(e % 2) * SEQ + (t + 1) * P],
                                             CBB[:, t, e, :], IDENT, start=True, stop=True)
                    last.then_inc(s_cbp, 1)
                    pe.wait_ge(s_cb, 4)
                    pe.wait_ge(s_silc, 3)
                experts("moe" if i else "ffn", c0, n)
                nm = "moe" if i else "ffn"
                if i == 1:
                    pe.wait_ge(s_mrl, 16)
                    pe.wait_ge(s_evd, ph["fa0"].d0)
                    for j in range(2):
                        for r in range(4):
                            last = pe.transpose(PS[3 + j][:, r * MOD_STEPS:(r + 1) * MOD_STEPS],
                                                MLD[:, r, j * P:(j + 1) * P], IDENT[0:MOD_STEPS, 0:MOD_STEPS])
                    last.then_inc(s_mrt, 1)
                norm(f"b{i}", H, ONES, c0, n, [(s_evd, ph[nm].evacs("d", ph[nm].n_iter, 0))])
            for i in range(DEPTH):
                nb = T2 if i == 0 else SEQ
                experts(f"fa{i}", NMETA, T2)
                norm(f"2a{i}", H, ONES, NMETA, T2, [(s_evd, ph[f"fa{i}"].evacs("d", 2, 0))])
                if i == 0:
                    p = ph["naqkv"]
                    all_evacuated(p)
                    with pe.Fori(0, p.n_iter) as it:
                        for s in range(4):
                            pair_step(p, it, s, chunks(UH, NMETA, T2), chunks(UL, NMETA, T2), U_IDX["naqkv"] if s == 0 else None)
                    pe.wait_ge(s_eva, p.evacs("a", 3, 0))
                    attention("na")
                else:
                    p = ph["waqkv"]
                    straight("waqkv", 0, 0, True, [(NMETA, SEQ)] * 4 + [(NMETA, T2)] * 2)
                    pe.wait_ge(s_eva, p.evacs("a", 0, 6))
                    for c in range(10):
                        if c >= 2:
                            pe.wait_ge(s_rope, c - 1)
                        pe.matmul(PS[c % 2][:, 0:SEQ], CST[:, C_PERM:C_PERM + P], QKV[:, c, 0:SEQ],
                                  start=True, stop=True).then_inc(s_rsw, 1)
                    pe.wait_ge(s_rope, 10)
                    attention("wa")
                pe.wait_ge(s_atl, atts["na" if i == 0 else "wa"].it0 + 8)
                straight(f"wo{i}", NMETA, nb, False)
                norm(f"2n{i}", H, ONES, NMETA, nb, [(s_evd, ph[f"wo{i}"].evacs("d", 0, 4))])
                experts(f"fb{i}", NMETA, nb)
                norm(f"2b{i}", H, ONES, NMETA, nb, [(s_evd, ph[f"fb{i}"].evacs("d", 2, 0))])

        @block.scalar
        def _(act):
            for dst, src in ((CST[:, :], ins["consts"]), (VEC[:, :], ins["vectors"]), (OHT[:, :], ins["onehot"]),
                             (RB[0:NBUCK, :], ins["rel_bias"]), (RB[NBUCK:NBUCK + 1, :], ins["neg_row"]),
                             (RT[:, :, :], ins["router"]), (CC[:, :, :], ins["cond"])):
                act.dma_start(dst, src).then_inc(s_const, 16)
            for l in range(2):
                act.dma_start(SK1[:, l, :], ins["sinks"][l:l + 1, :].to_broadcast([P, 8])).then_inc(s_const, 16)
            act.dma_start(SK2[:, :], ins["sinks_2"].to_broadcast([P, 16])).then_inc(s_const, 16)
            act.dma_start(H[:, :, 0:L1], ins["tokens"]).then_inc(s_x, 16)
            act.dma_start(H[:, :, L1:TALL], ins["ctx"]).then_inc(s_x, 16)

            def high(p, i, s, h):
                if h == 0:
                    act.wait_ge(s_raw[s % RAW_SLOTS], p.loads(i, s) * 16)
                lo, hi = bounds(p, s, h)
                slot = p.piece_slot(s, h)
                if not (p.prev is None and s < 2):
                    act.wait_ge(s_pc, p.piece_user(i, s, h))
                act.activation(WH[slot][:, 0:hi - lo], RAW[:, s % RAW_SLOTS, lo:hi], ACT.Copy).then_inc(s_hi, 1)

            def ahead(p, i, s, pieces=range(PIECES)):
                later = p.step_ahead(i, s)
                for h in pieces if later else ():
                    high(*later, h)

            def norm(name, src, dst, gcol, c0, n, func=ACT.Identity):
                b0, cs = LN_BASE[name], (KCV if name.startswith("cv") else KC)
                for c in range(cs):
                    act.wait_ge(s_xc, b0 + c + 1)
                    if b0 + c >= 4:
                        act.wait_ge(s_sqf, b0 + c - 3)
                    act.activation(TMP[:, c % 4, 0:n], src[:, c, c0:c0 + n], ACT.Square).then_inc(s_sq, 1)
                act.wait_ge(s_sqf, b0 + cs)
                act.activation(STD[:, 0:n], PS[1][:, 0:n], ACT.Sqrt, bias=EPST[:, 0:1]).then_inc(s_std, 1)
                for c in range(cs):
                    act.wait_ge(s_nrm, b0 + c + 1)
                    act.activation(dst[:, c, c0:c0 + n], src[:, c, c0:c0 + n], func,
                                   bias=vec(gcol + cs + c), scale=vec(gcol + c)).then_inc(s_ln, 1)

            def make_u(name, c0, n, modulated, ln):
                b = KC * U_IDX[name]
                for c in range(KC):
                    if modulated:
                        act.wait_ge(s_um, UM_IDX[name] * KC + c + 1)
                        act.activation(UH[:, c, c0:c0 + n], TMP[:, c % 4, 0:n], ACT.Copy).then_inc(s_uh, 1)
                    else:
                        if c == 0:
                            act.wait_ge(s_ln, LN_BASE[ln] + KC)
                        act.activation(UH[:, c, c0:c0 + n], H[:, c, c0:c0 + n], ACT.Copy).then_inc(s_uh, 1)

            def scale_h(name, c0, n):
                act.wait_ge(s_ul, KC * (U_IDX[name] + 1))
                if name == "moe":
                    act.wait_ge(s_rt, 1)
                act.mul(H[:, :, c0:c0 + n], H[:, :, c0:c0 + n], ALPHA).then_inc(s_hs, 1)

            def experts(name, n):
                p = ph[name]

                def body(i):
                    s = 0
                    for k in range(KH):
                        ahead(p, i, s, (0,))
                        multiplied(act, p, i, s)
                        if k >= 2:
                            act.wait_ge(s_hidl, HID_BASE[name] + k - 1 + i * KH)
                        act.activation(SIL[:, k % 2, 0:n], PS[2 * (s % BANK_SETS)][:, 0:n], ACT.Silu).then_inc(s_sil, 1)
                        if k < KH - 1:
                            ahead(p, i, s, (1,))
                        act.wait_ge(s_evd, p.evacs("d", i, s + 1))
                        act.activation(HIDH[:, k, 0:n], HT[:, k % 2, 0:n], ACT.Copy).then_inc(s_hid, 1)
                        if k == KH - 1:
                            ahead(p, i, s, (1,))
                        s += 1
                        if p.kinds[s] == "a":
                            ahead(p, i, s, (0,))
                            multiplied(act, p, i, s)
                            uses = len(range(k % 2, MOD_PER_EXPERT, 2))
                            if k >= 2:
                                act.wait_ge(s_mr[k % 2], (i * uses + k // 2) * 16)
                            act.activation(MROW[:, k % 2, :], PS[2 * (s % BANK_SETS)][0:4, 0:256], ACT.Copy).then_inc(s_eva, 1)
                            act.wait_ge(s_eva, p.evacs("a", i, s + 1))
                            act.dma_start(mod_rows[:, i * MOD_PER_EXPERT + k, :], MROW[:, k % 2, :]).then_inc(s_mr[k % 2], 16)
                            ahead(p, i, s, (1,))
                            s += 1
                    for m in range(KC):
                        ahead(p, i, s)
                        s += 1
                    if "a" in p.kinds:
                        for b in range(2):
                            act.wait_ge(s_mr[b], (i + 1) * 16 * len(range(b, MOD_PER_EXPERT, 2)))

                iterate(act, p, body)

            def copy_step(p, i, s, dsts, n):
                ahead(p, i, s, (0,))
                multiplied(act, p, i, s)
                act.activation(dsts[0], PS[2 * (s % BANK_SETS)][:, 0:n], ACT.Copy)
                act.activation(dsts[1], PS[2 * (s % BANK_SETS) + 1][:, 0:n], ACT.Copy).then_inc(s_eva, 1)
                ahead(p, i, s, (1,))

            def attention(name):
                a = atts[name]

                def exps(it, u):
                    half, qt, k0, nk, _ = unit_of(a, u)
                    nq = a.qts[qt][1]
                    b = u % 2
                    g = a.unit0 + it * a.units + u
                    act.wait_ge(s_sb, g + 1)
                    reach(act, s_o, two_ago(a, it, u))
                    last = act.activation(a.sbf[0:nq, b, 0:nk], a.sbf[0:nq, b, 0:nk], ACT.Exp, bias=NM[0:nq, b:b + 1],
                                          accum_out=DEN[0:nq, b:b + 1])
                    if a.sink:
                        c = 2 * it + half
                        col = SK1[:, a.layer, bass.ds(c, 1)] if name[0] == "b" else SK2[:, bass.ds(c, 1)]
                        last = act.activation(ESK[0:nq, b:b + 1], col[0:nq, :], ACT.Exp, bias=NM[0:nq, b:b + 1])
                    last.then_inc(s_ex, 1)

                def copy_turned(it, u):
                    half, qt, k0, nk, tiles = unit_of(a, u)
                    nq = a.qts[qt][1]
                    g = a.unit0 + it * a.units + u
                    act.wait_ge(s_tp, g + 1)
                    reach(act, s_pv, two_ago(a, it, u))
                    if nq == P and all(a.vt[j][1] == P for j in tiles):
                        act.activation(a.pt[:, u % 2, 0:len(tiles) * P], PS[2 + u % 2][:, 0:len(tiles) * P],
                                       ACT.Copy).then_inc(s_pt, 1)
                    else:
                        for x, j in enumerate(tiles):
                            nt = a.vt[j][1]
                            last = act.activation(a.pt[0:nt, u % 2, x * P:x * P + nq],
                                                  PS[2 + u % 2][0:nt, x * P:x * P + nq], ACT.Copy)
                        last.then_inc(s_pt, 1)

                def values(it, kv):
                    act.wait_ge(s_vt, a.kv0 + kv + 1)
                    reach(act, s_pv, a.unit0 + it * a.units)
                    for j, (c, nt) in enumerate(a.vt):
                        last = act.activation(a.vs[0:nt, j, :], PS[7][0:nt, j * P:(j + 1) * P], ACT.Copy)
                    last.then_inc(s_vs, 1)

                for grp in range(a.groups):
                    if not a.kv_dyn:
                        values(grp * a.inner, grp)
                    for loop in pairs_of_heads(act, a):
                        with loop as i:
                            it = i + grp * a.inner
                            if a.kv_dyn:
                                values(it, it)
                            exps(it, 0)
                            for u in range(a.units):
                                if u + 1 < a.units:
                                    exps(it, u + 1)
                                copy_turned(it, u)
                            act.wait_ge(s_ot, a.it0 + it + 1)
                            act.activation(UH[:, bass.ds(it, 1), a.u0 + a.lo:a.u0 + a.hi].rearrange("p a t -> p (a t)"),
                                           PS[6][:, a.lo:a.hi], ACT.Copy).then_inc(s_ath, 1)

            act.wait_ge(s_const, 16 * 10)
            act.activation(SCF[:, :, :], CC[:, :, :], ACT.Silu).then_inc(s_silc, 1)
            act.wait_ge(s_brow, 2)
            act.activation(BROW[:, 0:BW], PS[0][0:8, 0:BW], ACT.Copy).then_inc(s_brow, 1)
            act.activation(BROW[:, BW:2 * BW], PS[1][0:8, 0:BW], ACT.Copy).then_inc(s_brow, 1)
            for s in range(AHEAD):
                for h in range(PIECES):
                    high(ph["win0"], 0, s, h)
            norm("emb", H, H, V_EMB, 0, L1)
            for i in range(DEPTH):
                c0, n = (0, L1) if i == 0 else (NMETA, SEQ)
                p = ph[f"win{i}"]
                make_u(f"win{i}", 0, L1, False, "emb" if i == 0 else "b0")
                for s in range(3):
                    copy_step(p, 0, s, (Q1[:, 2 * s, :], Q1[:, 2 * s + 1, :]), L1)
                for s in range(3, 7):
                    ahead(p, 0, s, (0,))
                    multiplied(act, p, 0, s)
                    if s >= 5:
                        act.wait_ge(s_evd, p.evacs("d", 0, s - 1))
                    act.activation(TMP[:, s % 2, 0:L1], PS[2 * (s % BANK_SETS) + 1][:, 0:L1], ACT.Sigmoid).then_inc(s_sil, 1)
                    ahead(p, 0, s, (1,))
                for s in range(7, 15):
                    ahead(p, 0, s, (0,))
                    multiplied(act, p, 0, s)
                    for j in range(2):
                        last = act.activation(SG[:, 2 * (s - 7) + j, :], PS[2 * (s % BANK_SETS) + j][:, 0:L1], ACT.Sigmoid)
                    last.then_inc(s_eva, 1)
                    ahead(p, 0, s, (1,))
                attention(f"b{i}")
                norm(f"cv{i}", CONV, CONV, V_CLN + 8 * i, c0, n, ACT.Silu)
                for c in range(KCV):
                    act.wait_ge(s_ln, LN_BASE[f"cv{i}"] + c + 1)
                    act.activation(UH[:, 4 + c, c0:c0 + n], CONV[:, c, c0:c0 + n], ACT.Copy).then_inc(s_mixh, 1)
                p = ph[f"proj{i}"]
                for s in range(4):
                    ahead(p, 0, s)
                    for m in range(2):
                        act.wait_ge(s_mix, KC * i + 2 * s + m + 1)
                        act.activation(MIXH[:, 2 * s + m, c0:c0 + n], TMP[:, 2 + m, 0:n], ACT.Copy).then_inc(s_mixh, 1)
                p = ph[f"wout{i}"]
                for s in range(4):
                    ahead(p, 0, s)
                norm(f"a{i}", H, H, V_LN1 + 16 * i, c0, n)
                nm = "moe" if i else "ffn"
                make_u(nm, c0, n, False, f"a{i}")
                scale_h(nm, c0, n)
                if i == 1:
                    act.wait_ge(s_gate, 1)
                    act.activation(GT[:, :, 1:2], GT[:, :, 0:1], ACT.Exp).then_inc(s_gexp, 1)
                    act.wait_ge(s_silc, 1)
                    for k in range(KC):
                        last = act.activation(SC4[:, k, :, 0:2], SCF[:, k:k + 1, :].to_broadcast([P, 32, 2]), ACT.Copy)
                    last.then_inc(s_silc, 1)
                    act.wait_ge(s_cbp, 1)
                    for b in range(4):
                        act.activation(CB[:, 2 * b:2 * b + 2, :].rearrange("p a t -> p (a t)"), PS[4 + b][:, :],
                                       ACT.Copy).then_inc(s_cb, 1)
                experts(nm, n)
                if i == 1:
                    act.dma_start(MLD[:, :, :], mod_rows.rearrange("r t n -> t r n")).then_inc(s_mrl, 16)
                norm(f"b{i}", H, H, V_LN2 + 16 * i, c0, n)
            for i in range(DEPTH):
                nb = T2 if i == 0 else SEQ
                make_u(f"fa{i}", NMETA, T2, True, None)
                scale_h(f"fa{i}", NMETA, T2)
                experts(f"fa{i}", T2)
                norm(f"2a{i}", H, H, V_B + 48 * i, NMETA, T2)
                nm = "waqkv" if i else "naqkv"
                make_u(nm, NMETA, T2, True, None)
                scale_h(nm, NMETA, nb)
                p = ph[nm]
                if i == 0:
                    with act.Fori(0, p.n_iter) as it:
                        for s in range(4):
                            copy_step(p, it, s, [QKV[:, bass.ds(it * 8 + 2 * s + j, 1), :].rearrange("p a t -> p (a t)")
                                                 for j in range(2)], T2)
                    attention("na")
                else:
                    for s in range(6):
                        n = SEQ if s < 4 else T2
                        copy_step(p, 0, s, (QKV[:, 2 * s, 0:n], QKV[:, 2 * s + 1, 0:n]), n)
                    attention("wa")
                p = ph[f"wo{i}"]
                for s in range(4):
                    ahead(p, 0, s)
                norm(f"2n{i}", H, H, V_B + 48 * i + 16, NMETA, nb)
                make_u(f"fb{i}", NMETA, nb, True, None)
                scale_h(f"fb{i}", NMETA, nb)
                experts(f"fb{i}", nb)
                norm(f"2b{i}", H, H, V_B + 48 * i + 32, NMETA, nb)

        @block.vector
        def _(dve):
            own = Tally(s_dve)

            def link(ins):
                own.inc(ins)
                dve.wait_ge(s_dve, own.value)

            class looped:

                def __init__(self, i, n_iter, per):
                    self.i, self.n_iter, self.per = i, n_iter, per

                def __enter__(self):
                    self.n0 = own.n
                    own.off = 0 if isinstance(self.i, int) else self.i * self.per

                def __exit__(self, *a):
                    assert own.n - self.n0 == self.per, (own.n - self.n0, self.per)
                    own.off = 0
                    if not isinstance(self.i, int):
                        own.n = self.n0 + self.per * self.n_iter

            def low(p, i, s, h):
                lo, hi = bounds(p, s, h)
                slot = p.piece_slot(s, h)
                dve.wait_ge(s_hi, p.piece(i, s, h) + 1)
                dve.tensor_tensor(WL[slot][:, 0:hi - lo], RAW[:, s % RAW_SLOTS, lo:hi],
                                  WH[slot][:, 0:hi - lo].bitcast(F32), ALU.subtract).then_inc(s_lo, 1)

            def ahead(p, i, s, pieces=range(PIECES)):
                later = p.step_ahead(i, s)
                for h in pieces if later else ():
                    low(*later, h)

            def norm(name, src, c0, n):
                b0, cs = LN_BASE[name], (KCV if name.startswith("cv") else KC)
                dve.wait_ge(s_mean, LN_IDX[name] + 1)
                for c in range(cs):
                    x = src[:, c, c0:c0 + n]
                    dve.tensor_tensor(x, x, PS[0][:, 0:n], ALU.subtract).then_inc(s_xc, 1)
                dve.wait_ge(s_std, LN_IDX[name] + 1)
                dve.wait_ge(s_sq, b0 + cs)
                link(dve.reciprocal(RSTD[:, 0:n], STD[:, 0:n]))
                for c in range(cs):
                    x = src[:, c, c0:c0 + n]
                    dve.tensor_tensor(x, x, RSTD[:, 0:n], ALU.mult).then_inc(s_nrm, 1)

            def make_u(name, c0, n, ln, layer=None, idx=None):
                ub = KC * U_IDX[name]
                if layer is None:
                    for c in range(KC):
                        dve.wait_ge(s_uh, ub + c + 1)
                        dve.tensor_tensor(UL[:, c, c0:c0 + n], H[:, c, c0:c0 + n], UH[:, c, c0:c0 + n].bitcast(F32),
                                          ALU.subtract).then_inc(s_ul, 1)
                    return

                def modulate(c):
                    dve.wait_ge(s_ln, LN_BASE[ln] + min(c + 1, KC))
                    if c >= 4:
                        dve.wait_ge(s_ul, ub + c - 3)
                    for st, (t0, nt) in enumerate(STREAM):
                        if t0 < c0 + n:
                            last = dve.tensor_scalar(TMP[:, c % 4, t0 - c0:t0 - c0 + nt], H[:, c, t0:t0 + nt],
                                                     mod(layer, idx + 1, c, st), mod(layer, idx, c, st), ALU.mult, ALU.add)
                    last.then_inc(s_um, 1)

                modulate(0)
                modulate(1)
                for c in range(KC):
                    if c + 2 < KC:
                        modulate(c + 2)
                    dve.wait_ge(s_uh, ub + c + 1)
                    dve.tensor_tensor(UL[:, c, c0:c0 + n], TMP[:, c % 4, 0:n], UH[:, c, c0:c0 + n].bitcast(F32),
                                      ALU.subtract).then_inc(s_ul, 1)

            def experts(name, c0, n, gate=None):
                p = ph[name]
                moe = name == "moe"
                dve.wait_ge(s_hs, S_IDX[name] + 1)

                def body(i):
                    s = 0
                    for k in range(KH):
                        ahead(p, i, s, (0,))
                        multiplied(dve, p, i, s)
                        dve.wait_ge(s_sil, SIL_BASE[name] + k + 1 + i * KH)
                        dve.tensor_tensor(HT[:, k % 2, 0:n], SIL[:, k % 2, 0:n], PS[2 * (s % BANK_SETS) + 1][:, 0:n],
                                          ALU.mult).then_inc(s_evd, 1)
                        if k < KH - 1:
                            ahead(p, i, s, (1,))
                        dve.wait_ge(s_hid, HID_BASE[name] + k + 1 + i * KH)
                        dve.wait_ge(s_evd, p.evacs("d", i, s + 1))
                        dve.tensor_tensor(HIDL[:, k, 0:n], HT[:, k % 2, 0:n], HIDH[:, k, 0:n].bitcast(F32),
                                          ALU.subtract).then_inc(s_hidl, 1)
                        if k == KH - 1:
                            ahead(p, i, s, (1,))
                        s += 1
                        if p.kinds[s] == "a":
                            ahead(p, i, s)
                            s += 1
                    for m in range(KC):
                        ahead(p, i, s, (0,))
                        multiplied(dve, p, i, s)
                        ps = PS[2 * (s % BANK_SETS)]
                        if m == 0:
                            dve.wait_ge(s_evd, p.evacs("d", i, s))
                        if moe:
                            w = CB[:, bass.ds(i, 1), :].rearrange("p a t -> p (a t)")
                            link(dve.tensor_tensor(HT[:, m % 2, 0:n], ps[:, 0:n], w, ALU.mult))
                            x = H[:, m, c0:c0 + n]
                            dve.tensor_tensor(x, x, HT[:, m % 2, 0:n], ALU.add).then_inc(s_evd, 1)
                        elif gate is None:
                            x = H[:, m, c0:c0 + n]
                            dve.tensor_tensor(x, x, ps[:, 0:n], ALU.add).then_inc(s_evd, 1)
                        else:
                            gated(ps, m, n, gate)
                        ahead(p, i, s, (1,))
                        s += 1

                if moe:
                    with dve.Fori(0, p.n_iter) as i, looped(i, p.n_iter, KC):
                        body(i)
                else:
                    iterate(dve, p, body)

            def gated(ps, m, n, gate):
                for st, (t0, nt) in enumerate(STREAM):
                    if t0 < NMETA + n:
                        x = H[:, m, t0:t0 + nt]
                        last = dve.scalar_tensor_tensor(x, ps[:, t0 - NMETA:t0 - NMETA + nt], mod(*gate, m, st), x,
                                                        ALU.mult, ALU.add)
                last.then_inc(s_evd, 1)

            def attention(name):
                a = atts[name]
                first = name[0] == "b"

                def biased(it, u):
                    half, qt, k0, nk, _ = unit_of(a, u)
                    q0, nq = a.qts[qt]
                    b = u % 2
                    g = a.unit0 + it * a.units + u
                    dve.wait_ge(s_sc, g + 1)
                    reach(dve, s_tp, two_ago(a, it, u))
                    ps = PS[b]
                    if first:
                        bt = B1[qt + 3 - len(a.qts)]
                        bias = bt[0:nq, bass.ds(2 * it + half, 1), 0:nk].rearrange("p a t -> p (a t)")
                        ins_ = dve.scalar_tensor_tensor(a.sbf[0:nq, b, 0:nk], ps[0:nq, 0:nk], SCALE, bias,
                                                        ALU.mult, ALU.add)
                    else:
                        nbias = SEQ if nk == T2 else 0
                        if nbias:
                            bias = NB[:, qt, half, :] if name == "na" else CST[:, C_WAM + SEQ * qt:C_WAM + SEQ * (qt + 1)]
                            dve.scalar_tensor_tensor(a.sbf[:, b, 0:SEQ], ps[:, 0:SEQ], SCALE, bias, ALU.mult, ALU.add)
                        ins_ = dve.tensor_scalar(a.sbf[:, b, nbias:nk], ps[:, nbias:nk], SCALE, None, ALU.mult)
                    link(ins_)
                    if a.sink:
                        link(dve.tensor_reduce(NMX[0:nq, b:b + 1], a.sbf[0:nq, b, 0:nk], AX_X, ALU.max, negate=True))
                        nsk = NSK1[:, a.layer, bass.ds(2 * it + half, 1)] if first else NSK2[:, bass.ds(2 * it + half, 1)]
                        dve.tensor_tensor(NM[0:nq, b:b + 1], NMX[0:nq, b:b + 1], nsk[0:nq, :], ALU.min).then_inc(s_sb, 1)
                    else:
                        dve.tensor_reduce(NM[0:nq, b:b + 1], a.sbf[0:nq, b, 0:nk], AX_X, ALU.max,
                                          negate=True).then_inc(s_sb, 1)

                def scaled(it, u):
                    half, qt, k0, nk, _ = unit_of(a, u)
                    nq = a.qts[qt][1]
                    b = u % 2
                    g = a.unit0 + it * a.units + u
                    dve.wait_ge(s_ex, g + 1)
                    if a.sink:
                        link(dve.tensor_tensor(DEN[0:nq, b:b + 1], DEN[0:nq, b:b + 1], ESK[0:nq, b:b + 1], ALU.add))
                    link(dve.reciprocal(RDEN[0:nq, b:b + 1], DEN[0:nq, b:b + 1]))
                    dve.wait_ge(s_pv, g + 1)
                    dve.tensor_scalar(a.os[0:nq, qt, HD * half:HD * half + HD], PS[4 + b][0:nq, 0:HD],
                                      RDEN[0:nq, b:b + 1], None, ALU.mult).then_inc(s_o, 1)

                per = a.units * (2 + 2 * a.sink)
                for grp in range(a.groups):
                    for loop in pairs_of_heads(dve, a):
                        with loop as i, looped(i, a.inner, per):
                            it = i + grp * a.inner
                            if name == "na":
                                dve.wait_ge(s_nb, it + 1)
                            biased(it, 0)
                            biased(it, 1)
                            reach(dve, s_ot, a.it0 + it)
                            for u in range(a.units):
                                if u + 2 < a.units:
                                    biased(it, u + 2)
                                scaled(it, u)
                            dve.wait_ge(s_ath, a.it0 + it + 1)
                            uu = slice(a.u0 + a.lo, a.u0 + a.hi)
                            dve.tensor_tensor(UL[:, bass.ds(it, 1), uu].rearrange("p a t -> p (a t)"),
                                              PS[6][:, a.lo:a.hi],
                                              UH[:, bass.ds(it, 1), uu].rearrange("p a t -> p (a t)").bitcast(F32),
                                              ALU.subtract).then_inc(s_atl, 1)

            def conv(layer, c0, n, lo, hi):
                for w in range(lo, hi):
                    for c in range(KCV):
                        x = HPAD[:, c, c0 + w:c0 + w + n]
                        y = CONV[:, c, c0:c0 + n]
                        tap = vec(V_DW + (layer * KCV + c) * TAPS + w)
                        if w == 0:
                            own.inc(dve.tensor_scalar(y, x, tap, vec(V_CB + 4 * layer + c), ALU.mult, ALU.add))
                        elif w < TAPS - 1:
                            dve.wait_ge(s_dve, own.value - KCV + 1)
                            own.inc(dve.scalar_tensor_tensor(y, x, tap, y, ALU.mult, ALU.add))
                        else:
                            dve.wait_ge(s_dve, own.value - KCV + 1 + c)
                            dve.scalar_tensor_tensor(y, x, tap, y, ALU.mult, ALU.add).then_inc(s_cv, 1)

            dve.wait_ge(s_const, 16 * 10)
            own.inc(dve.tensor_scalar(NSK1[:, :, :], SK1[:, :, :], -1.0, None, ALU.mult))
            link(dve.tensor_scalar(NSK2[:, :], SK2[:, :], -1.0, None, ALU.mult))
            for s in range(AHEAD):
                for h in range(PIECES):
                    low(ph["win0"], 0, s, h)
            norm("emb", H, 0, L1)
            for i in range(DEPTH):
                c0, n = (0, L1) if i == 0 else (NMETA, SEQ)
                make_u(f"win{i}", 0, L1, None)
                p = ph[f"win{i}"]
                for s in range(3):
                    ahead(p, 0, s)
                dve.wait_ge(s_ms, 4 + i)
                for s in range(3, 7):
                    ahead(p, 0, s, (0,))
                    multiplied(dve, p, 0, s)
                    dve.wait_ge(s_sil, SIL_BASE[f"win{i}"] + s - 2)
                    dve.tensor_tensor(HPAD[:, s - 3, TAPS - 1:TAPS - 1 + L1], PS[2 * (s % BANK_SETS)][:, 0:L1],
                                      TMP[:, s % 2, 0:L1], ALU.mult).then_inc(s_evd, 1)
                    ahead(p, 0, s, (1,))
                dve.wait_ge(s_evd, p.evacs("d", 0, 7))
                for s in range(7, 15):
                    ahead(p, 0, s)
                    conv(i, c0, n, 4 * (s - 7), min(4 * (s - 6), TAPS))
                dve.wait_ge(s_b1, 16 * 5 * (i + 1))
                attention(f"b{i}")
                norm(f"cv{i}", CONV, c0, n)
                for c in range(KCV):
                    dve.wait_ge(s_mixh, (KCV + KC) * i + c + 1)
                    dve.tensor_tensor(UL[:, 4 + c, c0:c0 + n], CONV[:, c, c0:c0 + n],
                                      UH[:, 4 + c, c0:c0 + n].bitcast(F32), ALU.subtract).then_inc(s_mixl, 1)
                p = ph[f"proj{i}"]
                for s in range(4):
                    ahead(p, 0, s, (0,))
                    multiplied(dve, p, 0, s)
                    for m in range(2):
                        c = 2 * s + m
                        ps = [PS[4 * (s % 2) + 2 * m + b][:, 0:n] for b in range(2)]
                        dve.tensor_tensor(TMP[:, 0, 0:n], ps[0], SG[:, c, c0:c0 + n], ALU.mult)
                        second = dve.tensor_tensor(TMP[:, 1, 0:n], ps[1], SG[:, KC + c, c0:c0 + n], ALU.mult)
                        if m:
                            second.then_inc(s_evd, 1)
                            dve.wait_ge(s_evd, p.evacs("d", 0, s + 1))
                        else:
                            link(second)
                        dve.tensor_tensor(TMP[:, 2 + m, 0:n], TMP[:, 0, 0:n], TMP[:, 1, 0:n], ALU.add).then_inc(s_mix, 1)
                        dve.wait_ge(s_mixh, (KCV + KC) * i + KCV + c + 1)
                        dve.tensor_tensor(MIXL[:, c, c0:c0 + n], TMP[:, 2 + m, 0:n],
                                          MIXH[:, c, c0:c0 + n].bitcast(F32), ALU.subtract).then_inc(s_mixl, 1)
                    ahead(p, 0, s, (1,))
                p = ph[f"wout{i}"]
                for s in range(4):
                    ahead(p, 0, s, (0,))
                    multiplied(dve, p, 0, s)
                    for j in range(2):
                        x = H[:, 2 * s + j, c0:c0 + n]
                        last = dve.scalar_tensor_tensor(x, x, ALPHA, PS[2 * (s % BANK_SETS) + j][:, 0:n], ALU.mult, ALU.add)
                    last.then_inc(s_evd, 1)
                    ahead(p, 0, s, (1,))
                norm(f"a{i}", H, c0, n)
                nm = "moe" if i else "ffn"
                make_u(nm, c0, n, None)
                if i == 1:
                    dve.wait_ge(s_rt, 1)
                    link(dve.tensor_copy(LG[:, :, :].rearrange("p a e -> p (a e)"), PS[2][:, 0:16]))
                    for t in range(2):
                        link(dve.max(MX8[:, t, :], LG[:, t, :]))
                        link(dve.max_index(IX8[:, t, :], MX8[:, t, :], LG[:, t, :]))
                    link(dve.tensor_copy(IXF[:, :, :], IX8[:, :, :]))
                    dve.tensor_tensor(GT[:, :, 0:1], MX8[:, :, 1:2], MX8[:, :, 0:1], ALU.subtract).then_inc(s_gate, 1)
                    dve.wait_ge(s_gexp, 1)
                    link(dve.tensor_scalar(GT[:, :, 2:3], GT[:, :, 1:2], 1.0, None, ALU.add))
                    link(dve.reciprocal(GT[:, :, 2:3], GT[:, :, 2:3]))
                    link(dve.tensor_tensor(GT[:, :, 3:4], GT[:, :, 1:2], GT[:, :, 2:3], ALU.mult))
                    for t in range(2):
                        for r, oh in enumerate((OH1, OH2)):
                            link(dve.tensor_scalar(oh[:, t, :], CST[:, C_IOTA:C_IOTA + 8], IXF[:, t, r:r + 1],
                                                   GT[:, t, 2 + r:3 + r], ALU.is_equal, ALU.mult))
                    link(dve.tensor_tensor(OH1[:, :, :], OH1[:, :, :], OH2[:, :, :], ALU.add))
                    for t in range(2):
                        last = dve.tensor_copy(CBB[:, t, :, :], OH1[:, t, :].rearrange("p (e a) -> p e a", a=1)
                                               .to_broadcast([P, N_EXP, P]))
                    last.then_inc(s_gate, 1)
                    dve.wait_ge(s_silc, 2)
                    for k in range(KC):
                        last = dve.tensor_tensor(SC4[:, k, :, 2:4], SCF[:, k:k + 1, :].to_broadcast([P, 32, 2]),
                                                 SC4[:, k, :, 0:2].bitcast(F32), ALU.subtract)
                    last.then_inc(s_silc, 1)
                    dve.wait_ge(s_cb, 4)
                experts(nm, c0, n)
                dve.wait_ge(s_evd, ph[nm].evacs("d", ph[nm].n_iter, 0))
                norm(f"b{i}", H, c0, n)
            dve.wait_ge(s_mrt, 1)
            for st in range(2):
                for j in range(2):
                    turned = PS[3 + j]
                    own.inc(dve.tensor_tensor(MOD[:, st, :, j], turned[:, st * MOD_STEPS:(st + 1) * MOD_STEPS],
                                              VEC[:, V_BM + j:V_BM + 2 * MOD_STEPS:2], ALU.add))
            dve.wait_ge(s_dve, own.value)
            for st in range(2):
                for j in range(2):
                    turned = PS[3 + j]
                    own.inc(dve.tensor_tensor(MOD[:, st, :, j], MOD[:, st, :, j],
                                              turned[:, (2 + st) * MOD_STEPS:(3 + st) * MOD_STEPS], ALU.add))
            dve.wait_ge(s_dve, own.value)
            for l in range(2):
                for idx in (1, 4, 7, 2, 8):
                    m = MOD[:, :, l * 36 + idx * 4:l * 36 + idx * 4 + 4, :]
                    own.inc(dve.tensor_scalar(m, m, *((1.0, None, ALU.add) if idx in (1, 4, 7) else (0.5, None, ALU.mult))))
            dve.wait_ge(s_dve, own.value)
            for i in range(DEPTH):
                nb = T2 if i == 0 else SEQ
                make_u(f"fa{i}", NMETA, T2, "b1" if i == 0 else "2b0", i, 0)
                experts(f"fa{i}", NMETA, T2, (i, 2))
                dve.wait_ge(s_evd, ph[f"fa{i}"].evacs("d", 2, 0))
                norm(f"2a{i}", H, NMETA, T2)
                nm = "waqkv" if i else "naqkv"
                make_u(nm, NMETA, T2, f"2a{i}", i, 3)
                p = ph[nm]
                if i == 0:
                    with dve.Fori(0, p.n_iter) as it:
                        for s in range(4):
                            ahead(p, it, s)
                    attention("na")
                else:
                    for s in range(6):
                        ahead(p, 0, s)
                    dve.wait_ge(s_eva, p.evacs("a", 0, 6))
                    for c in range(10):
                        dve.wait_ge(s_rsw, c + 1)
                        x = QKV[:, c, 0:SEQ]
                        own.inc(dve.tensor_tensor(TMP[:, c % 2, 0:SEQ], PS[c % 2][:, 0:SEQ], CST[:, C_SIN:C_SIN + SEQ], ALU.mult))
                        link(dve.tensor_tensor(x, x, CST[:, C_COS:C_COS + SEQ], ALU.mult))
                        dve.tensor_tensor(x, x, TMP[:, c % 2, 0:SEQ], ALU.add).then_inc(s_rope, 1)
                    attention("wa")
                p = ph[f"wo{i}"]
                dve.wait_ge(s_hs, S_IDX[nm] + 1)
                for s in range(4):
                    ahead(p, 0, s, (0,))
                    multiplied(dve, p, 0, s)
                    for j in range(2):
                        m = 2 * s + j
                        for st, (t0, nt) in enumerate(STREAM):
                            if t0 < NMETA + nb:
                                x = H[:, m, t0:t0 + nt]
                                last = dve.scalar_tensor_tensor(x, PS[2 * (s % BANK_SETS) + j][:, t0 - NMETA:t0 - NMETA + nt],
                                                                mod(i, 5, m, st), x, ALU.mult, ALU.add)
                    last.then_inc(s_evd, 1)
                    ahead(p, 0, s, (1,))
                norm(f"2n{i}", H, NMETA, nb)
                make_u(f"fb{i}", NMETA, nb, f"2n{i}", i, 6)
                experts(f"fb{i}", NMETA, nb, (i, 8))
                dve.wait_ge(s_evd, ph[f"fb{i}"].evacs("d", 2, 0))
                norm(f"2b{i}", H, NMETA, nb)


def _linear(w, order=None):
    if order is not None:
        w = w[:, order]
    k, m = w.shape
    return np.ascontiguousarray(w.reshape(k // P, P, m // 256, 256).transpose(2, 1, 0, 3).reshape(m // 256, P, -1))


def _gate_up(g, u):
    e = g.shape[0]
    both = np.stack([g, u], 2).reshape(e, KC, P, 2, KH, P)
    return both.transpose(0, 4, 2, 1, 3, 5).reshape(e, KH, P, W_STEP)


def _down(w):
    e = w.shape[0]
    return w.reshape(e, KH, P, KC, P).transpose(0, 3, 2, 1, 4).reshape(e, KC, P, D_EXP)


def _halves(w_in):
    return np.stack([w_in[:, :D_EXP], w_in[:, D_EXP:]])


def _features(v):
    v = np.asarray(v)
    return v.reshape(-1, P).T


def lay_out(x):
    x = {k: np.asarray(v) for k, v in x.items()}
    consts, onehot = shape_constants()
    heads = [h for c in range(4) for h in (c, 4 + c)]
    hcols = np.concatenate([np.arange(h * HD, (h + 1) * HD) for h in heads])
    order = [hcols, np.arange(512, 768)]
    for t in range(KCV):
        order += [768 + t * P + np.arange(P), 768 + CONVC + t * P + np.arange(P)]
    order = np.concatenate(order + [np.arange(768 + 2 * CONVC, 768 + 2 * CONVC + 2 * D)])
    wheads = [8 * p + 4 * half + i for p in range(2) for i in range(4) for half in range(2)]
    wcols = np.concatenate([np.arange(h * HD, (h + 1) * HD) for h in wheads])
    arrays = {
        "consts": consts, "onehot": onehot, "neg_row": np.full((1, 8), NEG, np.float32),
        "tokens": np.concatenate([x["meta_tokens"], x["x"][0]]).T.reshape(KC, P, L1).transpose(1, 0, 2),
        "ctx": x["ctx_2"][0].T.reshape(KC, P, CTX).transpose(1, 0, 2),
        "cond": np.stack([x["c_2"][0], x["c_ctx_2"]]).reshape(2, KC, P).transpose(2, 1, 0),
        "rel_bias": x["rel_bias"][:, heads],
        "sinks": x["sinks"][:, heads],
        "sinks_2": x["wa_sinks_2"][:, wheads],
        "router": x["router"][0].reshape(KC, P, N_EXP).transpose(1, 0, 2),
        "na_rpb": x["na_rpb_2"].reshape(1, -1),
        "w_in": np.stack([_linear(x["w_in"][i], order) for i in range(DEPTH)]),
        "w_proj": np.stack([np.concatenate([_linear(x["w_attn_proj"][i][hcols]), _linear(x["w_conv_proj"][i])], 2)
                            for i in range(DEPTH)]),
        "w_out": np.stack([_linear(x["w_out"][i]) for i in range(DEPTH)]),
        "w_mod": np.concatenate([_linear(x["w_mod_2"][i]) for i in range(DEPTH)]),
        "w_na": _linear(x["na_w_qkv_2"][0]),
        "w_wa": _linear(x["wa_w_qkv_2"][0], np.concatenate([wcols, np.arange(D, D + 512)])),
        "w_o": np.stack([_linear(x["na_w_o_2"][0]), _linear(x["wa_w_o_2"][0][wcols])]),
    }
    g, u, d = [_halves(x["ffn_w_gate"][0]), x["moe_w_gate"][0]], [_halves(x["ffn_w_up"][0]), x["moe_w_up"][0]], \
        [x["ffn_w_down"][0].reshape(2, D_EXP, D), x["moe_w_down"][0]]
    for i in range(DEPTH):
        for j in range(2):
            w = x["ffn_w_in_2"][i, j]
            g.append(_halves(w[:, :2 * D_EXP]))
            u.append(_halves(w[:, 2 * D_EXP:]))
            d.append(x["ffn_w_out_2"][i, j].reshape(2, D_EXP, D))
    arrays["w_gu"] = np.concatenate([_gate_up(a, b) for a, b in zip(g, u)])
    arrays["w_dn"] = np.concatenate([_down(a) for a in d])
    cols = [_features(x["emb_ln_g"]), _features(x["emb_ln_b"])]
    for gg, bb in (("ln1_g", "ln1_b"), ("ln2_g", "ln2_b")):
        for i in range(DEPTH):
            cols += [_features(x[gg][i]), _features(x[bb][i])]
    for i in range(DEPTH):
        for j in range(3):
            cols += [_features(x["ln_g_2"][i, j]), _features(x["ln_b_2"][i, j])]
    for i in range(DEPTH):
        cols += [_features(x["conv_ln_g"][i]), _features(x["conv_ln_b"][i])]
    cols += [_features(x["conv_b"])]
    for i in range(DEPTH):
        cols += [x["conv_dw"][i].T.reshape(KCV, P, TAPS).transpose(1, 0, 2).reshape(P, -1)]
    cols += [_features(x["b_mod_2"])]
    arrays["vectors"] = np.concatenate(cols, 1)
    return {k: np.ascontiguousarray(v) for k, v in arrays.items()}


def kernel(**inputs):
    import concourse.bacc as bacc
    from concourse.bass_utils import run_bass_kernel_spmd as run

    nc = bacc.Bacc("TRN2", target_bir_lowering=False, num_devices=1)
    arrays = lay_out(inputs)
    ins = {k: nc.dram_tensor(f"in_{k}", a.shape, F32, kind="ExternalInput").ap() for k, a in arrays.items()}
    out = nc.dram_tensor("out_h", (P, KC, SEQ), F32, kind="ExternalOutput").ap()
    build(nc, ins, out)
    r = run(nc, [{f"in_{k}": a for k, a in arrays.items()}], core_ids=[0])
    got = r.results[0]["out_h"]
    return got.transpose(2, 1, 0).reshape(1, SEQ, D)
```

```python
import math
from contextlib import ExitStack, nullcontext

import numpy as np

import concourse.bass as bass
import concourse.mybir as mybir

F32 = mybir.dt.float32
F32R = mybir.dt.float32r
U32 = mybir.dt.uint32
ACT = mybir.ActivationFunctionType
ALU = mybir.AluOpType
AX_X = mybir.AxisListType.X

P = 128
D = 1024
KC = D // P
NMETA, SEQ, CTX = 16, 256, 256
L1 = NMETA + SEQ
T2 = SEQ + CTX
TALL = L1 + CTX
DEPTH = 2
ALPHA = float((2 * DEPTH) ** 0.25)
EPS = 1e-5
HD = 64
SCALE = HD ** -0.5
D_EXP = 1408
KH = D_EXP // P
DOWN_CUT = 6
N_EXP = 8
CONVC = 512
KCV = CONVC // P
TAPS = 31
DVE_CONV = 3
POOL_STEPS = 2 * TAPS - 1
NBUCK = 32
NEG = -1e30
RAW_SLOTS = 4
PIECES = 2
PIECE_SLOTS = 4
PIECE_W = 1024
AHEAD = 2
BANK_SETS = 4
W_STEP = 2048
MOD_STEPS = 2 * 9 * D // 256
MOD_PER_EXPERT = MOD_STEPS // N_EXP
BW = 400
RPB_R, RPB_C = 15, 31
RPB_LEN = 16 * RPB_R * RPB_C

C_ID, C_PERM, C_COS, C_SIN = 0, 128, 256, 512
C_NAM, C_WAM, C_IOTA, C_END = 768, 832, 1344, 1352

V_EMB = 0
V_LN1 = 16
V_LN2 = V_LN1 + 32
V_B = V_LN2 + 32
V_CLN = V_B + 96
V_CB = V_CLN + 16
V_DW = V_CB + 8
V_BM = V_DW + 2 * KCV * TAPS
V_END = V_BM + 144


def shape_constants():
    c = np.zeros((P, C_END), np.float32)
    c[:, C_ID:C_ID + P] = np.eye(P)
    inv = (10000.0 ** (-np.arange(16, dtype=np.float32) / 16)).astype(np.float32)
    t = np.arange(SEQ)
    for p in range(P):
        d = p % HD
        second = d % 32 >= 16
        partner = p - 16 if second else p + 16
        c[partner, C_PERM + p] = 1.0
        pos = (t // 64 if d < 32 else t % 64).astype(np.float32)
        ang = pos * inv[d % 16]
        c[p, C_COS:C_COS + SEQ] = np.cos(ang)
        c[p, C_SIN:C_SIN + SEQ] = np.sin(ang) * (1.0 if second else -1.0)
    qc, kc = np.arange(64)[:, None], np.arange(64)[None, :]
    start = np.clip(qc - 8, 0, 48)
    seen = (kc >= start) & (kc < start + 16)
    c[:, C_NAM:C_NAM + 64] = np.tile(np.where(seen, 0.0, NEG), (2, 1))
    for b in range(2):
        q = b * P + np.arange(P)[:, None]
        far = np.abs(q - np.arange(SEQ)[None, :]) > 128
        c[:, C_WAM + b * SEQ:C_WAM + (b + 1) * SEQ] = np.where(far, NEG, 0.0)
    c[:, C_IOTA:C_IOTA + 8] = np.arange(8)
    oh = np.zeros((NBUCK + 1, 2, BW), np.float32)
    dist = L1 - np.arange(BW)
    n = np.maximum(dist, 0)
    nf = np.maximum(n, 1).astype(np.float32)
    large = 16 + (np.log(nf / np.float32(16)) / np.float32(math.log(8)) * 16).astype(np.int32)
    bucket = np.where(n < 16, n, np.minimum(large, 31))
    for v in range(2):
        oh[bucket, v, np.arange(BW)] = 1.0
        masked = (dist < 0) | ((dist >= 128) if v else False)
        oh[NBUCK, v] = np.where(masked, 1.0, 0.0)
    return c, oh.reshape(NBUCK + 1, 2 * BW)


class Phase:

    def __init__(self, name, prev, n_iter, kinds, cols, last):
        self.name, self.n_iter, self.kinds, self.cols, self.n, self.last = name, n_iter, kinds, cols, len(kinds), last
        self.pieces = PIECES * self.n
        self.prev = prev
        self.a0 = self.d0 = self.p0 = 0
        self.raw0 = [0] * RAW_SLOTS
        self.next = None
        if prev is not None:
            prev.next = self
            self.a0 = prev.evacs("a", prev.n_iter, 0)
            self.d0 = prev.evacs("d", prev.n_iter, 0)
            self.p0 = prev.p0 + prev.pieces * prev.n_iter
            self.raw0 = [prev.raw0[r] + prev.n_iter * len(range(r, prev.n, RAW_SLOTS)) for r in range(RAW_SLOTS)]

    def piece(self, i, s, h):
        return self.p0 + PIECES * s + h + i * self.pieces

    def piece_slot(self, s, h):
        return (PIECES * s + h) % PIECE_SLOTS

    def evacs(self, kind, i, s):
        if kind == "d":
            return self.d0 + self.kinds[:s].count("d") + i * self.kinds.count("d")
        return self.a0 + s - self.kinds[:s].count("d") + i * (self.n - self.kinds.count("d"))

    def loads(self, i, s):
        r = s % RAW_SLOTS
        per = len(range(r, self.n, RAW_SLOTS))
        return self.raw0[r] + s // RAW_SLOTS + 1 + i * per

    def behind(self, r):
        phases = [p for p in (self if self.n_iter > 1 else None, self.prev) if p is not None]
        return min(p.n - 1 - max(x for x in range(p.n) if x % RAW_SLOTS == r) for p in phases)

    def step_ahead(self, i, s):
        if s + AHEAD < self.n:
            return self, i, s + AHEAD
        if self.n_iter > 1 and not (isinstance(i, int) and i + 1 == self.n_iter):
            return self, i + 1, s + AHEAD - self.n
        return self.next and (self.next, 0, s + AHEAD - self.n)

    def raw_user(self, i, s):
        if s >= RAW_SLOTS:
            return self.piece(i, s - RAW_SLOTS, PIECES - 1) + 1
        return self.piece(i, 0, 0) - PIECES * self.behind(s % RAW_SLOTS)

    def piece_user(self, i, s, h):
        q = PIECES * s + h
        if q >= PIECE_SLOTS:
            return self.piece(i, s, h) - PIECE_SLOTS + 1
        before = self.prev if isinstance(i, int) and i == 0 else self
        follow = before.pieces - 1 - max(x for x in range(before.pieces) if x % PIECE_SLOTS == q)
        return self.piece(i, 0, 0) - follow

    def bank_user(self, i, s):
        if s >= BANK_SETS:
            kind = self.kinds[s - BANK_SETS]
            return kind, self.evacs(kind, i, s - BANK_SETS + 1)
        kind = self.kinds[-1]
        after = self.n - 1 - max(x for x in range(self.n) if x % BANK_SETS == s)
        assert set(self.kinds[self.n - BANK_SETS:]) == {kind}
        return kind, self.evacs(kind, i, 0) - after


def plan():
    ph = {}
    prev = None
    full, down = [W_STEP] * KH, [D_EXP] * KC

    def add(name, n_iter, kinds, cols=None):
        nonlocal prev
        prev = ph[name] = Phase(name, prev, n_iter, kinds, cols or [W_STEP] * len(kinds), name == "fb1")

    moe_kinds, moe_cols = "", []
    for k in range(KH):
        moe_kinds += "d" + ("a" if k < MOD_PER_EXPERT else "")
        moe_cols += [W_STEP] * (2 if k < MOD_PER_EXPERT else 1)
    for i in range(2):
        add(f"win{i}", 1, "aaa" + "dddd" + "a" * 8)
        add(f"proj{i}", 1, "dddd")
        add(f"wout{i}", 1, "dddd")
        if i == 0:
            add("ffn", 2, "d" * 19, full + down)
        else:
            add("moe", N_EXP, moe_kinds + "d" * 8, moe_cols + down)
    for i in range(2):
        add(f"fa{i}", 2, "d" * 19, full + down)
        if i == 0:
            add("naqkv", 3, "aaaa")
        else:
            add("waqkv", 1, "aaaaaa")
        add(f"wo{i}", 1, "dddd")
        add(f"fb{i}", 2, "d" * 19, full + down)
    return ph


class Tally:

    def __init__(self, sem):
        self.sem, self.n, self.off = sem, 0, 0

    def inc(self, ins, by=1):
        self.n += by
        ins.then_inc(self.sem, by)
        return ins

    @property
    def value(self):
        return self.n + self.off


def build(nc, ins, out):
    ph = plan()
    ctx = ExitStack()
    with ctx:
        def sb(name, shape, dt=F32, where=None):
            return (where or ctx).enter_context(nc.sbuf_tensor(name, shape, dt))

        def sem(name):
            return ctx.enter_context(nc.semaphore(name))

        RAW = sb("RAW", [P, RAW_SLOTS, W_STEP])
        WH = [sb(f"WH{h}", [P, PIECE_W], F32R) for h in range(PIECE_SLOTS)]
        WL = [sb(f"WL{h}", [P, PIECE_W], F32R) for h in range(PIECE_SLOTS)]
        H = sb("H", [P, KC, TALL])
        UH = sb("UH", [P, KC, TALL], F32R)
        UL = sb("UL", [P, KC, TALL], F32R)
        TMP = sb("TMP", [P, 4, T2])
        MLD = TMP[0:MOD_STEPS, 0:2, :].rearrange("p a (b n) -> p (a b) n", b=2)
        STD = sb("STD", [P, T2])
        RSTD = sb("RSTD", [P, T2])
        CST = sb("CST", [P, C_END])
        VEC = sb("VEC", [P, V_END])
        MOD = sb("MOD", [P, 2, MOD_STEPS, 2])
        RT = sb("RT", [P, KC, N_EXP])
        CC = sb("CC", [P, KC, 2])
        SCF = sb("SCF", [P, KC, 2])
        ONES = sb("ONES", [P, P])
        ONESC = sb("ONESC", [P, P])
        EPST = sb("EPST", [P, 1])
        SK1 = sb("SK1", [P, 2, 8])
        SK2 = sb("SK2", [P, 16])
        NSK1 = sb("NSK1", [P, 2, 8])
        NSK2 = sb("NSK2", [P, 16])
        NM = sb("NM", [P, 4])
        NMX = sb("NMX", [P, 4])
        DEN = sb("DEN", [P, 4])
        ESK = sb("ESK", [P, 4])
        RDEN = sb("RDEN", [P, 4])
        LG = sb("LG", [P, 2, 8])
        MX8 = sb("MX8", [P, 2, 8])
        IX8 = sb("IX8", [P, 2, 8], U32)
        IXF = sb("IXF", [P, 2, 8])
        OH1 = sb("OH1", [P, 2, 8])
        OH2 = sb("OH2", [P, 2, 8])
        GT = sb("GT", [P, 2, 4])
        with ExitStack() as region:
            HIDH = sb("HIDH", [P, KH, T2], F32R, region)
            HIDL = sb("HIDL", [P, KH, T2], F32R, region)
            SILHT = sb("SILHT", [P, 4, T2], where=region)
            CB = sb("CB", [P, N_EXP, SEQ], where=region)
            SC4 = sb("SC4", [P, KC, 32, 4], F32R, region)
            MROW = sb("MROW", [4, 2, 256], where=region)
        SIL, HT = SILHT[:, 0:2, :], SILHT[:, 2:4, :]
        CBB = SILHT[:, :, :].rearrange("p a b -> p (a b)").rearrange("p (t e c) -> p t e c", t=2, e=N_EXP)
        with ExitStack() as region:
            QKV = sb("QKV", [P, 24, T2], where=region)
            NB = sb("NB", [P, 2, 2, SEQ], where=region)
            QS2 = sb("QS2", [P, 2, T2], where=region)
            SB2 = sb("SB2", [P, 4, T2], where=region)
            PT2 = sb("PT2", [P, 2, T2], where=region)
            OS2 = sb("OS2", [P, 4, P], where=region)
        with ExitStack() as region:
            SG = sb("SG", [P, 16, L1], where=region)
            HPAD = sb("HPAD", [P, KCV, TAPS - 1 + L1], where=region)
            CONV = sb("CONV", [P, KCV, L1], where=region)
            QS1 = sb("QS1", [P, 2, L1], where=region)
            VS1 = sb("VS1", [P, 3 * P], where=region)
            SB1 = sb("SB1", [P, 4, L1], where=region)
            PT1 = sb("PT1", [P, 2, 3 * P], where=region)
            OS1 = sb("OS1", [P, 3, P], where=region)
            OHT = sb("OHT", [NBUCK + 1, 2 * BW], where=region)
            BROW = sb("BROW", [8, 2 * BW], where=region)
            RB = sb("RB", [NBUCK + 1, 8], where=region)
            with ExitStack() as sub:
                Q1 = sb("Q1", [P, 6, L1], where=sub)
                B1 = [sb(f"B1_{q}", [P, 8, n], where=sub) for q, n in enumerate((NMETA, NMETA + P, L1))]
            with ExitStack() as sub:
                MIXH = sb("MIXH", [P, KC, L1], F32R, sub)
                MIXL = sb("MIXL", [P, KC, L1], F32R, sub)
        PS = [ctx.enter_context(nc.psum_tensor(f"PS{b}", [P, 512], F32)) for b in range(8)]
        bias_rows = nc.dram_tensor("bias_rows", (8, 2, P, BW), F32, kind="Internal").ap()
        rpb_rows = nc.dram_tensor("rpb_rows", (64, RPB_LEN), F32, kind="Internal").ap()
        mod_rows = nc.dram_tensor("mod_rows", (4, MOD_STEPS, 256), F32, kind="Internal").ap()
        na_bias = nc.dram_tensor("na_bias", (8, 2, 64, 2, 2, SEQ), F32, kind="Internal").ap()

        IDENT = CST[:, C_ID:C_ID + P]

        s_const = sem("s_const")
        s_x = sem("s_x")
        s_raw = [sem(f"s_raw{r}") for r in range(RAW_SLOTS)]
        s_hi = sem("s_hi")
        s_lo = sem("s_lo")
        s_pc = sem("s_pc")
        s_mr = [sem(f"s_mr{b}") for b in range(2)]
        s_mrl = sem("s_mrl")
        s_mrt = sem("s_mrt")
        s_eva = sem("s_eva")
        s_evd = sem("s_evd")
        s_ms = sem("s_ms")
        s_uh = sem("s_uh")
        s_ul = sem("s_ul")
        s_um = sem("s_um")
        s_hs = sem("s_hs")
        s_hid = sem("s_hid")
        s_hidl = sem("s_hidl")
        s_sil = sem("s_sil")
        s_mean = sem("s_mean")
        s_xc = sem("s_xc")
        s_sq = sem("s_sq")
        s_sqf = sem("s_sqf")
        s_std = sem("s_std")
        s_nrm = sem("s_nrm")
        s_ln = sem("s_ln")
        s_dve = sem("s_dve")
        s_sc = sem("s_sc")
        s_sb = sem("s_sb")
        s_ex = sem("s_ex")
        s_tp = sem("s_tp")
        s_pt = sem("s_pt")
        s_pv = sem("s_pv")
        s_o = sem("s_o")
        s_ot = sem("s_ot")
        s_ath = sem("s_ath")
        s_atl = sem("s_atl")
        s_zero = sem("s_zero")
        s_stq = sem("s_stq")
        s_vt = sem("s_vt")
        s_vs = sem("s_vs")
        s_nbd = [sem(f"s_nbd{h}") for h in range(2)]
        s_nb = sem("s_nb")
        s_rpb = sem("s_rpb")
        s_nas = sem("s_nas")
        s_brow = sem("s_brow")
        s_browd = sem("s_browd")
        s_b1 = sem("s_b1")
        s_cv = sem("s_cv")
        s_pcv = sem("s_pcv")
        s_mix = sem("s_mix")
        s_mixh = sem("s_mixh")
        s_mixl = sem("s_mixl")
        s_rt = sem("s_rt")
        s_gate = sem("s_gate")
        s_gexp = sem("s_gexp")
        s_cbp = sem("s_cbp")
        s_cb = sem("s_cb")
        s_silc = sem("s_silc")
        s_mod = sem("s_mod")
        s_rsw = sem("s_rsw")
        s_rope = sem("s_rope")
        s_out = sem("s_out")

        block = ctx.enter_context(nc.Block())

        U_BEFORE = ["win0", "ffn", "win1", "moe", "fa0", "naqkv", "fb0", "fa1", "waqkv", "fb1"]
        U_IDX = {n: k for k, n in enumerate(U_BEFORE)}
        S_BEFORE = ["ffn", "moe", "fa0", "naqkv", "fb0", "fa1", "waqkv", "fb1"]
        S_IDX = {n: k for k, n in enumerate(S_BEFORE)}
        LNS = ["emb", "cv0", "a0", "b0", "cv1", "a1", "b1", "2a0", "2n0", "2b0", "2a1", "2n1", "2b1"]
        LN_IDX = {n: k for k, n in enumerate(LNS)}
        LN_BASE, base = {}, 0
        for n in LNS:
            LN_BASE[n] = base
            base += KCV if n.startswith("cv") else KC
        UM_IDX = {n: k for k, n in enumerate(["fa0", "naqkv", "fb0", "fa1", "waqkv", "fb1"])}
        SIL_BASE, base = {}, 0
        for n in ("win0", "ffn", "win1", "moe", "fa0", "fb0", "fa1", "fb1"):
            SIL_BASE[n] = base
            base += KCV if n.startswith("win") else KH * ph[n].n_iter
        HID_BASE, base = {}, 0
        for n in ("ffn", "moe", "fa0", "fb0", "fa1", "fb1"):
            HID_BASE[n] = base
            base += KH * ph[n].n_iter

        def iterate(eng, p, body):
            if p.last:
                for i in range(p.n_iter):
                    body(i)
            else:
                with eng.Fori(0, p.n_iter) as i:
                    body(i)

        def pairs_of_heads(eng, a, count):
            if a.name == "b0":
                return [nullcontext(i) for i in range(count)]
            return [eng.Fori(0, count)]

        class Att:
            pass

        atts = {}
        unit = kvn = its = 0
        for name, nq, groups, inner, values in (
                ("b0", 3, 1, 4, 1), ("b1", 2, 1, 4, 1), ("na", 4, 1, 8, 8), ("wa", 2, 2, 4, 2)):
            a = atts[name] = Att()
            a.name, a.groups, a.inner, a.values = name, groups, inner, values
            a.units = 2 * nq
            a.unit0, a.it0, a.kv0 = unit, its, kvn
            unit += a.units * groups * inner
            its += groups * inner
            kvn += values
            if name[0] == "b":
                a.layer = int(name[1])
                a.qts = [(0, NMETA), (NMETA, P), (NMETA + P, P)][-nq:]
                a.keys = [(0, NMETA), (0, NMETA + P), (0, L1)][-nq:]
                a.vt = [(0, NMETA), (NMETA, P), (NMETA + P, P)]
                a.qs, a.sbf, a.pt, a.os = QS1, SB1, PT1, OS1
                a.vsrc, a.vdst = [Q1[:, 5, :]], [VS1[:, :]]
                a.keysof = lambda it, grp, c0, n: Q1[:, 4, c0:c0 + n]
                a.valuesof = lambda it, grp, nt, col: VS1[0:nt, col:col + HD]
                a.u0 = 0
            else:
                a.layer = 0 if name == "na" else 1
                a.qts = [(0, P), (P, P), (2 * P, P), (3 * P, P)][:nq]
                a.keys = [(0, T2), (0, T2), (SEQ, CTX), (SEQ, CTX)][:nq]
                a.vt = [(j * P, P) for j in range(4)]
                a.qs, a.sbf, a.pt, a.os = QS2, SB2, PT2, OS2
                first_v = 16 if name == "na" else 10
                a.vsrc = a.vdst = [QKV[:, first_v + v, :] for v in range(values)]
                if name == "na":
                    a.keysof = lambda it, grp, c0, n: QKV[:, bass.ds(8 + it, 1), c0:c0 + n].rearrange("p a t -> p (a t)")
                    a.valuesof = lambda it, grp, nt, col: QKV[0:nt, bass.ds(16 + it, 1), col:col + HD]\
                        .rearrange("p a t -> p (a t)")
                else:
                    a.keysof = lambda it, grp, c0, n: QKV[:, 8 + grp, c0:c0 + n]
                    a.valuesof = lambda it, grp, nt, col: QKV[0:nt, 10 + grp, col:col + HD]
                a.u0 = NMETA
            a.sink = name != "na"
            a.lo = a.qts[0][0]
            a.hi = a.qts[-1][0] + a.qts[-1][1]

        def bounds(p, s, h):
            if p.cols[s] == W_STEP:
                return h * PIECE_W, (h + 1) * PIECE_W
            return (0, DOWN_CUT * P) if h == 0 else (DOWN_CUT * P, D_EXP)

        def multiplied(eng, p, i, s):
            eng.wait_ge(s_pc, p.piece(i, s, PIECES - 1) + 1)

        def unit_of(a, u):
            half, qt = divmod(u, len(a.qts))
            k0, nk = a.keys[qt]
            tiles = [j for j, (c, n) in enumerate(a.vt) if c >= k0 and c + n <= k0 + nk]
            return half, qt, k0, nk, tiles

        def freed(a, it, u, ring):
            base = a.unit0 + it * a.units
            if u >= ring:
                return base + u - ring + 1
            return base - a.units + max(v for v in range(a.units) if v % ring == u) + 1

        def later_unit(a, it, u, more):
            if u < a.units:
                return it, u
            return (it + 1, u - a.units) if more else None

        def reach(eng, sm, value):
            if not (isinstance(value, int) and value <= 0):
                eng.wait_ge(sm, value)

        def vec(col, n=1):
            return VEC[:, col:col + n]

        def mod(layer, idx, c, s):
            t = layer * 72 + idx * KC + c
            return MOD[:, s, t // 2, t % 2:t % 2 + 1]

        STREAM = [(NMETA, SEQ), (L1, CTX)]

        @block.sync
        def _(sp):
            def load(p, i, s, src):
                if not (p.prev is None and s < RAW_SLOTS):
                    sp.wait_ge(s_lo, p.raw_user(i, s))
                sp.dma_start(RAW[:, s % RAW_SLOTS, 0:p.cols[s]], src).then_inc(s_raw[s % RAW_SLOTS], 16)

            def straight(name, w, k0=0):
                p = ph[name]
                for s in range(p.n):
                    load(p, 0, s, w[k0 + s])

            def experts(name, e0, with_mod=False):
                p = ph[name]

                def body(i):
                    s = 0
                    for k in range(KH):
                        load(p, i, s, ins["w_gu"][i + e0, k])
                        s += 1
                        if with_mod and k < MOD_PER_EXPERT:
                            load(p, i, s, ins["w_mod"][i * MOD_PER_EXPERT + k])
                            s += 1
                    for m in range(KC):
                        load(p, i, s, ins["w_dn"][i + e0, m])
                        s += 1

                iterate(sp, p, body)

            def bias_tiles(layer):
                if layer == 0:
                    sp.wait_ge(s_brow, 4)
                    for v in range(2):
                        row = BROW[:, v * BW:(v + 1) * BW].rearrange("h (a w) -> h a w", a=1)
                        sp.dma_start(bias_rows[:, v], row.to_broadcast([8, P, BW])).then_inc(s_browd, 16)
                    sp.wait_ge(s_browd, 32)
                else:
                    sp.wait_ge(s_pc, ph["win1"].p0)
                for q, (q0, nq) in enumerate(((0, NMETA), (NMETA, P), (NMETA + P, P))):
                    nk = q0 + nq
                    pieces = [(0, 0, NMETA)] + ([(1, NMETA, nk - NMETA)] if q else [])
                    for v, k0, n in pieces:
                        src = bass.AP(tensor=bias_rows.tensor, offset=v * P * BW + L1 - q0 + k0,
                                      ap=[[BW - 1, nq], [2 * P * BW, 8], [1, n]])
                        sp.dma_start(B1[q][0:nq, :, k0:k0 + n], src).then_inc(s_b1, 16)

            for i in range(DEPTH):
                if i == 0:
                    for s in range(3):
                        load(ph["win0"], 0, s, ins["w_in"][0, s])
                    bias_tiles(0)
                    for s in range(3, 15):
                        load(ph["win0"], 0, s, ins["w_in"][0, s])
                else:
                    straight(f"win{i}", ins["w_in"][i])
                    bias_tiles(1)
                straight(f"proj{i}", ins["w_proj"][i])
                straight(f"wout{i}", ins["w_out"][i])
                if i == 0:
                    experts("ffn", 0)
                else:
                    experts("moe", 2, True)
            for i in range(DEPTH):
                experts(f"fa{i}", 2 + N_EXP + 4 * i)
                if i == 0:
                    p = ph["naqkv"]
                    with sp.Fori(0, p.n_iter) as it:
                        for s in range(4):
                            load(p, it, s, ins["w_na"][it * 4 + s])
                else:
                    straight("waqkv", ins["w_wa"])
                straight(f"wo{i}", ins["w_o"][i])
                if i == 0:
                    a = atts["na"]
                    sp.wait_ge(s_nas, 16 * 64)
                    sp.wait_ge(s_pc, ph["naqkv"].p0)
                    with sp.Fori(0, a.inner) as it:
                        for half in range(2):
                            sp.wait_ge(s_sb, a.unit0 + it * a.units - a.units + half * len(a.qts) + 2)
                            sp.dma_start(NB[:, :, half, :], na_bias[it][:, :, :, half, :].rearrange("r q a k -> (r q) a k"))\
                                .then_inc(s_nbd[half], 16)
                experts(f"fb{i}", 2 + N_EXP + 4 * i + 2)
            sp.wait_ge(s_ln, LN_BASE["2b1"] + KC)
            sp.dma_start(out, H[:, :, NMETA:L1]).then_inc(s_out, 16)
            sp.wait_ge(s_out, 16)

        @block.gpsimd
        def _(pool):
            pool.memset(ONES[:, :], 1.0 / D).then_inc(s_ms, 1)
            pool.memset(ONESC[:, :], 1.0 / CONVC).then_inc(s_ms, 1)
            pool.memset(EPST[:, :], EPS).then_inc(s_ms, 1)
            pool.dma_start(rpb_rows, ins["na_rpb"].to_broadcast([64, RPB_LEN])).then_inc(s_rpb, 16)
            pool.wait_ge(s_rpb, 16)
            for qr in range(4):
                for h in range(16):
                    src = bass.AP(tensor=rpb_rows.tensor,
                                  offset=h * RPB_R * RPB_C + (7 - qr) * RPB_C + 15,
                                  ap=[[RPB_LEN - 1, 64], [RPB_C, 4], [1, 64]])
                    dst = na_bias[h // 2, qr % 2, :, qr // 2, h % 2, :].rearrange("q (r k) -> q r k", r=4)
                    pool.dma_start(dst, src).then_inc(s_nas, 16)

            def stage_queries(a, it, half, src, c0, n):
                reach(pool, s_sc, a.unit0 + it * a.units - (0 if half else a.units // 2))
                r = slice(HD * half, HD * half + HD)
                pool.tensor_copy(a.qs[r, half, 0:n], src[r, bass.ds(it, 1), c0:c0 + n]
                                 .rearrange("p a t -> p (a t)")).then_inc(s_stq, 1)

            def conv(layer, c0, n):
                pool.wait_ge(s_evd, ph[f"win{layer}"].evacs("d", 0, 7))
                c = KCV - 1
                steps0 = layer * POOL_STEPS
                y = CONV[:, c, c0:c0 + n]

                def product(w):
                    pool.tensor_scalar(PT1[:, w % 2, 0:n], HPAD[:, c, c0 + w:c0 + w + n],
                                       vec(V_DW + (layer * KCV + c) * TAPS + w), None, ALU.mult).then_inc(s_pcv, 1)

                pool.tensor_scalar(y, HPAD[:, c, c0:c0 + n], vec(V_DW + (layer * KCV + c) * TAPS),
                                   vec(V_CB + 4 * layer + c), ALU.mult, ALU.add).then_inc(s_pcv, 1)
                product(1)
                for w in range(1, TAPS):
                    pool.wait_ge(s_pcv, steps0 + 2 * w)
                    pool.tensor_tensor(y, y, PT1[:, w % 2, 0:n], ALU.add).then_inc(s_pcv, 1)
                    if w + 1 < TAPS:
                        product(w + 1)

            for i in range(DEPTH):
                if i == 1:
                    pool.wait_ge(s_pc, ph["win1"].p0)
                    pool.wait_ge(s_stq, 2 * atts["b1"].it0)
                pool.memset(HPAD[:, :, 0:TAPS - 1], 0.0).then_inc(s_ms, 1)
                a = atts[f"b{i}"]
                pool.memset(QS1[:, :, :], 0.0).then_inc(s_zero, 1)
                pool.wait_ge(s_eva, ph[f"win{i}"].evacs("a", 0, 3))
                pool.wait_ge(s_zero, i + 1)
                c0, n = (0, L1) if i == 0 else (NMETA, SEQ)
                pool.wait_ge(s_ms, 4 + i)
                conv(i, c0, n)
                pool.wait_ge(s_pcv, (i + 1) * POOL_STEPS)
                for loop in pairs_of_heads(pool, a, a.inner):
                    with loop as it:
                        for half in range(2):
                            stage_queries(a, it, half, Q1, 0, L1)

            def modulate(name, ln, layer, idx, n):
                for c in range(KC):
                    pool.wait_ge(s_ln, LN_BASE[ln] + c + 1)
                    if c >= 4:
                        pool.wait_ge(s_ul, KC * U_IDX[name] + c - 3)
                    for st, (t0, nt) in enumerate(STREAM):
                        if t0 < NMETA + n:
                            last = pool.tensor_scalar(TMP[:, c % 4, t0 - NMETA:t0 - NMETA + nt], H[:, c, t0:t0 + nt],
                                                      mod(layer, idx + 1, c, st), mod(layer, idx, c, st), ALU.mult, ALU.add)
                    last.then_inc(s_um, 1)

            pool.wait_ge(s_stq, 2 * atts["na"].it0)
            pool.wait_ge(s_mod, 10)
            modulate("fa0", "b1", 0, 0, T2)
            modulate("naqkv", "2a0", 0, 3, T2)
            a = atts["na"]
            pool.wait_ge(s_um, KC * UM_IDX["fb0"])
            pool.wait_ge(s_evd, ph["naqkv"].d0)
            pool.wait_ge(s_stq, 2 * a.it0)
            pool.memset(QS2[:, :, :], 0.0).then_inc(s_zero, 1)
            pool.wait_ge(s_eva, ph["naqkv"].evacs("a", 3, 0))
            pool.wait_ge(s_zero, 3)
            with pool.Fori(0, a.inner) as it:
                for half in range(2):
                    pool.wait_ge(s_nbd[half], (it + 1) * 16)
                    pool.wait_ge(s_stq, 2 * (a.it0 + it) + half)
                    mask = CST[:, C_NAM:C_NAM + 64].rearrange("p (a k) -> p a k", a=1).to_broadcast([P, 4, 64])
                    for qt in range(2):
                        nbv = NB[:, qt, half, :].rearrange("p (r k) -> p r k", r=4)
                        last = pool.tensor_tensor(nbv, nbv, mask, ALU.add)
                    last.then_inc(s_nb, 1)
                    pool.wait_ge(s_nb, 2 * it + half + 1)
                    stage_queries(a, it, half, QKV, 0, T2)
            pool.wait_ge(s_stq, 2 * atts["wa"].it0)
            modulate("fb0", "2n0", 0, 6, T2)
            modulate("fa1", "2b0", 1, 0, T2)
            modulate("waqkv", "2a1", 1, 3, T2)
            a = atts["wa"]
            pool.wait_ge(s_um, KC * UM_IDX["fb1"])
            pool.wait_ge(s_evd, ph["waqkv"].d0)
            pool.wait_ge(s_stq, 2 * a.it0)
            pool.memset(QS2[:, :, :], 0.0).then_inc(s_zero, 1)
            pool.wait_ge(s_rope, 10)
            pool.wait_ge(s_zero, 4)
            for grp in range(a.groups):
                with pool.Fori(0, a.inner) as i:
                    for half in range(2):
                        stage_queries(a, i + grp * a.inner, half, QKV, 0, SEQ)
            pool.wait_ge(s_stq, 2 * (a.it0 + a.groups * a.inner))
            modulate("fb1", "2n1", 1, 6, SEQ)

        @block.tensor
        def _(pe):
            def piece_product(p, i, s, h, groups, arrives=None):
                pe.wait_ge(s_lo, p.piece(i, s, h) + 1)
                slot = p.piece_slot(s, h)
                order = [(g, x) for g in range(len(groups)) for x in range(len(groups[g][1]))]
                if arrives:
                    order.sort(key=lambda gx: gx[1])
                for g, x in order:
                    ps, terms, opens, closes = groups[g]
                    if arrives and g == 0:
                        pe.wait_ge(arrives[0], arrives[1][x])
                    col, mh, ml = terms[x]
                    wh, wl = WH[slot][:, col:col + P], WL[slot][:, col:col + P]
                    pe.matmul(ps, wh, mh, start=opens and x == 0, stop=False)
                    pe.matmul(ps, wh, ml, start=False, stop=False)
                    last = pe.matmul(ps, wl, mh, start=False, stop=closes and x == len(terms) - 1)
                last.then_inc(s_pc, 1)

            def begin(p, i, s):
                if s >= BANK_SETS or p.n_iter > 1:
                    kind, count = p.bank_user(i, s)
                    pe.wait_ge(s_evd if kind == "d" else s_eva, count)

            def all_evacuated(p):
                if p.a0:
                    pe.wait_ge(s_eva, p.a0)
                if p.d0:
                    pe.wait_ge(s_evd, p.d0)

            def pair_step(p, i, s, xh, xl, u=None):
                begin(p, i, s)
                for h in range(PIECES):
                    groups = []
                    for j in range(2):
                        ps = PS[2 * (s % BANK_SETS) + j][:, 0:xh(0).shape[1]]
                        groups.append((ps, [(x * 256 + j * P, xh(4 * h + x), xl(4 * h + x)) for x in range(4)],
                                       h == 0, h == 1))
                    piece_product(p, i, s, h, groups, None if u is None else (s_ul, [KC * u + 4 * h + x + 1 for x in range(4)]))

            def mod_step(p, i, s):
                begin(p, i, s)
                for h in range(PIECES):
                    pe.wait_ge(s_lo, p.piece(i, s, h) + 1)
                    slot = p.piece_slot(s, h)
                    for x in range(4):
                        for w in (WH, WL):
                            last = pe.matmul(PS[2 * (s % BANK_SETS)][:, 0:256], SC4[:, 4 * h + x, :, :].rearrange("p a b -> p (a b)"),
                                             w[slot][:, x * 256:(x + 1) * 256], start=(h == 0 and x == 0 and w is WH),
                                             stop=(h == 1 and x == 3 and w is WL))
                    last.then_inc(s_pc, 1)

            def chunks(t, c0, n):
                return lambda k: t[:, k, c0:c0 + n]

            def experts(name, c0, n):
                p = ph[name]
                all_evacuated(p)

                def body(i):
                    s = 0
                    for k in range(KH):
                        pair_step(p, i, s, chunks(UH, c0, n), chunks(UL, c0, n), U_IDX[name] if k == 0 else None)
                        s += 1
                        if p.kinds[s] == "a":
                            mod_step(p, i, s)
                            s += 1
                    for m in range(KC):
                        begin(p, i, s)
                        for h, ks in enumerate((range(DOWN_CUT), range(DOWN_CUT, KH))):
                            terms = [((k - ks[0]) * P, HIDH[:, k, 0:n], HIDL[:, k, 0:n]) for k in ks]
                            made = (s_hidl, [HID_BASE[name] + k + 1 + i * KH for k in ks]) if m == 0 else None
                            piece_product(p, i, s, h, [(PS[2 * (s % BANK_SETS)][:, 0:n], terms, h == 0, h == 1)], made)
                        s += 1

                iterate(pe, p, body)

            def straight(name, c0, n, u=True, ranges=None, xh=UH, xl=UL):
                p = ph[name]
                all_evacuated(p)
                for s in range(p.n):
                    cc, nn = ranges[s] if ranges else (c0, n)
                    pair_step(p, 0, s, chunks(xh, cc, nn), chunks(xl, cc, nn), U_IDX[name] if u and s == 0 else None)

            def norm(name, src, ones, c0, n, sm, there):
                b0, cs = LN_BASE[name], (KCV if name.startswith("cv") else KC)
                for c in range(cs):
                    pe.wait_ge(sm, there(c))
                    last = pe.matmul(PS[0][:, 0:n], ones[:, :], src[:, c, c0:c0 + n], start=(c == 0), stop=(c == cs - 1))
                last.then_inc(s_mean, 1)
                for c in range(cs):
                    pe.wait_ge(s_sq, b0 + c + 1)
                    last = pe.matmul(PS[1][:, 0:n], ones[:, :], TMP[:, c % 4, 0:n], start=(c == 0), stop=(c == cs - 1))
                    last.then_inc(s_sqf, 1)

            def attention(name):
                a = atts[name]

                def values():
                    for v, src in enumerate(a.vsrc):
                        if v >= 2:
                            pe.wait_ge(s_vs, a.kv0 + v - 1)
                        for j, (c, nt) in enumerate(a.vt):
                            last = pe.transpose(PS[3 + v % 2][0:nt, j * P:(j + 1) * P], src[:, c:c + nt], IDENT)
                        last.then_inc(s_vt, 1)

                def scores(it, u, grp):
                    half, qt, k0, nk, _ = unit_of(a, u)
                    q0, nq = a.qts[qt]
                    if qt == 0:
                        pe.wait_ge(s_stq, 2 * (a.it0 + it) + half + 1)
                    reach(pe, s_ex, freed(a, it, u, 3))
                    pe.matmul(PS[u % 3][0:nq, 0:nk], a.qs[:, half, q0:q0 + nq], a.keysof(it, grp, k0, nk),
                              start=True, stop=True).then_inc(s_sc, 1)

                def turn(it, u):
                    half, qt, k0, nk, tiles = unit_of(a, u)
                    nq = a.qts[qt][1]
                    pe.wait_ge(s_ex, a.unit0 + it * a.units + u + 1)
                    reach(pe, s_pt, freed(a, it, u, 2))
                    for x, j in enumerate(tiles):
                        c, nt = a.vt[j]
                        last = pe.transpose(PS[3 + u % 2][0:nt, x * P:x * P + nq],
                                            a.sbf[0:nq, u % 4, c - k0:c - k0 + nt], IDENT[0:nq, 0:nq])
                    last.then_inc(s_tp, 1)

                def times_values(it, u, grp):
                    half, qt, k0, nk, tiles = unit_of(a, u)
                    nq = a.qts[qt][1]
                    reach(pe, s_o, freed(a, it, u, 2))
                    pe.wait_ge(s_pt, a.unit0 + it * a.units + u + 1)
                    for x, j in enumerate(tiles):
                        nt = a.vt[j][1]
                        last = pe.matmul(PS[5 + u % 2][0:nq, 0:HD], a.pt[0:nt, u % 2, x * P:x * P + nq],
                                         a.valuesof(it, grp, nt, j * P + HD * half),
                                         start=(x == 0), stop=(x == len(tiles) - 1))
                    last.then_inc(s_pv, 1)

                def pair(i, grp, more):
                    it = i + grp * a.inner
                    for u in range(a.units):
                        if u:
                            turn(it, u)
                        later = later_unit(a, it, u + 3, more)
                        if later:
                            scores(*later, grp)
                        times_values(it, u, grp)
                    if more:
                        turn(it + 1, 0)
                    pe.wait_ge(s_o, a.unit0 + it * a.units + a.units)
                    reach(pe, s_atl, a.it0 + it)
                    for q, (q0, nq) in enumerate(a.qts):
                        last = pe.transpose(PS[7][:, q0:q0 + nq], a.os[0:nq, q, :], IDENT[0:nq, 0:nq])
                    last.then_inc(s_ot, 1)

                values()
                pe.wait_ge(s_vs, a.kv0 + a.values)
                for grp in range(a.groups):
                    for u in range(3):
                        scores(grp * a.inner, u, grp)
                    turn(grp * a.inner, 0)
                    for loop in pairs_of_heads(pe, a, a.inner - 1):
                        with loop as i:
                            pair(i, grp, True)
                    pair(a.inner - 1, grp, False)

            pe.wait_ge(s_ms, 3)
            pe.wait_ge(s_const, 16 * 10)
            pe.matmul(PS[0][0:8, 0:BW], RB[:, :], OHT[:, 0:BW], start=True, stop=True).then_inc(s_brow, 1)
            pe.matmul(PS[1][0:8, 0:BW], RB[:, :], OHT[:, BW:2 * BW], start=True, stop=True).then_inc(s_brow, 1)
            pe.wait_ge(s_brow, 4)
            norm("emb", H, ONES, 0, L1, s_x, lambda c: 32)
            for i in range(DEPTH):
                c0, n = (0, L1) if i == 0 else (NMETA, SEQ)
                straight(f"win{i}", 0, L1)
                pe.wait_ge(s_eva, ph[f"win{i}"].evacs("a", 0, 15))
                attention(f"b{i}")
                pe.wait_ge(s_pcv, (i + 1) * POOL_STEPS)
                norm(f"cv{i}", CONV, ONESC, c0, n, s_cv, lambda c: DVE_CONV * (i + 1))
                p = ph[f"proj{i}"]
                all_evacuated(p)
                pe.wait_ge(s_atl, atts[f"b{i}"].it0 + 4)
                pe.wait_ge(s_ul, KC * (U_IDX["win0" if i == 0 else "win1"] + 1))
                pe.wait_ge(s_mixl, (KCV + KC) * i + KCV)
                for s in range(p.n):
                    if s >= 2:
                        pe.wait_ge(s_evd, p.evacs("d", 0, s - 1))
                    for b in range(2):
                        groups = [(PS[4 * (s % 2) + 2 * m + b][:, 0:n],
                                   [(k * 256 + m * P, UH[:, 4 * b + k, c0:c0 + n], UL[:, 4 * b + k, c0:c0 + n])
                                    for k in range(KCV)], True, True) for m in range(2)]
                        piece_product(p, 0, s, b, groups)
                p = ph[f"wout{i}"]
                pe.wait_ge(s_mixl, (KCV + KC) * (i + 1))
                straight(f"wout{i}", c0, n, False, None, MIXH, MIXL)
                norm(f"a{i}", H, ONES, c0, n, s_evd, lambda c: ph[f"wout{i}"].evacs("d", 0, c // 2 + 1))
                if i == 1:
                    pe.wait_ge(s_ln, LN_BASE["a1"] + KC)
                    for t in range(2):
                        for k in range(KC):
                            last = pe.matmul(PS[2][:, 8 * t:8 * t + 8], H[:, k, NMETA + t * P:NMETA + (t + 1) * P],
                                             RT[:, k, :], start=(k == 0), stop=(k == KC - 1))
                    last.then_inc(s_rt, 1)
                    pe.wait_ge(s_gate, 2)
                    for t in range(2):
                        for e in range(N_EXP):
                            last = pe.matmul(PS[4 + e // 2][:, (e % 2) * SEQ + t * P:(e % 2) * SEQ + (t + 1) * P],
                                             CBB[:, t, e, :], IDENT, start=True, stop=True)
                    last.then_inc(s_cbp, 1)
                    pe.wait_ge(s_cb, 4)
                    pe.wait_ge(s_silc, 3)
                experts("moe" if i else "ffn", c0, n)
                nm = "moe" if i else "ffn"
                if i == 1:
                    pe.wait_ge(s_mrl, 16)
                    pe.wait_ge(s_evd, ph["fa0"].d0)
                    for j in range(2):
                        for r in range(4):
                            last = pe.transpose(PS[3 + j][:, r * MOD_STEPS:(r + 1) * MOD_STEPS],
                                                MLD[:, r, j * P:(j + 1) * P], IDENT[0:MOD_STEPS, 0:MOD_STEPS])
                    last.then_inc(s_mrt, 1)
                norm(f"b{i}", H, ONES, c0, n, s_evd, lambda c: ph[nm].evacs("d", ph[nm].n_iter, 0) - KC + c + 1)
            for i in range(DEPTH):
                nb = T2 if i == 0 else SEQ
                experts(f"fa{i}", NMETA, T2)
                norm(f"2a{i}", H, ONES, NMETA, T2, s_evd, lambda c: ph[f"fa{i}"].evacs("d", 2, 0) - KC + c + 1)
                if i == 0:
                    p = ph["naqkv"]
                    all_evacuated(p)
                    with pe.Fori(0, p.n_iter) as it:
                        for s in range(4):
                            pair_step(p, it, s, chunks(UH, NMETA, T2), chunks(UL, NMETA, T2), U_IDX["naqkv"] if s == 0 else None)
                    pe.wait_ge(s_eva, p.evacs("a", 3, 0))
                    attention("na")
                else:
                    p = ph["waqkv"]
                    straight("waqkv", 0, 0, True, [(NMETA, SEQ)] * 4 + [(NMETA, T2)] * 2)
                    pe.wait_ge(s_eva, p.evacs("a", 0, 6))
                    for c in range(10):
                        if c >= 2:
                            pe.wait_ge(s_rope, c - 1)
                        pe.matmul(PS[c % 2][:, 0:SEQ], CST[:, C_PERM:C_PERM + P], QKV[:, c, 0:SEQ],
                                  start=True, stop=True).then_inc(s_rsw, 1)
                    pe.wait_ge(s_rope, 10)
                    attention("wa")
                pe.wait_ge(s_atl, atts["na" if i == 0 else "wa"].it0 + 8)
                straight(f"wo{i}", NMETA, nb, False)
                norm(f"2n{i}", H, ONES, NMETA, nb, s_evd, lambda c: ph[f"wo{i}"].evacs("d", 0, c // 2 + 1))
                experts(f"fb{i}", NMETA, nb)
                norm(f"2b{i}", H, ONES, NMETA, nb, s_evd, lambda c: ph[f"fb{i}"].evacs("d", 2, 0) - KC + c + 1)

        @block.scalar
        def _(act):
            for dst, src in ((CST[:, :], ins["consts"]), (VEC[:, :], ins["vectors"]), (OHT[:, :], ins["onehot"]),
                             (RB[0:NBUCK, :], ins["rel_bias"]), (RB[NBUCK:NBUCK + 1, :], ins["neg_row"]),
                             (RT[:, :, :], ins["router"]), (CC[:, :, :], ins["cond"])):
                act.dma_start(dst, src).then_inc(s_const, 16)
            for l in range(2):
                act.dma_start(SK1[:, l, :], ins["sinks"][l:l + 1, :].to_broadcast([P, 8])).then_inc(s_const, 16)
            act.dma_start(SK2[:, :], ins["sinks_2"].to_broadcast([P, 16])).then_inc(s_const, 16)
            act.dma_start(H[:, :, 0:L1], ins["tokens"]).then_inc(s_x, 16)
            act.dma_start(H[:, :, L1:TALL], ins["ctx"]).then_inc(s_x, 16)

            def high(p, i, s, h):
                if h == 0:
                    act.wait_ge(s_raw[s % RAW_SLOTS], p.loads(i, s) * 16)
                lo, hi = bounds(p, s, h)
                slot = p.piece_slot(s, h)
                if not (p.prev is None and s < 2):
                    act.wait_ge(s_pc, p.piece_user(i, s, h))
                act.activation(WH[slot][:, 0:hi - lo], RAW[:, s % RAW_SLOTS, lo:hi], ACT.Copy).then_inc(s_hi, 1)

            def ahead(p, i, s, pieces=range(PIECES)):
                later = p.step_ahead(i, s)
                for h in pieces if later else ():
                    high(*later, h)

            def norm(name, src, dst, gcol, c0, n, func=ACT.Identity, u=None):
                b0, cs = LN_BASE[name], (KCV if name.startswith("cv") else KC)
                for c in range(cs):
                    act.wait_ge(s_xc, b0 + c + 1)
                    if b0 + c >= 4:
                        act.wait_ge(s_sqf, b0 + c - 3)
                    act.activation(TMP[:, c % 4, 0:n], src[:, c, c0:c0 + n], ACT.Square).then_inc(s_sq, 1)
                act.wait_ge(s_sqf, b0 + cs)
                act.activation(STD[:, 0:n], PS[1][:, 0:n], ACT.Sqrt, bias=EPST[:, 0:1]).then_inc(s_std, 1)
                lag, make = u or (0, None)
                for c in range(cs + lag):
                    if c < cs:
                        act.wait_ge(s_nrm, b0 + c + 1)
                        act.activation(dst[:, c, c0:c0 + n], src[:, c, c0:c0 + n], func,
                                       bias=vec(gcol + cs + c), scale=vec(gcol + c)).then_inc(s_ln, 1)
                    if c >= lag and make:
                        make(c - lag)

            def plain_u(name, c0, n, ln):
                def make(c):
                    act.wait_ge(s_ln, LN_BASE[ln] + c + 1)
                    act.activation(UH[:, c, c0:c0 + n], H[:, c, c0:c0 + n], ACT.Copy).then_inc(s_uh, 1)
                return 1, make

            def modulated_u(name, c0, n):
                def make(c):
                    act.wait_ge(s_um, UM_IDX[name] * KC + c + 1)
                    act.activation(UH[:, c, c0:c0 + n], TMP[:, c % 4, 0:n], ACT.Copy).then_inc(s_uh, 1)
                return 2, make

            def scale_h(name, c0, n):
                act.wait_ge(s_ul, KC * (U_IDX[name] + 1))
                if name == "moe":
                    act.wait_ge(s_rt, 1)
                act.mul(H[:, :, c0:c0 + n], H[:, :, c0:c0 + n], ALPHA).then_inc(s_hs, 1)

            def experts(name, n):
                p = ph[name]

                def body(i):
                    s = 0
                    for k in range(KH):
                        ahead(p, i, s, (0,))
                        multiplied(act, p, i, s)
                        if k >= 2:
                            act.wait_ge(s_hidl, HID_BASE[name] + k - 1 + i * KH)
                        act.activation(SIL[:, k % 2, 0:n], PS[2 * (s % BANK_SETS)][:, 0:n], ACT.Silu).then_inc(s_sil, 1)
                        if k < KH - 1:
                            ahead(p, i, s, (1,))
                        act.wait_ge(s_evd, p.evacs("d", i, s + 1))
                        act.activation(HIDH[:, k, 0:n], HT[:, k % 2, 0:n], ACT.Copy).then_inc(s_hid, 1)
                        if k == KH - 1:
                            ahead(p, i, s, (1,))
                        s += 1
                        if p.kinds[s] == "a":
                            ahead(p, i, s, (0,))
                            multiplied(act, p, i, s)
                            uses = len(range(k % 2, MOD_PER_EXPERT, 2))
                            if k >= 2:
                                act.wait_ge(s_mr[k % 2], (i * uses + k // 2) * 16)
                            act.activation(MROW[:, k % 2, :], PS[2 * (s % BANK_SETS)][0:4, 0:256], ACT.Copy).then_inc(s_eva, 1)
                            act.wait_ge(s_eva, p.evacs("a", i, s + 1))
                            act.dma_start(mod_rows[:, i * MOD_PER_EXPERT + k, :], MROW[:, k % 2, :]).then_inc(s_mr[k % 2], 16)
                            ahead(p, i, s, (1,))
                            s += 1
                    for m in range(KC):
                        ahead(p, i, s)
                        s += 1
                    if "a" in p.kinds:
                        for b in range(2):
                            act.wait_ge(s_mr[b], (i + 1) * 16 * len(range(b, MOD_PER_EXPERT, 2)))

                iterate(act, p, body)

            def copy_step(p, i, s, dsts, n, scale=1.0):
                ahead(p, i, s, (0,))
                multiplied(act, p, i, s)
                act.activation(dsts[0], PS[2 * (s % BANK_SETS)][:, 0:n], ACT.Copy, scale=scale)
                act.activation(dsts[1], PS[2 * (s % BANK_SETS) + 1][:, 0:n], ACT.Copy, scale=scale).then_inc(s_eva, 1)
                ahead(p, i, s, (1,))

            def attention(name):
                a = atts[name]

                def exps(it, u):
                    half, qt, k0, nk, _ = unit_of(a, u)
                    nq = a.qts[qt][1]
                    b = u % 4
                    reach(act, s_o, freed(a, it, u, 4))
                    act.wait_ge(s_sb, a.unit0 + it * a.units + u + 1)
                    last = act.activation(a.sbf[0:nq, b, 0:nk], PS[u % 3][0:nq, 0:nk], ACT.Exp, bias=NM[0:nq, b:b + 1],
                                          accum_out=DEN[0:nq, b:b + 1])
                    if a.sink:
                        c = 2 * it + half
                        col = SK1[:, a.layer, bass.ds(c, 1)] if name[0] == "b" else SK2[:, bass.ds(c, 1)]
                        last = act.activation(ESK[0:nq, b:b + 1], col[0:nq, :], ACT.Exp, bias=NM[0:nq, b:b + 1])
                    last.then_inc(s_ex, 1)

                def copy_turned(it, u):
                    half, qt, k0, nk, tiles = unit_of(a, u)
                    nq = a.qts[qt][1]
                    reach(act, s_pv, freed(a, it, u, 2))
                    act.wait_ge(s_tp, a.unit0 + it * a.units + u + 1)
                    if nq == P and all(a.vt[j][1] == P for j in tiles):
                        act.activation(a.pt[:, u % 2, 0:len(tiles) * P], PS[3 + u % 2][:, 0:len(tiles) * P],
                                       ACT.Copy).then_inc(s_pt, 1)
                    else:
                        for x, j in enumerate(tiles):
                            nt = a.vt[j][1]
                            last = act.activation(a.pt[0:nt, u % 2, x * P:x * P + nq],
                                                  PS[3 + u % 2][0:nt, x * P:x * P + nq], ACT.Copy)
                        last.then_inc(s_pt, 1)

                def values():
                    for v, dst in enumerate(a.vdst):
                        act.wait_ge(s_vt, a.kv0 + v + 1)
                        if all(nt == P for _, nt in a.vt):
                            last = act.activation(dst, PS[3 + v % 2][:, :], ACT.Copy)
                        else:
                            for j, (c, nt) in enumerate(a.vt):
                                last = act.activation(dst[0:nt, j * P:(j + 1) * P], PS[3 + v % 2][0:nt, j * P:(j + 1) * P],
                                                      ACT.Copy)
                        last.then_inc(s_vs, 1)

                def pair(i, grp, more):
                    it = i + grp * a.inner
                    for u in range(a.units):
                        if u:
                            copy_turned(it, u)
                        later = later_unit(a, it, u + 2, more)
                        if later:
                            exps(*later)
                    if more:
                        copy_turned(it + 1, 0)
                    act.wait_ge(s_ot, a.it0 + it + 1)
                    act.activation(UH[:, bass.ds(it, 1), a.u0 + a.lo:a.u0 + a.hi].rearrange("p a t -> p (a t)"),
                                   PS[7][:, a.lo:a.hi], ACT.Copy).then_inc(s_ath, 1)

                values()
                for grp in range(a.groups):
                    for u in range(2):
                        exps(grp * a.inner, u)
                    copy_turned(grp * a.inner, 0)
                    for loop in pairs_of_heads(act, a, a.inner - 1):
                        with loop as i:
                            pair(i, grp, True)
                    pair(a.inner - 1, grp, False)

            act.wait_ge(s_const, 16 * 10)
            act.activation(SCF[:, :, :], CC[:, :, :], ACT.Silu).then_inc(s_silc, 1)
            act.wait_ge(s_brow, 2)
            act.activation(BROW[:, 0:BW], PS[0][0:8, 0:BW], ACT.Copy).then_inc(s_brow, 1)
            act.activation(BROW[:, BW:2 * BW], PS[1][0:8, 0:BW], ACT.Copy).then_inc(s_brow, 1)
            for s in range(AHEAD):
                for h in range(PIECES):
                    high(ph["win0"], 0, s, h)
            norm("emb", H, H, V_EMB, 0, L1, u=plain_u("win0", 0, L1, "emb"))
            for i in range(DEPTH):
                c0, n = (0, L1) if i == 0 else (NMETA, SEQ)
                p = ph[f"win{i}"]
                for s in range(3):
                    copy_step(p, 0, s, (Q1[:, 2 * s, :], Q1[:, 2 * s + 1, :]), L1, SCALE if s < 2 else 1.0)
                for s in range(3, 7):
                    ahead(p, 0, s, (0,))
                    multiplied(act, p, 0, s)
                    if s >= 5:
                        act.wait_ge(s_evd, p.evacs("d", 0, s - 1))
                    act.activation(TMP[:, s % 2, 0:L1], PS[2 * (s % BANK_SETS) + 1][:, 0:L1], ACT.Sigmoid).then_inc(s_sil, 1)
                    ahead(p, 0, s, (1,))
                for s in range(7, 15):
                    ahead(p, 0, s, (0,))
                    multiplied(act, p, 0, s)
                    for j in range(2):
                        last = act.activation(SG[:, 2 * (s - 7) + j, :], PS[2 * (s % BANK_SETS) + j][:, 0:L1], ACT.Sigmoid)
                    last.then_inc(s_eva, 1)
                    ahead(p, 0, s, (1,))
                attention(f"b{i}")
                norm(f"cv{i}", CONV, CONV, V_CLN + 8 * i, c0, n, ACT.Silu)
                for c in range(KCV):
                    act.wait_ge(s_ln, LN_BASE[f"cv{i}"] + c + 1)
                    act.activation(UH[:, 4 + c, c0:c0 + n], CONV[:, c, c0:c0 + n], ACT.Copy).then_inc(s_mixh, 1)
                p = ph[f"proj{i}"]
                for s in range(4):
                    ahead(p, 0, s)
                    for m in range(2):
                        act.wait_ge(s_mix, KC * i + 2 * s + m + 1)
                        act.activation(MIXH[:, 2 * s + m, c0:c0 + n], TMP[:, 2 + m, 0:n], ACT.Copy).then_inc(s_mixh, 1)
                p = ph[f"wout{i}"]
                for s in range(4):
                    ahead(p, 0, s)
                nm = "moe" if i else "ffn"
                norm(f"a{i}", H, H, V_LN1 + 16 * i, c0, n, u=plain_u(nm, c0, n, f"a{i}"))
                scale_h(nm, c0, n)
                if i == 1:
                    act.wait_ge(s_gate, 1)
                    act.activation(GT[:, :, 1:2], GT[:, :, 0:1], ACT.Exp).then_inc(s_gexp, 1)
                    act.wait_ge(s_silc, 1)
                    for k in range(KC):
                        last = act.activation(SC4[:, k, :, 0:2], SCF[:, k:k + 1, :].to_broadcast([P, 32, 2]), ACT.Copy)
                    last.then_inc(s_silc, 1)
                    act.wait_ge(s_cbp, 1)
                    for b in range(4):
                        act.activation(CB[:, 2 * b:2 * b + 2, :].rearrange("p a t -> p (a t)"), PS[4 + b][:, :],
                                       ACT.Copy).then_inc(s_cb, 1)
                experts(nm, n)
                if i == 1:
                    act.dma_start(MLD[:, :, :], mod_rows.rearrange("r t n -> t r n")).then_inc(s_mrl, 16)
                norm(f"b{i}", H, H, V_LN2 + 16 * i, c0, n,
                     u=modulated_u("fa0", NMETA, T2) if i else plain_u("win1", 0, L1, "b0"))
            for i in range(DEPTH):
                nb = T2 if i == 0 else SEQ
                scale_h(f"fa{i}", NMETA, T2)
                experts(f"fa{i}", T2)
                nm = "waqkv" if i else "naqkv"
                norm(f"2a{i}", H, H, V_B + 48 * i, NMETA, T2, u=modulated_u(nm, NMETA, T2))
                scale_h(nm, NMETA, nb)
                p = ph[nm]
                if i == 0:
                    for s in range(4):
                        copy_step(p, 0, s, (QKV[:, 2 * s, :], QKV[:, 2 * s + 1, :]), T2, SCALE)
                    with act.Fori(0, p.n_iter - 1) as later:
                        it = later + 1
                        for s in range(4):
                            copy_step(p, it, s, [QKV[:, bass.ds(it * 8 + 2 * s + j, 1), :].rearrange("p a t -> p (a t)")
                                                 for j in range(2)], T2)
                    attention("na")
                else:
                    for s in range(6):
                        n = SEQ if s < 4 else T2
                        copy_step(p, 0, s, (QKV[:, 2 * s, 0:n], QKV[:, 2 * s + 1, 0:n]), n, SCALE if s < 4 else 1.0)
                    attention("wa")
                p = ph[f"wo{i}"]
                for s in range(4):
                    ahead(p, 0, s)
                norm(f"2n{i}", H, H, V_B + 48 * i + 16, NMETA, nb, u=modulated_u(f"fb{i}", NMETA, nb))
                scale_h(f"fb{i}", NMETA, nb)
                experts(f"fb{i}", nb)
                norm(f"2b{i}", H, H, V_B + 48 * i + 32, NMETA, nb,
                     u=None if i else modulated_u("fa1", NMETA, T2))

        @block.vector
        def _(dve):
            own = Tally(s_dve)

            def link(ins):
                own.inc(ins)
                dve.wait_ge(s_dve, own.value)

            class looped:

                def __init__(self, i, n_iter, per):
                    self.i, self.n_iter, self.per = i, n_iter, per

                def __enter__(self):
                    self.n0 = own.n
                    own.off = 0 if isinstance(self.i, int) else self.i * self.per

                def __exit__(self, *a):
                    assert own.n - self.n0 == self.per, (own.n - self.n0, self.per)
                    own.off = 0
                    if not isinstance(self.i, int):
                        own.n = self.n0 + self.per * self.n_iter

            def low(p, i, s, h):
                lo, hi = bounds(p, s, h)
                slot = p.piece_slot(s, h)
                dve.wait_ge(s_hi, p.piece(i, s, h) + 1)
                dve.tensor_tensor(WL[slot][:, 0:hi - lo], RAW[:, s % RAW_SLOTS, lo:hi],
                                  WH[slot][:, 0:hi - lo].bitcast(F32), ALU.subtract).then_inc(s_lo, 1)

            def ahead(p, i, s, pieces=range(PIECES)):
                later = p.step_ahead(i, s)
                for h in pieces if later else ():
                    low(*later, h)

            def norm(name, src, c0, n, u=None):
                b0, cs = LN_BASE[name], (KCV if name.startswith("cv") else KC)
                dve.wait_ge(s_mean, LN_IDX[name] + 1)
                for c in range(cs):
                    x = src[:, c, c0:c0 + n]
                    dve.tensor_tensor(x, x, PS[0][:, 0:n], ALU.subtract).then_inc(s_xc, 1)
                dve.wait_ge(s_std, LN_IDX[name] + 1)
                dve.wait_ge(s_sq, b0 + cs)
                link(dve.reciprocal(RSTD[:, 0:n], STD[:, 0:n]))
                lag, make = u or (0, None)
                for c in range(cs + lag):
                    if c < cs:
                        x = src[:, c, c0:c0 + n]
                        dve.tensor_tensor(x, x, RSTD[:, 0:n], ALU.mult).then_inc(s_nrm, 1)
                    if c >= lag and make:
                        make(c - lag)

            def low_u(name, c0, n):
                modulated = name in UM_IDX

                def make(c):
                    dve.wait_ge(s_uh, KC * U_IDX[name] + c + 1)
                    full = TMP[:, c % 4, 0:n] if modulated else H[:, c, c0:c0 + n]
                    dve.tensor_tensor(UL[:, c, c0:c0 + n], full, UH[:, c, c0:c0 + n].bitcast(F32),
                                      ALU.subtract).then_inc(s_ul, 1)
                return (3 if modulated else 2), make

            def experts(name, c0, n, gate=None):
                p = ph[name]
                moe = name == "moe"
                dve.wait_ge(s_hs, S_IDX[name] + 1)

                def body(i):
                    s = 0
                    for k in range(KH):
                        ahead(p, i, s, (0,))
                        multiplied(dve, p, i, s)
                        dve.wait_ge(s_sil, SIL_BASE[name] + k + 1 + i * KH)
                        dve.tensor_tensor(HT[:, k % 2, 0:n], SIL[:, k % 2, 0:n], PS[2 * (s % BANK_SETS) + 1][:, 0:n],
                                          ALU.mult).then_inc(s_evd, 1)
                        if k < KH - 1:
                            ahead(p, i, s, (1,))
                        dve.wait_ge(s_hid, HID_BASE[name] + k + 1 + i * KH)
                        dve.wait_ge(s_evd, p.evacs("d", i, s + 1))
                        dve.tensor_tensor(HIDL[:, k, 0:n], HT[:, k % 2, 0:n], HIDH[:, k, 0:n].bitcast(F32),
                                          ALU.subtract).then_inc(s_hidl, 1)
                        if k == KH - 1:
                            ahead(p, i, s, (1,))
                        s += 1
                        if p.kinds[s] == "a":
                            ahead(p, i, s)
                            s += 1
                    for m in range(KC):
                        if m < KC - 2:
                            ahead(p, i, s, (0,))
                        elif m == KC - 1:
                            ahead(p, i, s - 1, (0,))
                        multiplied(dve, p, i, s)
                        ps = PS[2 * (s % BANK_SETS)]
                        if m == 0:
                            dve.wait_ge(s_evd, p.evacs("d", i, s))
                        if moe:
                            w = CB[:, bass.ds(i, 1), :].rearrange("p a t -> p (a t)")
                            link(dve.tensor_tensor(HT[:, m % 2, 0:n], ps[:, 0:n], w, ALU.mult))
                            x = H[:, m, c0:c0 + n]
                            dve.tensor_tensor(x, x, HT[:, m % 2, 0:n], ALU.add).then_inc(s_evd, 1)
                        elif gate is None:
                            x = H[:, m, c0:c0 + n]
                            dve.tensor_tensor(x, x, ps[:, 0:n], ALU.add).then_inc(s_evd, 1)
                        else:
                            gated(ps, m, n, gate)
                        if m < KC - 2:
                            ahead(p, i, s, (1,))
                        elif m == KC - 1:
                            ahead(p, i, s - 1, (1,))
                            ahead(p, i, s)
                        s += 1

                if moe:
                    with dve.Fori(0, p.n_iter) as i, looped(i, p.n_iter, KC):
                        body(i)
                else:
                    iterate(dve, p, body)

            def gated(ps, m, n, gate):
                for st, (t0, nt) in enumerate(STREAM):
                    if t0 < NMETA + n:
                        x = H[:, m, t0:t0 + nt]
                        last = dve.scalar_tensor_tensor(x, ps[:, t0 - NMETA:t0 - NMETA + nt], mod(*gate, m, st), x,
                                                        ALU.mult, ALU.add)
                last.then_inc(s_evd, 1)

            def attention(name):
                a = atts[name]
                first = name[0] == "b"

                def has_bias(u):
                    return first or unit_of(a, u)[3] == T2

                def biased(it, u):
                    half, qt, k0, nk, _ = unit_of(a, u)
                    q0, nq = a.qts[qt]
                    b = u % 4
                    reach(dve, s_ex, freed(a, it, u, 4))
                    dve.wait_ge(s_sc, a.unit0 + it * a.units + u + 1)
                    ps = PS[u % 3]
                    if has_bias(u):
                        n = nk if first else SEQ
                        if first:
                            bt = B1[qt + 3 - len(a.qts)]
                            bias = bt[0:nq, bass.ds(2 * it + half, 1), 0:nk].rearrange("p a t -> p (a t)")
                        elif name == "na":
                            bias = NB[:, qt, half, :]
                            if qt == 0:
                                dve.wait_ge(s_nb, 2 * it + half + 1)
                        else:
                            bias = CST[:, C_WAM + SEQ * qt:C_WAM + SEQ * (qt + 1)]
                        link(dve.tensor_tensor(ps[0:nq, 0:n], ps[0:nq, 0:n], bias, ALU.add))
                    if a.sink:
                        link(dve.tensor_reduce(NMX[0:nq, b:b + 1], ps[0:nq, 0:nk], AX_X, ALU.max, negate=True))
                        nsk = NSK1[:, a.layer, bass.ds(2 * it + half, 1)] if first else NSK2[:, bass.ds(2 * it + half, 1)]
                        dve.tensor_tensor(NM[0:nq, b:b + 1], NMX[0:nq, b:b + 1], nsk[0:nq, :], ALU.min).then_inc(s_sb, 1)
                    else:
                        dve.tensor_reduce(NM[0:nq, b:b + 1], ps[0:nq, 0:nk], AX_X, ALU.max,
                                          negate=True).then_inc(s_sb, 1)

                def scaled(it, u):
                    half, qt, k0, nk, _ = unit_of(a, u)
                    nq = a.qts[qt][1]
                    b = u % 4
                    if a.sink:
                        link(dve.tensor_tensor(DEN[0:nq, b:b + 1], DEN[0:nq, b:b + 1], ESK[0:nq, b:b + 1], ALU.add))
                    link(dve.reciprocal(RDEN[0:nq, b:b + 1], DEN[0:nq, b:b + 1]))
                    dve.wait_ge(s_pv, a.unit0 + it * a.units + u + 1)
                    dve.tensor_scalar(a.os[0:nq, qt, HD * half:HD * half + HD], PS[5 + u % 2][0:nq, 0:HD],
                                      RDEN[0:nq, b:b + 1], None, ALU.mult).then_inc(s_o, 1)

                def pair(i, grp, more):
                    it = i + grp * a.inner
                    reach(dve, s_ot, a.it0 + it)
                    for u in range(a.units):
                        later = later_unit(a, it, u + 3, more)
                        if later:
                            biased(*later)
                        dve.wait_ge(s_ex, a.unit0 + it * a.units + u + 1)
                        scaled(it, u)
                    dve.wait_ge(s_ath, a.it0 + it + 1)
                    uu = slice(a.u0 + a.lo, a.u0 + a.hi)
                    dve.tensor_tensor(UL[:, bass.ds(it, 1), uu].rearrange("p a t -> p (a t)"),
                                      PS[7][:, a.lo:a.hi],
                                      UH[:, bass.ds(it, 1), uu].rearrange("p a t -> p (a t)").bitcast(F32),
                                      ALU.subtract).then_inc(s_atl, 1)

                per = sum(has_bias(u) + 1 + 2 * a.sink for u in range(a.units))
                for grp in range(a.groups):
                    for u in range(3):
                        biased(grp * a.inner, u)
                    for loop in pairs_of_heads(dve, a, a.inner - 1):
                        with loop as i, looped(i, a.inner - 1, per):
                            pair(i, grp, True)
                    pair(a.inner - 1, grp, False)

            def conv(layer, c0, n, lo, hi):
                for w in range(lo, hi):
                    for c in range(DVE_CONV):
                        x = HPAD[:, c, c0 + w:c0 + w + n]
                        y = CONV[:, c, c0:c0 + n]
                        tap = vec(V_DW + (layer * KCV + c) * TAPS + w)
                        if w == 0:
                            own.inc(dve.tensor_scalar(y, x, tap, vec(V_CB + 4 * layer + c), ALU.mult, ALU.add))
                        elif w < TAPS - 1:
                            dve.wait_ge(s_dve, own.value - DVE_CONV + 1)
                            own.inc(dve.scalar_tensor_tensor(y, x, tap, y, ALU.mult, ALU.add))
                        else:
                            dve.wait_ge(s_dve, own.value - DVE_CONV + 1 + c)
                            dve.scalar_tensor_tensor(y, x, tap, y, ALU.mult, ALU.add).then_inc(s_cv, 1)

            dve.wait_ge(s_const, 16 * 10)
            own.inc(dve.tensor_scalar(NSK1[:, :, :], SK1[:, :, :], -1.0, None, ALU.mult))
            link(dve.tensor_scalar(NSK2[:, :], SK2[:, :], -1.0, None, ALU.mult))
            for s in range(AHEAD):
                for h in range(PIECES):
                    low(ph["win0"], 0, s, h)
            norm("emb", H, 0, L1, low_u("win0", 0, L1))
            for i in range(DEPTH):
                c0, n = (0, L1) if i == 0 else (NMETA, SEQ)
                p = ph[f"win{i}"]
                for s in range(3):
                    ahead(p, 0, s)
                dve.wait_ge(s_ms, 4 + i)
                for s in range(3, 7):
                    ahead(p, 0, s, (0,))
                    multiplied(dve, p, 0, s)
                    dve.wait_ge(s_sil, SIL_BASE[f"win{i}"] + s - 2)
                    dve.tensor_tensor(HPAD[:, s - 3, TAPS - 1:TAPS - 1 + L1], PS[2 * (s % BANK_SETS)][:, 0:L1],
                                      TMP[:, s % 2, 0:L1], ALU.mult).then_inc(s_evd, 1)
                    ahead(p, 0, s, (1,))
                dve.wait_ge(s_evd, p.evacs("d", 0, 7))
                for s in range(7, 15):
                    ahead(p, 0, s)
                    conv(i, c0, n, 4 * (s - 7), min(4 * (s - 6), TAPS))
                dve.wait_ge(s_b1, 16 * 5 * (i + 1))
                attention(f"b{i}")
                norm(f"cv{i}", CONV, c0, n)
                for c in range(KCV):
                    dve.wait_ge(s_mixh, (KCV + KC) * i + c + 1)
                    dve.tensor_tensor(UL[:, 4 + c, c0:c0 + n], CONV[:, c, c0:c0 + n],
                                      UH[:, 4 + c, c0:c0 + n].bitcast(F32), ALU.subtract).then_inc(s_mixl, 1)
                p = ph[f"proj{i}"]
                for s in range(4):
                    ahead(p, 0, s, (0,))
                    multiplied(dve, p, 0, s)
                    for m in range(2):
                        c = 2 * s + m
                        ps = [PS[4 * (s % 2) + 2 * m + b][:, 0:n] for b in range(2)]
                        dve.tensor_tensor(TMP[:, 0, 0:n], ps[0], SG[:, c, c0:c0 + n], ALU.mult)
                        second = dve.tensor_tensor(TMP[:, 1, 0:n], ps[1], SG[:, KC + c, c0:c0 + n], ALU.mult)
                        if m:
                            second.then_inc(s_evd, 1)
                            dve.wait_ge(s_evd, p.evacs("d", 0, s + 1))
                        else:
                            link(second)
                        dve.tensor_tensor(TMP[:, 2 + m, 0:n], TMP[:, 0, 0:n], TMP[:, 1, 0:n], ALU.add).then_inc(s_mix, 1)
                        dve.wait_ge(s_mixh, (KCV + KC) * i + KCV + c + 1)
                        dve.tensor_tensor(MIXL[:, c, c0:c0 + n], TMP[:, 2 + m, 0:n],
                                          MIXH[:, c, c0:c0 + n].bitcast(F32), ALU.subtract).then_inc(s_mixl, 1)
                    ahead(p, 0, s, (1,))
                p = ph[f"wout{i}"]
                for s in range(4):
                    ahead(p, 0, s, (0,))
                    multiplied(dve, p, 0, s)
                    for j in range(2):
                        x = H[:, 2 * s + j, c0:c0 + n]
                        last = dve.scalar_tensor_tensor(x, x, ALPHA, PS[2 * (s % BANK_SETS) + j][:, 0:n], ALU.mult, ALU.add)
                    last.then_inc(s_evd, 1)
                    ahead(p, 0, s, (1,))
                nm = "moe" if i else "ffn"
                norm(f"a{i}", H, c0, n, low_u(nm, c0, n))
                if i == 1:
                    dve.wait_ge(s_rt, 1)
                    link(dve.tensor_copy(LG[:, :, :].rearrange("p a e -> p (a e)"), PS[2][:, 0:16]))
                    for t in range(2):
                        link(dve.max(MX8[:, t, :], LG[:, t, :]))
                        link(dve.max_index(IX8[:, t, :], MX8[:, t, :], LG[:, t, :]))
                    link(dve.tensor_copy(IXF[:, :, :], IX8[:, :, :]))
                    dve.tensor_tensor(GT[:, :, 0:1], MX8[:, :, 1:2], MX8[:, :, 0:1], ALU.subtract).then_inc(s_gate, 1)
                    dve.wait_ge(s_gexp, 1)
                    link(dve.tensor_scalar(GT[:, :, 2:3], GT[:, :, 1:2], 1.0, None, ALU.add))
                    link(dve.reciprocal(GT[:, :, 2:3], GT[:, :, 2:3]))
                    link(dve.tensor_tensor(GT[:, :, 3:4], GT[:, :, 1:2], GT[:, :, 2:3], ALU.mult))
                    for t in range(2):
                        for r, oh in enumerate((OH1, OH2)):
                            link(dve.tensor_scalar(oh[:, t, :], CST[:, C_IOTA:C_IOTA + 8], IXF[:, t, r:r + 1],
                                                   GT[:, t, 2 + r:3 + r], ALU.is_equal, ALU.mult))
                    link(dve.tensor_tensor(OH1[:, :, :], OH1[:, :, :], OH2[:, :, :], ALU.add))
                    for t in range(2):
                        last = dve.tensor_copy(CBB[:, t, :, :], OH1[:, t, :].rearrange("p (e a) -> p e a", a=1)
                                               .to_broadcast([P, N_EXP, P]))
                    last.then_inc(s_gate, 1)
                    dve.wait_ge(s_silc, 2)
                    for k in range(KC):
                        last = dve.tensor_tensor(SC4[:, k, :, 2:4], SCF[:, k:k + 1, :].to_broadcast([P, 32, 2]),
                                                 SC4[:, k, :, 0:2].bitcast(F32), ALU.subtract)
                    last.then_inc(s_silc, 1)
                    dve.wait_ge(s_cb, 4)
                experts(nm, c0, n)
                dve.wait_ge(s_evd, ph[nm].evacs("d", ph[nm].n_iter, 0))
                if i == 1:
                    dve.wait_ge(s_mrt, 1)
                    for st in range(2):
                        for j in range(2):
                            turned = PS[3 + j]
                            own.inc(dve.tensor_tensor(MOD[:, st, :, j], turned[:, st * MOD_STEPS:(st + 1) * MOD_STEPS],
                                                      VEC[:, V_BM + j:V_BM + 2 * MOD_STEPS:2], ALU.add))
                    dve.wait_ge(s_dve, own.value)
                    for st in range(2):
                        for j in range(2):
                            turned = PS[3 + j]
                            own.inc(dve.tensor_tensor(MOD[:, st, :, j], MOD[:, st, :, j],
                                                      turned[:, (2 + st) * MOD_STEPS:(3 + st) * MOD_STEPS], ALU.add))
                    dve.wait_ge(s_dve, own.value)
                    for l in range(2):
                        for idx in (1, 4, 7, 2, 8):
                            m = MOD[:, :, l * 36 + idx * 4:l * 36 + idx * 4 + 4, :]
                            dve.tensor_scalar(m, m, *((1.0, None, ALU.add) if idx in (1, 4, 7) else (0.5, None, ALU.mult)))\
                                .then_inc(s_mod, 1)
                    dve.wait_ge(s_mod, 10)
                norm(f"b{i}", H, c0, n, low_u("fa0", NMETA, T2) if i else low_u("win1", 0, L1))
            for i in range(DEPTH):
                nb = T2 if i == 0 else SEQ
                experts(f"fa{i}", NMETA, T2, (i, 2))
                dve.wait_ge(s_evd, ph[f"fa{i}"].evacs("d", 2, 0))
                nm = "waqkv" if i else "naqkv"
                norm(f"2a{i}", H, NMETA, T2, low_u(nm, NMETA, T2))
                p = ph[nm]
                if i == 0:
                    with dve.Fori(0, p.n_iter) as it:
                        for s in range(4):
                            ahead(p, it, s)
                    attention("na")
                else:
                    for s in range(6):
                        ahead(p, 0, s)
                    dve.wait_ge(s_eva, p.evacs("a", 0, 6))
                    for c in range(10):
                        dve.wait_ge(s_rsw, c + 1)
                        x = QKV[:, c, 0:SEQ]
                        own.inc(dve.tensor_tensor(TMP[:, c % 2, 0:SEQ], PS[c % 2][:, 0:SEQ], CST[:, C_SIN:C_SIN + SEQ], ALU.mult))
                        link(dve.tensor_tensor(x, x, CST[:, C_COS:C_COS + SEQ], ALU.mult))
                        dve.tensor_tensor(x, x, TMP[:, c % 2, 0:SEQ], ALU.add).then_inc(s_rope, 1)
                    attention("wa")
                p = ph[f"wo{i}"]
                dve.wait_ge(s_hs, S_IDX[nm] + 1)
                for s in range(4):
                    ahead(p, 0, s, (0,))
                    multiplied(dve, p, 0, s)
                    for j in range(2):
                        m = 2 * s + j
                        for st, (t0, nt) in enumerate(STREAM):
                            if t0 < NMETA + nb:
                                x = H[:, m, t0:t0 + nt]
                                last = dve.scalar_tensor_tensor(x, PS[2 * (s % BANK_SETS) + j][:, t0 - NMETA:t0 - NMETA + nt],
                                                                mod(i, 5, m, st), x, ALU.mult, ALU.add)
                    last.then_inc(s_evd, 1)
                    ahead(p, 0, s, (1,))
                norm(f"2n{i}", H, NMETA, nb, low_u(f"fb{i}", NMETA, nb))
                experts(f"fb{i}", NMETA, nb, (i, 8))
                dve.wait_ge(s_evd, ph[f"fb{i}"].evacs("d", 2, 0))
                norm(f"2b{i}", H, NMETA, nb, None if i else low_u("fa1", NMETA, T2))


def _linear(w, order=None):
    if order is not None:
        w = w[:, order]
    k, m = w.shape
    return np.ascontiguousarray(w.reshape(k // P, P, m // 256, 256).transpose(2, 1, 0, 3).reshape(m // 256, P, -1))


def _gate_up(g, u):
    e = g.shape[0]
    both = np.stack([g, u], 2).reshape(e, KC, P, 2, KH, P)
    return both.transpose(0, 4, 2, 1, 3, 5).reshape(e, KH, P, W_STEP)


def _down(w):
    e = w.shape[0]
    return w.reshape(e, KH, P, KC, P).transpose(0, 3, 2, 1, 4).reshape(e, KC, P, D_EXP)


def _halves(w_in):
    return np.stack([w_in[:, :D_EXP], w_in[:, D_EXP:]])


def _features(v):
    v = np.asarray(v)
    return v.reshape(-1, P).T


def lay_out(x):
    x = {k: np.asarray(v) for k, v in x.items()}
    consts, onehot = shape_constants()
    heads = [h for c in range(4) for h in (c, 4 + c)]
    hcols = np.concatenate([np.arange(h * HD, (h + 1) * HD) for h in heads])
    order = [hcols, np.arange(512, 768)]
    for t in range(KCV):
        order += [768 + t * P + np.arange(P), 768 + CONVC + t * P + np.arange(P)]
    order = np.concatenate(order + [np.arange(768 + 2 * CONVC, 768 + 2 * CONVC + 2 * D)])
    wheads = [8 * p + 4 * half + i for p in range(2) for i in range(4) for half in range(2)]
    wcols = np.concatenate([np.arange(h * HD, (h + 1) * HD) for h in wheads])
    arrays = {
        "consts": consts, "onehot": onehot, "neg_row": np.full((1, 8), NEG, np.float32),
        "tokens": np.concatenate([x["meta_tokens"], x["x"][0]]).T.reshape(KC, P, L1).transpose(1, 0, 2),
        "ctx": x["ctx_2"][0].T.reshape(KC, P, CTX).transpose(1, 0, 2),
        "cond": np.stack([x["c_2"][0], x["c_ctx_2"]]).reshape(2, KC, P).transpose(2, 1, 0),
        "rel_bias": x["rel_bias"][:, heads],
        "sinks": x["sinks"][:, heads],
        "sinks_2": x["wa_sinks_2"][:, wheads],
        "router": x["router"][0].reshape(KC, P, N_EXP).transpose(1, 0, 2),
        "na_rpb": x["na_rpb_2"].reshape(1, -1),
        "w_in": np.stack([_linear(x["w_in"][i], order) for i in range(DEPTH)]),
        "w_proj": np.stack([np.concatenate([_linear(x["w_attn_proj"][i][hcols]), _linear(x["w_conv_proj"][i])], 2)
                            for i in range(DEPTH)]),
        "w_out": np.stack([_linear(x["w_out"][i]) for i in range(DEPTH)]),
        "w_mod": np.concatenate([_linear(x["w_mod_2"][i]) for i in range(DEPTH)]),
        "w_na": _linear(x["na_w_qkv_2"][0]),
        "w_wa": _linear(x["wa_w_qkv_2"][0], np.concatenate([wcols, np.arange(D, D + 512)])),
        "w_o": np.stack([_linear(x["na_w_o_2"][0]), _linear(x["wa_w_o_2"][0][wcols])]),
    }
    g, u, d = [_halves(x["ffn_w_gate"][0]), x["moe_w_gate"][0]], [_halves(x["ffn_w_up"][0]), x["moe_w_up"][0]], \
        [x["ffn_w_down"][0].reshape(2, D_EXP, D), x["moe_w_down"][0]]
    for i in range(DEPTH):
        for j in range(2):
            w = x["ffn_w_in_2"][i, j]
            g.append(_halves(w[:, :2 * D_EXP]))
            u.append(_halves(w[:, 2 * D_EXP:]))
            d.append(x["ffn_w_out_2"][i, j].reshape(2, D_EXP, D))
    arrays["w_gu"] = np.concatenate([_gate_up(a, b) for a, b in zip(g, u)])
    arrays["w_dn"] = np.concatenate([_down(a) for a in d])
    cols = [_features(x["emb_ln_g"]), _features(x["emb_ln_b"])]
    for gg, bb in (("ln1_g", "ln1_b"), ("ln2_g", "ln2_b")):
        for i in range(DEPTH):
            cols += [_features(x[gg][i]), _features(x[bb][i])]
    for i in range(DEPTH):
        for j in range(3):
            cols += [_features(x["ln_g_2"][i, j]), _features(x["ln_b_2"][i, j])]
    for i in range(DEPTH):
        cols += [_features(x["conv_ln_g"][i]), _features(x["conv_ln_b"][i])]
    cols += [_features(x["conv_b"])]
    for i in range(DEPTH):
        cols += [x["conv_dw"][i].T.reshape(KCV, P, TAPS).transpose(1, 0, 2).reshape(P, -1)]
    cols += [_features(x["b_mod_2"])]
    arrays["vectors"] = np.concatenate(cols, 1)
    return {k: np.ascontiguousarray(v) for k, v in arrays.items()}


def kernel(**inputs):
    import concourse.bacc as bacc
    from concourse.bass_utils import run_bass_kernel_spmd as run

    nc = bacc.Bacc("TRN2", target_bir_lowering=False, num_devices=1)
    arrays = lay_out(inputs)
    ins = {k: nc.dram_tensor(f"in_{k}", a.shape, F32, kind="ExternalInput").ap() for k, a in arrays.items()}
    out = nc.dram_tensor("out_h", (P, KC, SEQ), F32, kind="ExternalOutput").ap()
    build(nc, ins, out)
    r = run(nc, [{f"in_{k}": a for k, a in arrays.items()}], core_ids=[0])
    got = r.results[0]["out_h"]
    return got.transpose(2, 1, 0).reshape(1, SEQ, D)
```
